# Optimizing a Trainium2 kernel written in Bass

```python
import jax, jax.numpy as jnp
from jax import lax
import numpy as np

D_MODEL = 1024
BATCH = 1
SEQ = 1024
DEPTH = 2

CHUNK = 64
Q_BLOCK = 128
MLA_HEADS = 8
QK_NOPE_DIM = 64
QK_ROPE_DIM = 32
QK_DIM = QK_NOPE_DIM + QK_ROPE_DIM
V_HEAD_DIM = 64
Q_RANK = 256
KV_RANK = 128
ROPE_THETA = 10000.0
MLA_WIDTH = MLA_HEADS * V_HEAD_DIM
GM_GROUPS = 8
GM_GROUP_DIM = 64
GM_WIDTH = GM_GROUPS * GM_GROUP_DIM
GM_BLOCK = 128
MIX_WIDTH = MLA_WIDTH + GM_WIDTH
IN_WIDTH = Q_RANK + KV_RANK + QK_ROPE_DIM + 2 * GM_WIDTH
N_EXPERT_GROUPS = 4
EXPERTS_PER_GROUP = 8
N_EXPERTS = N_EXPERT_GROUPS * EXPERTS_PER_GROUP
TOP_K_IN_GROUP = 2
D_EXPERT = 512
MOE_BLOCK = 128
PLE_DIM = 256
RMS_EPS = 1e-6

kernel_name = 'hybrid_mla_gmlp_hiermoe_ple'

def rms_norm(x, g):
    xf = x.astype(jnp.float32)
    y = xf * lax.rsqrt(jnp.mean(xf * xf, axis=-1, keepdims=True) + RMS_EPS)
    return (y * g.astype(jnp.float32)).astype(x.dtype)

def rope_tables(seq, dtype):
    inv = ROPE_THETA ** (-jnp.arange(0, QK_ROPE_DIM, 2, dtype=jnp.float32) / QK_ROPE_DIM)
    ang = jnp.arange(seq, dtype=jnp.float32)[:, None] * inv[None, :]
    return jnp.cos(ang).astype(dtype), jnp.sin(ang).astype(dtype)

def apply_rope(x, cos, sin):
    half = x.shape[-1] // 2
    x1, x2 = x[..., :half], x[..., half:]
    c = cos[None, :, None, :]
    s = sin[None, :, None, :]
    return jnp.concatenate([x1 * c - x2 * s, x2 * c + x1 * s], axis=-1)

def block_causal_attention(q, k, v):
    S = q.shape[1]
    scale = QK_DIM ** -0.5
    chunk_id = jnp.arange(S) // CHUNK
    neg = jnp.finfo(jnp.float32).min
    outs = []
    for blk in range(S // Q_BLOCK):
        q0 = blk * Q_BLOCK
        kend = q0 + Q_BLOCK
        qb = q[:, q0:kend]
        kb = k[:, :kend]
        vb = v[:, :kend]
        s = jnp.einsum('bqhd,bkhd->bhqk', qb, kb, preferred_element_type=jnp.float32) * scale
        mask = chunk_id[None, :kend] <= chunk_id[q0:kend, None]
        s = jnp.where(mask[None, None], s, neg)
        pr = jax.nn.softmax(s, axis=-1).astype(vb.dtype)
        outs.append(jnp.einsum('bhqk,bkhd->bqhd', pr, vb))
    return jnp.concatenate(outs, axis=1)

def mla_branch(c_q, c_kv, k_r, g_cq, g_ckv, w_uq, w_ukv, g_qn, g_kn, cos, sin):
    B, S, _ = c_q.shape
    q = (rms_norm(c_q, g_cq) @ w_uq).reshape(B, S, MLA_HEADS, QK_DIM)
    kv = (rms_norm(c_kv, g_ckv) @ w_ukv).reshape(B, S, MLA_HEADS, QK_NOPE_DIM + V_HEAD_DIM)
    k_nope, v = kv[..., :QK_NOPE_DIM], kv[..., QK_NOPE_DIM:]
    k_rope = jnp.broadcast_to(k_r[:, :, None, :], (B, S, MLA_HEADS, QK_ROPE_DIM))
    k = jnp.concatenate([k_nope, k_rope], axis=-1)
    q = rms_norm(q, g_qn)
    k = rms_norm(k, g_kn)
    q = jnp.concatenate([q[..., :QK_NOPE_DIM], apply_rope(q[..., QK_NOPE_DIM:], cos, sin)], axis=-1)
    k = jnp.concatenate([k[..., :QK_NOPE_DIM], apply_rope(k[..., QK_NOPE_DIM:], cos, sin)], axis=-1)
    o = block_causal_attention(q, k, v)
    return o.reshape(B, S, MLA_WIDTH)

def gmlp_branch(u_raw, v_raw, g_v, w_s, b_s):
    B, S, _ = u_raw.shape
    nb = S // GM_BLOCK
    u = jax.nn.gelu(u_raw).reshape(B, nb, GM_BLOCK, GM_GROUPS, GM_GROUP_DIM)
    v = rms_norm(jax.nn.gelu(v_raw).reshape(B, S, GM_GROUPS, GM_GROUP_DIM), g_v)
    v = v.reshape(B, nb, GM_BLOCK, GM_GROUPS, GM_GROUP_DIM)
    pos_chunk = jnp.arange(GM_BLOCK) // CHUNK
    mask = pos_chunk[None, :] <= pos_chunk[:, None]
    w = jnp.where(mask[None], w_s, jnp.zeros((), w_s.dtype))
    s = jnp.einsum('gtj,bnjgc->bntgc', w, v) + b_s.T[None, None, :, :, None]
    return (u * s).reshape(B, S, GM_WIDTH)

def hier_moe(xn, w_rg, w_re, w1, w3, w2):
    B, S, D = xn.shape
    T = B * S
    K = TOP_K_IN_GROUP
    xt = xn.reshape(T, D)
    lg = jnp.matmul(xt, w_rg, preferred_element_type=jnp.float32)
    pg = jax.nn.softmax(lg, axis=-1)
    g_sel = jnp.argmax(lg, axis=-1).astype(jnp.int32)
    p_sel = jnp.take_along_axis(pg, g_sel[:, None], axis=-1)
    le = jnp.matmul(xt, w_re, preferred_element_type=jnp.float32).reshape(T, N_EXPERT_GROUPS, EXPERTS_PER_GROUP)
    le_sel = jnp.take_along_axis(le, g_sel[:, None, None], axis=1)[:, 0]
    top_v, top_i = lax.top_k(le_sel, K)
    gates = p_sel * jax.nn.softmax(top_v, axis=-1)
    ids = (g_sel[:, None] * EXPERTS_PER_GROUP + top_i).reshape(-1).astype(jnp.int32)
    A = T * K
    tok = jnp.arange(A, dtype=jnp.int32) // K
    n_blocks = -(-A // MOE_BLOCK) + N_EXPERTS
    n_slots = n_blocks * MOE_BLOCK
    order = jnp.argsort(ids)
    s_ids = ids[order]
    counts = jnp.bincount(ids, length=N_EXPERTS).astype(jnp.int32)
    padded = (counts + MOE_BLOCK - 1) // MOE_BLOCK * MOE_BLOCK
    p_end = jnp.cumsum(padded)
    p_start = p_end - padded
    c_start = jnp.cumsum(counts) - counts
    dest = p_start[s_ids] + jnp.arange(A, dtype=jnp.int32) - c_start[s_ids]
    slot_tok = jnp.full((n_slots,), T, jnp.int32).at[dest].set(tok[order])
    slot_gate = jnp.zeros((n_slots,), jnp.float32).at[dest].set(gates.reshape(-1)[order])
    block_start = jnp.arange(n_blocks, dtype=jnp.int32) * MOE_BLOCK
    block_expert = jnp.minimum(jnp.sum(block_start[:, None] >= p_end[None, :], axis=1), N_EXPERTS - 1)
    x_pad = jnp.concatenate([xt, jnp.zeros((1, D), xt.dtype)], axis=0)
    x_slots = x_pad[slot_tok].reshape(n_blocks, MOE_BLOCK, D)

    def expert_block(args):
        xb, e = args
        return (jax.nn.silu(xb @ w1[e]) * (xb @ w3[e])) @ w2[e]

    y_slots = lax.map(expert_block, (x_slots, block_expert)).reshape(n_slots, D)
    y = jnp.zeros((T + 1, D), xt.dtype).at[slot_tok].add(y_slots * slot_gate[:, None].astype(xt.dtype))
    return y[:T].reshape(B, S, D)

def setup_inputs(seed: int = 0) -> dict:
    key = jax.random.key(seed)
    ks = jax.random.split(key, 32)
    L, D = DEPTH, D_MODEL

    def nrm(k, shape, scale):
        return jax.random.normal(k, shape, jnp.float32) * scale

    def gain(k, shape):
        return 1.0 + 0.1 * jax.random.normal(k, shape, jnp.float32)

    return {
        'x': nrm(ks[0], (BATCH, SEQ, D), 1.0),
        'p': nrm(ks[1], (DEPTH, BATCH, SEQ, PLE_DIM), 1.0),
        'g_mix_norm': gain(ks[2], (L, D)),
        'w_in': nrm(ks[3], (L, D, IN_WIDTH), D ** -0.5),
        'g_cq': gain(ks[4], (L, Q_RANK)),
        'g_ckv': gain(ks[5], (L, KV_RANK)),
        'w_uq': nrm(ks[6], (L, Q_RANK, MLA_HEADS * QK_DIM), Q_RANK ** -0.5),
        'w_ukv': nrm(ks[7], (L, KV_RANK, MLA_HEADS * (QK_NOPE_DIM + V_HEAD_DIM)), KV_RANK ** -0.5),
        'g_qn': gain(ks[8], (L, QK_DIM)),
        'g_kn': gain(ks[9], (L, QK_DIM)),
        'g_v': gain(ks[10], (L, GM_GROUPS, GM_GROUP_DIM)),
        'w_s': nrm(ks[11], (L, GM_GROUPS, GM_BLOCK, GM_BLOCK), GM_BLOCK ** -0.5),
        'b_s': gain(ks[12], (L, GM_GROUPS, GM_BLOCK)),
        'g_out_mla': gain(ks[13], (L, MLA_WIDTH)),
        'g_out_gmlp': gain(ks[14], (L, GM_WIDTH)),
        'w_out': nrm(ks[15], (L, MIX_WIDTH, D), MIX_WIDTH ** -0.5),
        'g_ffn_norm': gain(ks[16], (L, D)),
        'w_router_group': nrm(ks[17], (L, D, N_EXPERT_GROUPS), D ** -0.5),
        'w_router_expert': nrm(ks[18], (L, D, N_EXPERTS), D ** -0.5),
        'w1': nrm(ks[19], (L, N_EXPERTS, D, D_EXPERT), D ** -0.5),
        'w3': nrm(ks[20], (L, N_EXPERTS, D, D_EXPERT), D ** -0.5),
        'w2': nrm(ks[21], (L, N_EXPERTS, D_EXPERT, D), D_EXPERT ** -0.5),
        'g_ple': gain(ks[22], (L, D)),
        'w_ple_gate': nrm(ks[23], (L, D, D), D ** -0.5),
        'b_ple_gate': nrm(ks[24], (L, D), 0.02),
        'w_ple': nrm(ks[25], (L, PLE_DIM, D), PLE_DIM ** -0.5),
    }

def reference(x, p, g_mix_norm, w_in, g_cq, g_ckv, w_uq, w_ukv, g_qn, g_kn, g_v, w_s, b_s,
              g_out_mla, g_out_gmlp, w_out, g_ffn_norm, w_router_group, w_router_expert,
              w1, w3, w2, g_ple, w_ple_gate, b_ple_gate, w_ple):
    S = x.shape[1]
    cos, sin = rope_tables(S, x.dtype)
    s0 = Q_RANK
    s1 = s0 + KV_RANK
    s2 = s1 + QK_ROPE_DIM
    s3 = s2 + GM_WIDTH
    h = x
    for i in range(DEPTH):
        hn = rms_norm(h, g_mix_norm[i])
        proj = hn @ w_in[i]
        c_q = proj[..., :s0]
        c_kv = proj[..., s0:s1]
        k_r = proj[..., s1:s2]
        u_raw = proj[..., s2:s3]
        v_raw = proj[..., s3:]
        a = mla_branch(c_q, c_kv, k_r, g_cq[i], g_ckv[i], w_uq[i], w_ukv[i], g_qn[i], g_kn[i], cos, sin)
        m = gmlp_branch(u_raw, v_raw, g_v[i], w_s[i], b_s[i])
        mixed = jnp.concatenate([rms_norm(a, g_out_mla[i]), rms_norm(m, g_out_gmlp[i])], axis=-1)
        h = h + mixed @ w_out[i]
        h = h + hier_moe(rms_norm(h, g_ffn_norm[i]), w_router_group[i], w_router_expert[i], w1[i], w3[i], w2[i])
        gate = jax.nn.sigmoid(rms_norm(h, g_ple[i]) @ w_ple_gate[i] + b_ple_gate[i])
        h = h + (p[i] @ w_ple[i]) * gate
    return h


_drawn_inputs = setup_inputs


def setup_inputs(seed=0):
    import zlib

    import numpy as np

    out = dict(_drawn_inputs(seed))
    spreads = {}
    factors = {'b_ple_gate': 7.451}
    for name, (base, spread) in spreads.items():
        noise = np.random.default_rng([zlib.crc32(name.encode()), seed]).standard_normal(out[name].shape)
        drawn = base * np.exp(spread * noise) if base else spread * noise
        out[name] = __import__('jax').numpy.asarray(drawn.astype(out[name].dtype))
    for name, factor in factors.items():
        out[name] = (out[name] * factor).astype(out[name].dtype)
    return out
```

```python
from contextlib import ExitStack

import concourse.bass as bass
from concourse import mybir

P = 128
BANK = 512
F32 = mybir.dt.float32
F32R = mybir.dt.float32r
I32 = mybir.dt.int32
U32 = mybir.dt.uint32
ALU = mybir.AluOpType
ACT = mybir.ActivationFunctionType
AX_X = mybir.AxisListType.X
ds = bass.ds

EPS = 1e-6
NEG = -3.0e38
HEADS, NOPE, ROPE, VDIM = 8, 64, 32, 64
QK = NOPE + ROPE
Q_RANK, KV_RANK = 256, 128
GROUPS, GDIM = 8, 64
CHUNK = 64
NG, PER_G, NE, TOPK = 4, 8, 32, 2
FE = 512
PLE = 256
CONSTS = 4 * P + 8 * ROPE * 2 + 32 + 8 + 8 + 16


class Count:

    def __init__(self, per, turn):
        self.per, self.base, self.n = per, turn * per, 0

    def next(self):
        self.n += 1
        return self.base + self.n

    def close(self):
        assert self.n == self.per, (self.n, self.per)


def hybrid_trunk(nc, x, p, g_mix_norm, w_in, g_cq, g_ckv, w_uq, w_ukv, g_qn, g_kn, g_v, w_s, b_s,
                 g_out_mla, g_out_gmlp, w_out, g_ffn_norm, w_router_group, w_router_expert,
                 w1, w3, w2, g_ple, w_ple_gate, b_ple_gate, w_ple, shape_consts, out):
    DEPTH, D, IN_W = w_in.shape
    SEQ = x.shape[1]
    NT = SEQ // P
    KD = D // P
    KF = FE // P
    MIXW = HEADS * VDIM
    CQKV = Q_RANK + KV_RANK
    W_C = CQKV + ROPE
    U0, V0 = W_C, W_C + GROUPS * GDIM
    MAX_OVER = (TOPK * SEQ - 1) // P
    NBLK = NE + MAX_OVER
    NROUTE = NG + NE
    SCALE = float(QK) ** -0.5
    PHASES = 6
    AB_LOADS = 11
    PH_WS, PH_A, PH_B, PH_C, PH_D, PH_E = range(PHASES)

    with ExitStack() as ctx:
        sem = lambda name: ctx.enter_context(nc.semaphore(name))

        arena = ctx.enter_context(nc.sbuf_tensor("arena", [P, 212832 // 4], F32))
        ARENA0 = 16512

        def at(name, shape, dt, offset):
            size = 4
            for n in shape[1:]:
                size *= n
            assert offset + size <= 212832, (name, offset, size)
            return nc.alloc_sbuf_tensor_at(name, shape, dt, offset=ARENA0 + offset)

        K = 1024
        h = at("h", [P, NT * D], F32, 0)
        RAW = NT * D * 4
        ring_raw = at("ring_raw", [P, 6, 2048], F32, RAW)
        w_in_sb = at("w_in_sb", [P, KD, IN_W], F32, RAW)
        w_out_sb = at("w_out_sb", [P, KD, D], F32, RAW)
        g_out_sb = at("g_out_sb", [P, D], F32, RAW + 32 * K)
        g_ffn_sb = at("g_ffn_sb", [P, D], F32, RAW + 36 * K)
        w_router = at("w_router", [P, KD, NROUTE], F32, RAW + 40 * K)
        R = RAW + 48 * K
        ring_hi = at("ring_hi", [P, 3, 2048], F32R, R)
        ring_lo = at("ring_lo", [P, 3, 2048], F32R, R + 24 * K)
        xg = at("xg", [P, D], F32, R + 48 * K)
        xg_hi = at("xg_hi", [P, KD, P], F32R, R + 52 * K)
        xg_lo = at("xg_lo", [P, KD, P], F32R, R + 56 * K)
        silu_sb = at("silu_sb", [P, FE], F32, R + 60 * K)
        gate_sb = at("gate_sb", [P, FE], F32, R + 62 * K)
        gT_hi = at("gT_hi", [P, KF, P], F32R, R + 64 * K)
        gT_lo = at("gT_lo", [P, KF, P], F32R, R + 66 * K)
        y_sb = at("y_sb", [P, D], F32, R + 68 * K)
        w_gate_sb = at("w_gate_sb", [P, KD, D], F32, R + 76 * K)
        w_ple_sb = at("w_ple_sb", [P, 2, D], F32, R + 108 * K)
        xT = [at(f"xT{j}", [P, KD, P], F32, R + 4 * K * j) for j in range(2)]
        xn = [at(f"xn{j}", [P, D], F32, R + (8 + 4 * j) * K) for j in range(2)]
        junk = at("junk", [P, D], F32, R + 16 * K)
        gv_sb = at("gv_sb", [P, 512], F32, R + 20 * K)
        gu_sb = at("gu_sb", [P, 512], F32, R + 22 * K)
        vsq = at("vsq", [P, 512], F32, R + 24 * K)
        vn = at("vn", [P, 512], F32, R + 26 * K)
        vn1 = at("vn1", [P, 512], F32, R + 28 * K)
        s_sb = at("s_sb", [P, 512], F32, R + 30 * K)
        cn = at("cn", [P, CQKV], F32, R + 32 * K)
        junk_c = at("junk_c", [P, CQKV], F32, R + 34 * K)
        ws_nat = [at("ws_nat0", [P, 6 * P], F32, RAW + 45 * K), at("ws_nat1", [P, 2 * P], F32, R + 116 * K)]
        g_mix_sb = at("g_mix_sb", [P, D], F32, R + 48 * K)
        g_c_sb = at("g_c_sb", [P, CQKV], F32, R + 52 * K)
        g_v_sb = at("g_v_sb", [P, 512], F32, R + 54 * K)
        g_qk_sb = at("g_qk_sb", [P, 2, QK], F32, R + 56 * K)
        bs_sb = at("bs_sb", [P, GROUPS], F32, R + 57 * K)
        w_uq_sb = at("w_uq_sb", [P, 2, HEADS * QK], F32, R + 58 * K)
        w_ukv_sb = at("w_ukv_sb", [P, HEADS * P], F32, R + 64 * K)
        wsT = at("wsT", [P, GROUPS, P], F32, R + 68 * K)
        kr_all = at("kr_all", [P, NT, ROPE], F32, R + 72 * K)
        cT = at("cT", [P, 3, SEQ], F32, R + 73 * K)
        m_all = at("m_all", [P, NT * 512], F32, R + 85 * K)
        a_all = at("a_all", [P, NT, MIXW], F32, R + 101 * K)
        qkb = at("qkb", [P, 2, NT, QK], F32, R)
        qksq = at("qksq", [P, 2, NT, QK], F32, R + 6 * K)
        rope_c = at("rope_c", [P, 2, NT, ROPE], F32, R + 12 * K)
        rope_s = at("rope_s", [P, 2, NT, ROPE], F32, R + 14 * K)
        qkT = [at(f"qkT{j}", [QK, 2, SEQ], F32, R + (16 + 8 * j) * K) for j in range(2)]
        v_sb = [at(f"v_sb{j}", [P, NT, VDIM], F32, R + (32 + 2 * j) * K) for j in range(2)]
        prob = [at(f"prob{j}", [P, SEQ], F32, R + (36 + 4 * j) * K) for j in range(2)]
        probT = at("probT", [P, NT, P], F32, R + 44 * K)
        xf = at("xf", [P, D], F32, R + 20 * K)
        xfT = at("xfT", [P, KD, P], F32, R + 24 * K)
        yg = [[at(f"yg{j}{k}", [P, D], F32, R + (20 + 8 * j + 4 * k) * K) for k in range(2)] for j in range(2)]
        g_ple_sb = at("g_ple_sb", [P, D], F32, R + 36 * K)
        b_gate_sb = at("b_gate_sb", [P, D], F32, R + 40 * K)
        gs = at("gs", [P, D], F32, R + 44 * K)
        p_sb = [at(f"p_sb{j}", [P, PLE], F32, R + (72 + j) * K) for j in range(2)]
        pT = [at(f"pT{j}", [P, 2, P], F32, R + (74 + j) * K) for j in range(2)]

        S0 = R + 117 * K
        off = [S0]

        def small(name, shape, dt=F32):
            n = 4
            for d in shape[1:]:
                n *= d
            off[0] += -off[0] % 32
            o = off[0]
            off[0] += n
            return at(name, shape, dt, o)

        consts = small("consts", [P, CONSTS])
        c0 = [0]

        def const(n):
            a = c0[0]
            c0[0] += n
            return consts[:, a:a + n]

        ident = const(P)
        before = const(P)
        ones = const(P)
        cos2 = const(8 * ROPE).rearrange("p (t r) -> p t r", t=8)
        sin2 = const(8 * ROPE).rearrange("p (t r) -> p t r", t=8)
        iota_r = const(P)
        iota_e = iota_r[:, 0:NE]
        block_e = const(NE)
        steps = const(8)
        tok_id = const(8)
        over_id = const(16)
        assert c0[0] == CONSTS

        half = small("half", [P, 16])
        stat_x = small("stat_x", [P, 2])
        rstd_x = small("rstd_x", [P, 2])
        stat_c = small("stat_c", [P, 2])
        rstd_c = small("rstd_c", [P, 2])
        stat_v = small("stat_v", [P, GROUPS])
        rstd_v = small("rstd_v", [P, GROUPS])
        tmp_p = small("tmp_p", [P, 16])
        stat_qk = small("stat_qk", [P, 16])
        rstd_qk = small("rstd_qk", [P, 16])
        row_max = small("row_max", [P, 2])
        neg_max = small("neg_max", [P, 2])
        row_sum = small("row_sum", [P, NT])
        row_inv = small("row_inv", [P, NT])
        stat_f = small("stat_f", [P, 1])
        rstd_f = small("rstd_f", [P, 1])
        lg8 = small("lg8", [P, 8])
        le = small("le", [P, NE])
        top8 = small("top8", [P, 8])
        gi8 = small("gi8", [P, 8], U32)
        gf = small("gf", [P, 1])
        lgm = small("lgm", [P, NG])
        lge = small("lge", [P, NG])
        gmask = small("gmask", [P, NG])
        gbias = small("gbias", [P, NG])
        top8e = small("top8e", [P, 8])
        ei8 = small("ei8", [P, 8], U32)
        sum_all = small("sum_all", [P, NT])
        gap_all = small("gap_all", [P, NT])
        ef_all = small("ef_all", [P, TOPK, NT])
        picks = small("picks", [P, NT + 1, NE])
        rank_k = small("rank_k", [P, TOPK * NT])
        ovs_k = small("ovs_k", [P, TOPK * NT])
        q_k = small("q_k", [P, TOPK * NT])
        ge_k = small("ge_k", [P, TOPK * NT])
        blk_k = small("blk_k", [P, TOPK * NT])
        row_k = small("row_k", [P, TOPK * NT])
        dest_u = small("dest_u", [P, TOPK * NT], U32)
        over_e = small("over_e", [P, NE])
        over_s = small("over_s", [P, NE])
        over_end = small("over_end", [P, NE])
        nb_f = small("nb_f", [P, 1])
        nb2_f = small("nb2_f", [P, 1])
        gb_f = small("gb_f", [P, 1])
        plan = small("plan", [P, 2], I32)
        next_gb = small("next_gb", [P, DEPTH + 1], I32)
        expert_i = small("expert_i", [P, NE + 16], I32)
        ex_f = small("ex_f", [P, 16])
        gates = small("gates", [P, TOPK * NT])
        exp_g = small("exp_g", [P, NT])
        slot_tok = small("slot_tok", [P, NBLK + 1], U32)
        idx_x = small("idx_x", [P, 1], U32)
        idx_y = [[small(f"idx_y{j}{k}", [P, 1], U32) for k in range(2)] for j in range(2)]
        cmp_s = at("cmp_s", [P, NE * 16], F32, R + 52 * K)
        oh_row = [at(f"oh_row{j}", [P, P], F32, R + 60 * K + 512 * j) for j in range(2)]
        oh_blk = [at(f"oh_blk{j}", [P, NBLK + 1], F32, R + 62 * K + 256 * j) for j in range(2)]
        onehot = at("onehot", [P, TOPK, NT, NE], F32, R + 56 * K)
        chosen = at("chosen", [P, NT, NE], F32, R + 58 * K)
        overT = at("overT", [NE, P], F32, R + 70 * K)
        sel = at("sel", [P, NT, NE], F32, R + 68 * K)
        rank_sb = at("rank_sb", [P, NT, NE], F32, R + 64 * K)
        blk_iota = iota_r[:, 0:NBLK + 1]

        ps = ctx.enter_context(nc.psum_tensor("ps", [P, 8 * BANK], F32))

        def bank(b, n=1):
            return ps[:, b * BANK:(b + n) * BANK]

        xn_rows = nc.dram_tensor("xn_rows", (SEQ, D), F32, kind="Internal").ap()
        y_rows = nc.dram_tensor("y_rows", (NBLK * P, D), F32, kind="Internal").ap()
        x_v = x.rearrange("b (t p) d -> p (b t) d", p=P)
        out_v = out.rearrange("b (t p) d -> p (b t) d", p=P)
        p_v = p.rearrange("l b (t p) d -> (l b t) p d", p=P)
        w_in_v = w_in.rearrange("l (k p) n -> l p k n", p=P)
        w_out_v = w_out.rearrange("l (k p) n -> l p k n", p=P)
        w_gate_v = w_ple_gate.rearrange("l (k p) n -> l p k n", p=P)
        w_ple_v = w_ple.rearrange("l (k p) n -> l p k n", p=P)
        w_uq_v = w_uq.rearrange("l (k p) n -> l p k n", p=P)
        w_rg_v = w_router_group.rearrange("l (k p) n -> l p k n", p=P)
        w_re_v = w_router_expert.rearrange("l (k p) n -> l p k n", p=P)
        w_s_v = w_s.rearrange("l g t j -> l t g j")
        b_s_v = b_s.rearrange("l g t -> l t g")
        g_v_v = g_v.rearrange("l g c -> l (g c)")
        w1_v = w1.rearrange("l e (k p) f -> (l e) p k f", p=P)
        w3_v = w3.rearrange("l e (k p) f -> (l e) p k f", p=P)
        w2_v = w2.rearrange("l e (k p) d -> (l e) p k d", p=P)
        xn_v = xn_rows.rearrange("(t p) d -> t p d", p=P)
        y_v = y_rows.rearrange("(b p) d -> b p d", p=P)

        consts_in, x_in = sem("consts_in"), sem("x_in")
        w_in_in, ab_in, wout_in, cpar_in = sem("w_in_in"), sem("ab_in"), sem("wout_in"), sem("cpar_in")
        ple_w_in, e_par_in, out_done = sem("ple_w_in"), sem("e_par_in"), sem("out_done")
        p_in = [sem(f"p_in{j}") for j in range(2)]
        raw_in = [sem(f"raw_in{s}") for s in range(6)]
        ACT_E, DVE_E, PE_E, POOL_E = "act", "dve", "pe", "pool"
        done = {e: sem(f"phase_done_{e}") for e in (ACT_E, DVE_E, PE_E, POOL_E)}
        half_set, y_filled = sem("half_set"), sem("y_filled")
        f_stat, f_pool, f_rstd, f_xn = sem("f_stat"), sem("f_pool"), sem("f_rstd"), sem("f_xn")
        f_tp0, f_tp1, f_ev0, f_ev1 = sem("f_tp0"), sem("f_tp1"), sem("f_ev0"), sem("f_ev1")
        a_mv, a_mc, a_mu = sem("a_mv"), sem("a_mc"), sem("a_mu")
        a_gv, a_gu, a_csq, a_rc = sem("a_gv"), sem("a_gu"), sem("a_csq"), sem("a_rc")
        a_v2, a_rv, a_cn, a_vn, a_m = sem("a_v2"), sem("a_rv"), sem("a_cn"), sem("a_vn"), sem("a_m")
        a_tc, a_ce, a_s = sem("a_tc"), sem("a_ce"), sem("a_s")
        a_pool_c, a_pool_v, a_dve = sem("a_pool_c"), sem("a_pool_v"), sem("a_dve")
        ws_t, ws_e, ws_dve = sem("ws_t"), sem("ws_e"), sem("ws_dve")
        b_proj = [sem(f"b_proj{i}") for i in range(4)]
        b_pev = [sem(f"b_pev{i}") for i in range(4)]
        b_kr, b_sq, b_ss, b_rs, b_qs, b_rp, b_qk = (sem(n) for n in
                                                  ("b_kr", "b_sq", "b_ss", "b_rs", "b_qs", "b_rp", "b_qk"))
        b_t = [sem(f"b_t{i}") for i in range(4)]
        b_tev = [sem(f"b_tev{i}") for i in range(4)]
        b_s, b_max, b_exp = sem("b_s"), sem("b_max"), sem("b_exp")
        b_pt, b_pte_a, b_pte_d = sem("b_pt"), sem("b_pte_a"), sem("b_pte_d")
        b_pv, b_o = sem("b_pv"), sem("b_o")
        b_dve, b_pool, b_pool2, b_max_c = (sem(n) for n in ("b_dve", "b_pool", "b_pool2", "b_max_c"))
        c_y0, c_y1, c_h0, c_h1 = sem("c_y0"), sem("c_y1"), sem("c_h0"), sem("c_h1")
        c_sf, c_rf, c_xf, c_xst = sem("c_sf"), sem("c_rf"), sem("c_xf"), sem("c_xst")
        c_f0, c_f1, c_fe0, c_fe1 = sem("c_f0"), sem("c_f1"), sem("c_fe0"), sem("c_fe1")
        c_rt, c_lgm, c_lge = sem("c_rt"), sem("c_lgm"), sem("c_lge")
        c_pool2, c_dve, c_dve2 = sem("c_pool2"), sem("c_dve"), sem("c_dve2")
        r_rank, r_dve, r_ovt, r_ovsb, r_ovs, r_exp, r_gap = (sem("r_rank"), sem("r_dve"), sem("r_ovt"), sem("r_ovsb"),
                                                     sem("r_ovs"), sem("r_exp"), sem("r_gap"))
        r_oh, r_idx = sem("r_oh"), sem("r_idx")
        r_plan = sem("r_plan")
        d_idx, d_xg = sem("d_idx"), sem("d_xg")
        d_tx, d_xhi0, d_xhi1, d_xlo0, d_xlo1 = sem("d_tx"), sem("d_xhi0"), sem("d_xhi1"), sem("d_xlo0"), sem("d_xlo1")
        d_hi, d_lo, d_mm = sem("d_hi"), sem("d_lo"), sem("d_mm")
        d_silu, d_gm, d_tg, d_ghi, d_glo = sem("d_silu"), sem("d_gm"), sem("d_tg"), sem("d_ghi"), sem("d_glo")
        d_yev, d_yst = sem("d_yev"), sem("d_yst")
        e_idx, e_yg = sem("e_idx"), [sem(f"e_yg{j}") for j in range(2)]
        e_comb = sem("e_comb")
        e_tpp, e_evp = sem("e_tpp"), sem("e_evp")
        e_g0, e_g1, e_pl = sem("e_g0"), sem("e_g1"), sem("e_pl")
        e_b0, e_b1, e_sg, e_h = sem("e_b0"), sem("e_b1"), sem("e_sg"), sem("e_h")
        e_dve, e_fin = sem("e_dve"), sem("e_fin")
        r_gates, r_sel = sem("r_gates"), sem("r_sel")

        def steady(eng):
            eng.nop(nofuse=True)

        def next_phase(eng, me, layer, phase):
            steady(eng)
            eng.drain().then_inc(done[me], 1)
            for other in done:
                eng.wait_ge(done[other], layer * PHASES + phase + 1)

        def over_tiles(eng, turn):
            turn(0, 0, True, False)
            steady(eng)
            with eng.Fori(0, NT // 2 - 1) as i:
                turn(i * 2 + 1, 1, False, False)
                turn(i * 2 + 2, 0, False, False)
            turn(NT - 1, 1, False, True)

        def credit(eng, n, *signals):
            for s in signals:
                eng.sem_inc(s, n)

        def grouped(ap, g):
            return ap.rearrange("p (g c) -> p g c", g=g)

        def spread(ap, n):
            return ap.unsqueeze(2).broadcast_to([ap.shape[0], ap.shape[1], n])

        block = ctx.enter_context(nc.Block())

        @block.sync
        def _(sp):
            def load_ab(layer):
                one = lambda v: v[ds(layer, 1)]
                sp.dma_start(w_in_sb[:, :, :], one(w_in_v).rearrange("o p k n -> p (o k) n")).then_inc(w_in_in, 16)
                sp.dma_start(g_mix_sb[:, :], one(g_mix_norm).broadcast_to([P, D])).then_inc(ab_in, 16)
                sp.dma_start(g_c_sb[:, 0:Q_RANK], one(g_cq).broadcast_to([P, Q_RANK])).then_inc(ab_in, 16)
                sp.dma_start(g_c_sb[:, Q_RANK:CQKV], one(g_ckv).broadcast_to([P, KV_RANK])).then_inc(ab_in, 16)
                sp.dma_start(g_v_sb[:, :], one(g_v_v).broadcast_to([P, 512])).then_inc(ab_in, 16)
                sp.dma_start(g_qk_sb[:, 0, :], one(g_qn).broadcast_to([P, QK])).then_inc(ab_in, 16)
                sp.dma_start(g_qk_sb[:, 1, :], one(g_kn).broadcast_to([P, QK])).then_inc(ab_in, 16)
                sp.dma_start(bs_sb[:, :], one(b_s_v).rearrange("o t g -> (o t) g"),
                             allow_slow_non_contiguous=True).then_inc(ab_in, 16)
                for dst, g0, g1 in ((ws_nat[0], 0, 6), (ws_nat[1], 6, GROUPS)):
                    sp.dma_start(grouped(dst[:, :], g1 - g0),
                                 one(w_s_v)[:, :, g0:g1, :].rearrange("o t g j -> t (o g) j")).then_inc(ab_in, 16)
                sp.dma_start(w_uq_sb[:, :, :], one(w_uq_v).rearrange("o p k n -> p (o k) n")).then_inc(ab_in, 16)
                sp.dma_start(w_ukv_sb[:, :], one(w_ukv).rearrange("o p n -> (o p) n")).then_inc(ab_in, 16)

            def chunk(layer, expert, which, part, slot):
                if which == 2:
                    src = w2_v[ds(layer * NE + expert, 1)][:, :, 2 * part:2 * part + 2, :]
                    dst = ring_raw[:, slot, :].rearrange("p (k n) -> p k n", k=2)
                else:
                    src = (w1_v if which == 1 else w3_v)[ds(layer * NE + expert, 1)][:, :, 4 * part:4 * part + 4, :]
                    dst = ring_raw[:, slot, :].rearrange("p (k n) -> p k n", k=4)
                sp.dma_start(dst, src.rearrange("o p k n -> p (o k) n")).then_inc(raw_in[slot], 16)

            sp.sem_inc(c_xst, 16)
            sp.dma_start(consts[:, :], shape_consts).then_inc(consts_in, 16)
            sp.dma_start(h[:, :].rearrange("p (t d) -> p t d", t=NT), x_v).then_inc(x_in, 16)
            load_ab(0)
            x_rows = x.rearrange("b s d -> (b s) d")
            for row in range(NE * P, NBLK * P, SEQ):
                n = min(SEQ, NBLK * P - row)
                sp.dma_start(y_rows[row:row + n, :], x_rows[0:n, :]).then_inc(y_filled, 16)
            with sp.Fori(0, DEPTH) as layer:
                ph = lambda e, phase: sp.wait_ge(done[e], layer * PHASES + phase + 1)
                ph(PE_E, PH_A)
                one = lambda v: v[ds(layer, 1)]
                sp.dma_start(w_out_sb[:, :, :], one(w_out_v).rearrange("o p k n -> p (o k) n")).then_inc(wout_in, 16)
                sp.dma_start(g_out_sb[:, 0:MIXW], one(g_out_mla).broadcast_to([P, MIXW])).then_inc(cpar_in, 16)
                sp.dma_start(g_out_sb[:, MIXW:D], one(g_out_gmlp).broadcast_to([P, MIXW])).then_inc(cpar_in, 16)
                sp.dma_start(g_ffn_sb[:, :], one(g_ffn_norm).broadcast_to([P, D])).then_inc(cpar_in, 16)
                sp.dma_start(w_router[:, :, 0:NG], one(w_rg_v).rearrange("o p k n -> p (o k) n")).then_inc(cpar_in, 16)
                sp.dma_start(w_router[:, :, NG:NROUTE], one(w_re_v).rearrange("o p k n -> p (o k) n")).then_inc(cpar_in, 16)
                steady(sp)
                with sp.Fori(0, NT) as t:
                    sp.wait_ge(c_xf, layer * NT + t + 1)
                    sp.dma_start(xn_v[ds(t, 1)].rearrange("o p d -> (o p) d"), xf[:, :]).then_inc(c_xst, 16)
                sp.wait_ge(c_rt, (layer + 1) * NT)
                steady(sp)
                before_here = sp.value_load(next_gb[0:1, ds(layer, 1)], min_val=0, max_val=DEPTH * NBLK)
                n = [0]

                def stream(expert, which, part, turn):
                    s = n[0]
                    n[0] += 1
                    sp.wait_ge(d_lo, before_here * 6 + turn * 6 + s + 1)
                    chunk(layer, expert, which, part, s % 6)

                for b in range(2):
                    for which in (1, 3):
                        for part in range(2):
                            stream(b, which, part, 0)

                def turn(b, before_last, this):
                    n[0] = 8
                    for part in range(2):
                        stream(before_last, 2, part, b - 2)
                    for which in (1, 3):
                        for part in range(2):
                            stream(this, which, part, b - 2)

                steady(sp)
                with sp.Fori(2, NE) as b:
                    turn(b, b - 2, b)
                sp.dma_start(w_gate_sb[:, :, :], one(w_gate_v).rearrange("o p k n -> p (o k) n")).then_inc(ple_w_in, 16)
                sp.dma_start(w_ple_sb[:, :, :], one(w_ple_v).rearrange("o p k n -> p (o k) n")).then_inc(ple_w_in, 16)
                sp.wait_ge(r_plan, layer + 1)
                steady(sp)
                nb2 = sp.value_load(plan[0:1, 0:1], min_val=NE - 2, max_val=NBLK - 2)
                nb = nb2 + 2
                expert_of = lambda b: sp.value_load(expert_i[0:1, ds(b, 1)], min_val=0, max_val=NE - 1)
                steady(sp)
                with sp.Fori(NE, NBLK) as b:
                    with sp.If(b < nb):
                        steady(sp)
                        turn(b, expert_of(b - 2), expert_of(b))
                n[0] = 8
                for back in (2, 1):
                    steady(sp)
                    e = expert_of(nb2 + 2 - back)
                    for part in range(2):
                        stream(e, 2, part, nb2)
                for e in (PE_E, DVE_E, ACT_E):
                    ph(e, PH_D)
                sp.dma_start(g_ple_sb[:, :], one(g_ple).broadcast_to([P, D])).then_inc(e_par_in, 16)
                sp.dma_start(b_gate_sb[:, :], one(b_ple_gate).broadcast_to([P, D])).then_inc(e_par_in, 16)

                def load_p(t, j):
                    sp.wait_ge(e_tpp, layer * NT + t + 1)
                    sp.dma_start(p_sb[j][:, :], p_v[ds(layer * NT + t, 1)].rearrange("o p d -> (o p) d"))\
                      .then_inc(p_in[j], 16)

                load_p(0, 0)
                load_p(1, 1)
                with sp.If(layer < DEPTH - 1):
                    load_ab(nc.s_assert_within(
                        layer + 1, min_val=1, max_val=DEPTH - 1,
                        skip_runtime_bounds_check_because="only where layer < DEPTH - 1"))
                steady(sp)
                with sp.Fori(1, NT // 2) as i:
                    load_p(i * 2, 0)
                    load_p(i * 2 + 1, 1)
            for t in range(NT):
                sp.wait_ge(e_h, (DEPTH - 1) * NT + t + 2)
                sp.dma_start(out_v[:, t, :], h[:, t * D:(t + 1) * D]).then_inc(out_done, 16)
            sp.wait_ge(out_done, 16 * NT)

        @block.gpsimd
        def _(pool):
            def rsqrt(out_ap, in_ap, scale, order, done, raises):
                n = in_ap.shape[1]
                steady(pool)
                pool.tensor_scalar(tmp_p[:, 0:n], in_ap, scale, EPS, ALU.mult, ALU.add).then_inc(order, 1)
                pool.wait_ge(order, done)
                pool.tensor_tensor(out_ap, tmp_p[:, 0:n], half[:, 0:n], ALU.pow).then_inc(raises, 1)

            pool.memset(half[:, :], -0.5).then_inc(half_set, 1)
            pool.wait_ge(half_set, 1)
            pool.wait_ge(consts_in, 16)
            with pool.Fori(0, DEPTH) as layer:
                it = lambda t: layer * NT + t
                ft = lambda phase, t: (layer * 3 + phase) * NT + t
                next_phase(pool, POOL_E, layer, PH_WS)

                def rstd_x_of(t, j):
                    pool.wait_ge(f_stat, ft(0, t) + 1)
                    rsqrt(rstd_x[:, j:j + 1], stat_x[:, j:j + 1], 1.0, f_pool, ft(0, t) + 1, f_rstd)
                    pool.wait_ge(f_rstd, ft(0, t) + 1)

                def turn(t, j, first, last):
                    if first:
                        rstd_x_of(0, 0)
                    if not last:
                        rstd_x_of(t + 1, 1 - j)
                    pool.wait_ge(a_csq, it(t) + 1)
                    rsqrt(rstd_c[:, :], stat_c[:, :], 1.0, a_pool_c, it(t) + 1, a_rc)
                    pool.wait_ge(a_rc, it(t) + 1)
                    pool.wait_ge(a_v2, it(t) + 1)
                    rsqrt(rstd_v[:, :], stat_v[:, :], 1.0 / GDIM, a_pool_v, it(t) + 1, a_rv)
                    pool.wait_ge(a_rv, it(t) + 1)

                over_tiles(pool, turn)
                next_phase(pool, POOL_E, layer, PH_A)

                def normalise(hd):
                    pool.wait_ge(b_tev[3], it(hd) + 1)
                    pool.wait_ge(b_tev[2], it(hd) + 1)
                    steady(pool)
                    pool.tensor_copy(qkb[:, 1, :, NOPE:QK], kr_all[:, :, :]).then_inc(b_kr, 1)
                    pool.wait_ge(b_ss, it(hd) + 1)
                    rsqrt(rstd_qk[:, :], stat_qk[:, :], 1.0, b_pool, it(hd) + 1, b_rs)
                    pool.wait_ge(b_qs, it(hd) + 1)
                    c = Count(2, it(hd))
                    for i in range(2):
                        ins = pool.tensor_tensor(qkb[:, i, :, :], qkb[:, i, :, :],
                                                 g_qk_sb[:, i:i + 1, :].broadcast_to([P, NT, QK]), ALU.mult)
                        ins.then_inc(b_pool2, 1)
                        pool.wait_ge(b_pool2, c.next())
                    c.close()
                    for i in range(2):
                        pool.tensor_tensor(rope_c[:, i, :, :], qkb[:, i, :, NOPE:QK], cos2, ALU.mult)
                        last = pool.tensor_tensor(rope_s[:, i, :, :], qkb[:, i, :, NOPE:QK], sin2, ALU.mult)
                    last.then_inc(b_rp, 1)

                def turn(hd, j, first, last):
                    if first:
                        normalise(0)
                    if not last:
                        normalise(hd + 1)

                over_tiles(pool, turn)
                next_phase(pool, POOL_E, layer, PH_B)

                def rstd_c_of(t):
                    pool.wait_ge(f_stat, ft(1, t) + 1)
                    rsqrt(rstd_c[:, :], stat_c[:, :], 1.0, f_pool, ft(1, t) + 1, f_rstd)
                    pool.wait_ge(f_rstd, ft(1, t) + 1)

                def turn(t, j, first, last):
                    if first:
                        rstd_c_of(0)
                    if not last:
                        rstd_c_of(t + 1)
                    pool.wait_ge(c_sf, it(t) + 2)
                    rsqrt(rstd_f[:, :], stat_f[:, :], 1.0, c_pool2, it(t) + 1, c_rf)
                    pool.wait_ge(c_rf, it(t) + 1)

                over_tiles(pool, turn)
                next_phase(pool, POOL_E, layer, PH_C)

                pool.wait_ge(c_xst, (layer * NT + NT + 1) * 16)
                pool.wait_ge(r_plan, layer + 1)
                steady(pool)
                nb2 = pool.value_load(plan[0:1, 0:1], min_val=NE - 2, max_val=NBLK - 2)
                nb = nb2 + 2
                gb = pool.value_load(plan[0:1, 1:2], min_val=0, max_val=DEPTH * NBLK)

                def gather(b):
                    pool.wait_ge(d_tx, gb + b + 1)
                    steady(pool)
                    pool.tensor_copy(idx_x[:, :], slot_tok[:, ds(b, 1)]).then_inc(d_idx, 1)
                    pool.wait_ge(d_idx, gb + b + 1)
                    steady(pool)
                    pool.indirect_dma_start(xg[:, :], None, xn_rows,
                                            bass.IndirectOffsetOnAxis(ap=idx_x[:, :], axis=0)).then_inc(d_xg, 16)

                steady(pool)
                with pool.Fori(0, NE) as b:
                    gather(b)
                steady(pool)
                with pool.Fori(NE, NBLK) as b:
                    with pool.If(b < nb):
                        gather(b)
                next_phase(pool, POOL_E, layer, PH_D)

                pool.wait_ge(d_yst, (gb + nb + 1) * 16)

                def gather2(t, j):
                    pool.wait_ge(e_comb, it(t) + 1)
                    steady(pool)
                    for k in range(TOPK):
                        pool.tensor_copy(idx_y[j][k][:, :], dest_u[:, ds(t + k * NT, 1)]).then_inc(e_idx, 1)
                    pool.wait_ge(e_idx, (it(t) + 1) * 2)
                    steady(pool)
                    for k in range(TOPK):
                        pool.indirect_dma_start(yg[j][k][:, :], None, y_rows,
                                                bass.IndirectOffsetOnAxis(ap=idx_y[j][k][:, :], axis=0))\
                            .then_inc(e_yg[j], 16)

                def rstd_e(t, j):
                    pool.wait_ge(f_stat, ft(2, t) + 1)
                    rsqrt(rstd_x[:, j:j + 1], stat_x[:, j:j + 1], 1.0, f_pool, ft(2, t) + 1, f_rstd)
                    pool.wait_ge(f_rstd, ft(2, t) + 1)

                def turn(t, j, first, last):
                    if first:
                        gather2(0, 0)
                        rstd_e(0, 0)
                    if not last:
                        gather2(t + 1, 1 - j)
                        rstd_e(t + 1, 1 - j)

                over_tiles(pool, turn)
                next_phase(pool, POOL_E, layer, PH_E)

        @block.scalar
        def _(act):
            credit(act, 1, c_sf, f_ev0, a_gv, a_gu, a_ce, b_pev[1], b_pev[2], b_tev[1], b_tev[3], b_pte_a,
                   c_fe0, c_lge, d_silu, d_yev, e_evp)
            credit(act, 2, b_exp)
            act.sem_inc(d_yst, 16)
            act.wait_ge(consts_in, 16)
            act.wait_ge(x_in, 16)

            def copy(out_ap, in_ap):
                return act.activation(out_ap, in_ap, ACT.Copy)

            with act.Fori(0, DEPTH) as layer:
                it = lambda t: layer * NT + t
                ft = lambda phase, t: (layer * 3 + phase) * NT + t
                h_t = lambda t: h[:, ds(t * D, D)]
                next_phase(act, ACT_E, layer, PH_WS)

                def front(t, j):
                    steady(act)
                    act.activation(junk[:, :], h_t(t), ACT.Square, scale=float(D) ** -0.5,
                                   accum_out=stat_x[:, j:j + 1]).then_inc(f_stat, 1)
                    act.wait_ge(f_tp0, ft(0, t) + 1)
                    copy(xT[j][:, 0:4, :], grouped(bank(0), 4)).then_inc(f_ev0, 1)

                def turn(t, j, first, last):
                    if first:
                        front(0, 0)
                    if not last:
                        front(t + 1, 1 - j)
                    act.wait_ge(a_mv, it(t) + 1)
                    act.wait_ge(a_m, it(t) + 1)
                    act.activation(gv_sb[:, :], bank(4), ACT.Gelu_apprx_tanh).then_inc(a_gv, 1)
                    act.wait_ge(a_mc, it(t) + 1)
                    act.activation(junk_c[:, 0:Q_RANK], bank(2)[:, 0:Q_RANK], ACT.Square, scale=float(Q_RANK) ** -0.5,
                                   accum_out=stat_c[:, 0:1])
                    act.activation(junk_c[:, Q_RANK:CQKV], bank(2)[:, Q_RANK:CQKV], ACT.Square,
                                   scale=float(KV_RANK) ** -0.5, accum_out=stat_c[:, 1:2]).then_inc(a_csq, 1)
                    act.wait_ge(a_mu, it(t) + 1)
                    act.activation(gu_sb[:, :], bank(3), ACT.Gelu_apprx_tanh).then_inc(a_gu, 1)
                    act.wait_ge(a_tc, it(t) + 2)
                    steady(act)
                    copy(cT[:, :, ds(t * P, P)], grouped(bank(5)[:, 0:CQKV], 3)).then_inc(a_ce, 1)

                over_tiles(act, turn)
                next_phase(act, ACT_E, layer, PH_A)

                def front_ev(step, hd, j):
                    if step == 1:
                        act.wait_ge(b_proj[1], it(hd) + 1)
                        copy(qkb[:, 0, 4:8, :], grouped(bank(0)[:, 0:4 * QK], 4)).then_inc(b_pev[1], 1)
                    elif step == 2:
                        act.wait_ge(b_proj[2], it(hd) + 1)
                        kv = grouped(bank(0), 4)
                        copy(qkb[:, 1, 0:4, 0:NOPE], kv[:, :, 0:NOPE])
                        copy(v_sb[j][:, 0:4, :], kv[:, :, NOPE:P]).then_inc(b_pev[2], 1)
                    elif step == 4:
                        for k in range(4):
                            act.wait_ge(b_pev[k], it(hd) + 2)
                        act.wait_ge(b_kr, it(hd) + 1)
                        act.activation(qksq[:, :, :, :], qkb[:, :, :, :], ACT.Square,
                                       scale=SCALE).then_inc(b_sq, 1)
                    elif step == 7:
                        act.wait_ge(b_t[1], it(hd) + 1)
                        copy(qkT[j][:, 0, 512:1024], bank(0)[0:QK, :]).then_inc(b_tev[1], 1)
                    elif step == 8:
                        act.wait_ge(b_t[3], it(hd) + 1)
                        copy(qkT[j][:, 1, 512:1024], bank(3)[0:QK, :]).then_inc(b_tev[3], 1)

                def exp_of(hd, i):
                    act.wait_ge(b_max, it(hd) * 8 + i + 1)
                    before_i = sum(1 + (m >= 4) for m in range(i)) - (0 if i == 0 else 1 + (i - 1 >= 4))
                    act.wait_ge(b_pt, it(hd) * 12 + (before_i if i >= 2 else (0 if i == 1 else -2)) + 12)
                    w = (i + 1) * P
                    act.activation(prob[i % 2][:, 0:w], bank(2 + 2 * (i % 2), 2)[:, 0:w], ACT.Exp,
                                   bias=neg_max[:, i % 2:i % 2 + 1], scale=SCALE,
                                   accum_out=row_sum[:, i:i + 1]).then_inc(b_exp, 1)

                def turn(hd, j, first, last):
                    if first:
                        for step in range(9):
                            front_ev(step, 0, 0)
                    act.wait_ge(b_o, it(hd) + 1)
                    exp_of(hd, 0)
                    g = 0
                    for i in range(NT):
                        for gi in range(1 + (i >= 4)):
                            if g % 2 == 0:
                                act.wait_ge(b_pt, it(hd) * 12 + g + 13)
                                n = min(4, i + 1 - 4 * gi)
                                copy(probT[:, 4 * gi:4 * gi + n, :], grouped(bank(1)[:, 0:n * P], n))\
                                    .then_inc(b_pte_a, 1)
                            g += 1
                        if i + 1 < NT:
                            exp_of(hd, i + 1)
                        if not last:
                            front_ev(i, hd + 1, 1 - j)
                    if not last:
                        front_ev(8, hd + 1, 1 - j)

                over_tiles(act, turn)
                next_phase(act, ACT_E, layer, PH_B)

                def stats(t):
                    act.wait_ge(f_xn, ft(1, t) + 1)
                    steady(act)
                    act.activation(junk[:, 0:MIXW], a_all[:, ds(t, 1), :].rearrange("p o c -> p (o c)"), ACT.Square,
                                   scale=float(MIXW) ** -0.5, accum_out=stat_c[:, 0:1])
                    act.activation(junk[:, MIXW:D], m_all[:, ds(t * MIXW, MIXW)], ACT.Square,
                                   scale=float(MIXW) ** -0.5, accum_out=stat_c[:, 1:2]).then_inc(f_stat, 1)

                def front(t, j):
                    act.wait_ge(f_tp0, ft(1, t) + 1)
                    copy(xT[j][:, 0:4, :], grouped(bank(0), 4)).then_inc(f_ev0, 1)

                def tail_ev(t):
                    act.wait_ge(c_f0, it(t) + 1)
                    copy(xfT[:, 0:4, :], grouped(bank(4), 4)).then_inc(c_fe0, 1)

                def tail_exp(t):
                    act.wait_ge(c_lgm, it(t) + 1)
                    steady(act)
                    act.activation(lge[:, :], lgm[:, :], ACT.Exp, accum_out=sum_all[:, ds(t, 1)]).then_inc(c_lge, 1)

                def turn(t, j, first, last):
                    if first:
                        stats(0)
                        front(0, 0)
                    if not last:
                        act.wait_ge(c_sf, it(t) + 1)
                        stats(t + 1)
                    if not first:
                        tail_ev(t - 1)
                    if not last:
                        front(t + 1, 1 - j)
                    act.wait_ge(c_h1, it(t) + 2)
                    steady(act)
                    act.activation(junk[:, :], h_t(t), ACT.Square, scale=float(D) ** -0.5,
                                   accum_out=stat_f[:, :]).then_inc(c_sf, 1)
                    if not first:
                        tail_exp(t - 1)
                    if last:
                        tail_ev(t)
                        tail_exp(t)

                over_tiles(act, turn)
                act.wait_ge(r_gap, layer + 1)
                act.activation(exp_g[:, :], gap_all[:, :], ACT.Exp).then_inc(r_exp, 1)
                next_phase(act, ACT_E, layer, PH_C)

                steady(act)
                nb2 = act.value_load(plan[0:1, 0:1], min_val=NE - 2, max_val=NBLK - 2)
                nb = nb2 + 2
                gb = act.value_load(plan[0:1, 1:2], min_val=0, max_val=DEPTH * NBLK)

                def hi(s, turns):
                    q = s % 6
                    act.wait_ge(raw_in[q], (gb + turns + (s // 6 + 1)) * 16)
                    act.wait_ge(d_mm, gb * 6 + turns * 6 + s + 1)
                    copy(ring_hi[:, s % 3, :], ring_raw[:, q, :]).then_inc(d_hi, 1)

                def x_hi(b):
                    for i, s in enumerate((d_xhi0, d_xhi1)):
                        act.wait_ge(d_tx, gb + b + 2)
                        copy(xg_hi[:, 4 * i:4 * i + 4, :], grouped(bank(i), 4)).then_inc(s, 1)

                def silu_of(b, chunks):
                    act.wait_ge(d_mm, gb * 6 + chunks + 3)
                    act.wait_ge(d_gm, gb + b + 1)
                    act.activation(silu_sb[:, :], bank(3), ACT.Silu).then_inc(d_silu, 1)

                def g_hi(b):
                    act.wait_ge(d_tg, gb + b + 2)
                    copy(gT_hi[:, :, :], grouped(bank(2), 4)).then_inc(d_ghi, 1)

                def y_out(b, chunks):
                    act.wait_ge(d_mm, gb * 6 + chunks + 3)
                    act.wait_ge(d_yst, (gb + b + 1) * 16)
                    for i in range(2):
                        last = copy(y_sb[:, i * 512:(i + 1) * 512], bank(5 + i))
                    last.then_inc(d_yev, 1)
                    act.wait_ge(d_yev, gb + b + 2)
                    steady(act)
                    act.dma_start(y_v[ds(b, 1)].rearrange("o p d -> (o p) d"), y_sb[:, :]).then_inc(d_yst, 16)

                act.wait_ge(y_filled, 16 * -(-MAX_OVER * P // SEQ))
                x_hi(0)
                for s in range(3):
                    hi(s, 0)
                hi(3, 0)
                silu_of(0, 2)
                x_hi(1)
                for s in (4, 5):
                    hi(s, 0)
                g_hi(0)
                for s in (6, 7, 8, 9):
                    hi(s, 0)

                def turn(b):
                    silu_of(b - 1, (b - 2) * 6 + 6)
                    x_hi(b)
                    hi(10, b - 2)
                    hi(11, b - 2)
                    y_out(b - 2, (b - 2) * 6 + 10)
                    g_hi(b - 1)
                    for s in (12, 13, 14, 15):
                        hi(s, b - 2)

                steady(act)
                with act.Fori(2, NE) as b:
                    turn(b)
                steady(act)
                with act.Fori(NE, NBLK) as b:
                    with act.If(b < nb):
                        turn(b)
                silu_of(nb2 + 1, (nb2) * 6 + 6)
                y_out(nb2, (nb2) * 6 + 10)
                g_hi(nb2 + 1)
                for s in (10, 11):
                    hi(s, nb2)
                y_out(nb2 + 1, (nb2) * 6 + 12)
                next_phase(act, ACT_E, layer, PH_D)

                def front(t, j):
                    act.wait_ge(e_comb, it(t) + 3)
                    steady(act)
                    act.activation(junk[:, :], h_t(t), ACT.Square, scale=float(D) ** -0.5,
                                   accum_out=stat_x[:, j:j + 1]).then_inc(f_stat, 1)
                    act.wait_ge(f_tp0, ft(2, t) + 1)
                    copy(xT[j][:, 0:4, :], grouped(bank(0), 4)).then_inc(f_ev0, 1)
                    act.wait_ge(e_tpp, it(t) + 3)
                    copy(pT[j][:, :, :], grouped(bank(6)[:, 0:PLE], 2)).then_inc(e_evp, 1)

                def turn(t, j, first, last):
                    if first:
                        front(0, 0)
                    if not last:
                        front(t + 1, 1 - j)
                    act.wait_ge(e_b1, it(t) + 2)
                    act.activation(gs[:, :], gs[:, :], ACT.Sigmoid).then_inc(e_sg, 1)

                over_tiles(act, turn)
                next_phase(act, ACT_E, layer, PH_E)

        @block.vector
        def _(dve):
            credit(dve, 1, f_xn, f_ev1, a_cn, a_m, b_pev[0], b_pev[3], b_tev[0], b_tev[2], b_pte_d, b_o, c_h0,
                   c_h1, c_fe1, d_xlo0, d_xlo1, d_gm, d_glo, e_b0, e_b1, e_h)
            credit(dve, 2, e_comb)
            credit(dve, 6, d_lo)
            dve.memset(next_gb[:, :], 0)
            dve.memset(gb_f[:, :], 0.0)
            dve.memset(lg8[:, :], NEG)
            dve.memset(picks[:, 0, :], 0.0)
            dve.wait_ge(consts_in, 16)
            dve.wait_ge(x_in, 16)
            dve.tensor_copy(expert_i[:, 0:NE], iota_e)
            stt = dve.scalar_tensor_tensor
            tt = dve.tensor_tensor
            ts = dve.tensor_scalar

            with dve.Fori(0, DEPTH) as layer:
                it = lambda t: layer * NT + t
                ft = lambda phase, t: (layer * 3 + phase) * NT + t
                h_t = lambda t: h[:, ds(t * D, D)]

                c = Count(2, layer)
                for i in range(2):
                    dve.wait_ge(ws_t, layer * 2 + i + 1)
                    dve.tensor_copy(wsT[:, 4 * i:4 * i + 4, :], grouped(bank(i), 4)).then_inc(ws_dve, 1)
                    dve.wait_ge(ws_dve, c.next())
                c.close()
                dve.memset(wsT[CHUNK:P, :, 0:CHUNK], 0.0).then_inc(ws_e, 1)
                dve.wait_ge(ab_in, 16 * AB_LOADS * (layer + 1))
                next_phase(dve, DVE_E, layer, PH_WS)

                def front(t, j):
                    dve.wait_ge(f_rstd, ft(0, t) + 1)
                    stt(xn[j][:, :], h_t(t), rstd_x[:, j:j + 1], g_mix_sb[:, :], ALU.mult, ALU.mult)\
                        .then_inc(f_xn, 1)
                    dve.wait_ge(f_tp1, ft(0, t) + 1)
                    dve.tensor_copy(xT[j][:, 4:8, :], grouped(bank(1), 4)).then_inc(f_ev1, 1)

                def turn(t, j, first, last):
                    if first:
                        front(0, 0)
                    if not last:
                        front(t + 1, 1 - j)
                    c = Count(3, it(t))
                    dve.wait_ge(a_gv, it(t) + 2)
                    tt(vsq[:, :], gv_sb[:, :], gv_sb[:, :], ALU.mult).then_inc(a_dve, 1)
                    dve.wait_ge(a_dve, c.next())
                    dve.reduce_sum(stat_v[:, :], grouped(vsq[:, :], GROUPS), axis=AX_X).then_inc(a_v2, 1)
                    dve.wait_ge(a_rc, it(t) + 1)
                    dve.wait_ge(a_tc, it(t) + 1)
                    stt(cn[:, 0:Q_RANK], bank(2)[:, 0:Q_RANK], rstd_c[:, 0:1], g_c_sb[:, 0:Q_RANK], ALU.mult, ALU.mult)
                    stt(cn[:, Q_RANK:CQKV], bank(2)[:, Q_RANK:CQKV], rstd_c[:, 1:2], g_c_sb[:, Q_RANK:CQKV],
                        ALU.mult, ALU.mult)
                    dve.tensor_copy(kr_all[:, ds(t, 1), :].rearrange("p o r -> p (o r)"), bank(2)[:, CQKV:W_C])\
                        .then_inc(a_cn, 1)
                    dve.wait_ge(a_rv, it(t) + 1)
                    dve.wait_ge(a_s, it(t) + 1)
                    tt(grouped(vn1[:, :], GROUPS), grouped(gv_sb[:, :], GROUPS), spread(rstd_v[:, :], GDIM), ALU.mult).then_inc(a_dve, 1)
                    dve.wait_ge(a_dve, c.next())
                    tt(vn[:, :], vn1[:, :], g_v_sb[:, :], ALU.mult).then_inc(a_vn, 1)
                    dve.wait_ge(a_s, it(t) + 2)
                    tt(grouped(s_sb[:, :], GROUPS), grouped(bank(6), GROUPS), spread(bs_sb[:, :], GDIM), ALU.add).then_inc(a_dve, 1)
                    dve.wait_ge(a_dve, c.next())
                    c.close()
                    dve.wait_ge(a_gu, it(t) + 2)
                    tt(m_all[:, ds(t * 512, 512)], s_sb[:, :], gu_sb[:, :], ALU.mult).then_inc(a_m, 1)

                over_tiles(dve, turn)
                next_phase(dve, DVE_E, layer, PH_A)

                def front_ev(step, hd, j):
                    if step == 0:
                        dve.wait_ge(b_proj[0], it(hd) + 1)
                        dve.tensor_copy(qkb[:, 0, 0:4, :], grouped(bank(0)[:, 0:4 * QK], 4)).then_inc(b_pev[0], 1)
                    elif step == 3:
                        dve.wait_ge(b_proj[3], it(hd) + 1)
                        kv = grouped(bank(0), 4)
                        dve.tensor_copy(qkb[:, 1, 4:8, 0:NOPE], kv[:, :, 0:NOPE])
                        dve.tensor_copy(v_sb[j][:, 4:8, :], kv[:, :, NOPE:P]).then_inc(b_pev[3], 1)
                    elif step == 4:
                        dve.wait_ge(b_sq, it(hd) + 1)
                        dve.reduce_sum(stat_qk[:, :], qksq[:, :, :, :].rearrange("p a t c -> p (a t) c"),
                                       axis=AX_X).then_inc(b_ss, 1)
                    elif step == 5:
                        dve.wait_ge(b_rs, it(hd) + 1)
                        v = qkb[:, :, :, :].rearrange("p a t c -> p (a t) c")
                        tt(v, v, spread(rstd_qk[:, :], QK), ALU.mult).then_inc(b_qs, 1)
                    elif step == 6:
                        dve.wait_ge(b_rp, it(hd) + 1)
                        flat = lambda a: a[:, :, :, :].rearrange("p a t c -> p (a t) c")
                        q, rc, rs = flat(qkb), flat(rope_c), flat(rope_s)
                        hf = ROPE // 2
                        tt(q[:, :, NOPE:NOPE + hf], rc[:, :, 0:hf], rs[:, :, hf:ROPE], ALU.subtract)
                        tt(q[:, :, NOPE + hf:QK], rc[:, :, hf:ROPE], rs[:, :, 0:hf], ALU.add).then_inc(b_qk, 1)
                        dve.wait_ge(b_t[0], it(hd) + 1)
                        dve.tensor_copy(qkT[j][:, 0, 0:512], bank(0)[0:QK, :]).then_inc(b_tev[0], 1)
                    elif step == 8:
                        dve.wait_ge(b_t[2], it(hd) + 1)
                        dve.tensor_copy(qkT[j][:, 1, 0:512], bank(2)[0:QK, :]).then_inc(b_tev[2], 1)

                def max_of(hd, i):
                    w = (i + 1) * P
                    s = bank(2 + 2 * (i % 2), 2)
                    c = Count(2, it(hd) * 8 + i)
                    dve.wait_ge(b_s, it(hd) * 8 + i + 1)
                    dve.memset(s[0:CHUNK, w - CHUNK:w], NEG).then_inc(b_max_c, 1)
                    dve.wait_ge(b_max_c, c.next())
                    dve.reduce_max(row_max[:, i % 2:i % 2 + 1], s[:, 0:w], axis=AX_X).then_inc(b_max_c, 1)
                    dve.wait_ge(b_max_c, c.next())
                    dve.wait_ge(b_exp, it(hd) * 8 + i + 1)
                    ts(neg_max[:, i % 2:i % 2 + 1], row_max[:, i % 2:i % 2 + 1], -SCALE, None, ALU.mult)\
                        .then_inc(b_max, 1)

                def turn(hd, j, first, last):
                    if first:
                        for step in range(9):
                            front_ev(step, 0, 0)
                    max_of(hd, 0)
                    g = 0
                    for i in range(NT):
                        if i + 1 < NT:
                            max_of(hd, i + 1)
                        for gi in range(1 + (i >= 4)):
                            if g % 2 == 1:
                                dve.wait_ge(b_pt, it(hd) * 12 + g + 13)
                                n = min(4, i + 1 - 4 * gi)
                                dve.tensor_copy(probT[:, 4 * gi:4 * gi + n, :], grouped(bank(6)[:, 0:n * P], n))\
                                    .then_inc(b_pte_d, 1)
                            g += 1
                        if not last:
                            front_ev(i, hd + 1, 1 - j)
                    if not last:
                        front_ev(8, hd + 1, 1 - j)
                    dve.wait_ge(b_exp, it(hd) * 8 + 10)
                    dve.reciprocal(row_inv[:, :], row_sum[:, :]).then_inc(b_dve, 1)
                    dve.wait_ge(b_dve, it(hd) + 1)
                    dve.wait_ge(b_pv, it(hd) + 1)
                    tt(a_all[:, :, ds(hd * VDIM, VDIM)], grouped(bank(7), NT), spread(row_inv[:, :], VDIM), ALU.mult)\
                        .then_inc(b_o, 1)

                over_tiles(dve, turn)
                dve.wait_ge(cpar_in, 16 * 5 * (layer + 1))
                next_phase(dve, DVE_E, layer, PH_B)

                def cat(t, j):
                    dve.wait_ge(f_rstd, ft(1, t) + 1)
                    stt(xn[j][:, 0:MIXW], a_all[:, ds(t, 1), :].rearrange("p o c -> p (o c)"), rstd_c[:, 0:1],
                        g_out_sb[:, 0:MIXW], ALU.mult, ALU.mult)
                    stt(xn[j][:, MIXW:D], m_all[:, ds(t * MIXW, MIXW)], rstd_c[:, 1:2],
                        g_out_sb[:, MIXW:D], ALU.mult, ALU.mult).then_inc(f_xn, 1)

                def cat_ev(t, j):
                    dve.wait_ge(f_tp1, ft(1, t) + 1)
                    dve.tensor_copy(xT[j][:, 4:8, :], grouped(bank(1), 4)).then_inc(f_ev1, 1)

                def tail_ev(t):
                    dve.wait_ge(c_f1, it(t) + 2)
                    dve.tensor_copy(xfT[:, 4:8, :], grouped(bank(5), 4)).then_inc(c_fe1, 1)

                def route(t):
                    c = Count(12, it(t))
                    dve.wait_ge(c_rt, it(t) + 1)
                    dve.tensor_copy(le[:, :], bank(6)[:, NG:NROUTE])
                    dve.tensor_copy(lg8[:, 0:NG], bank(6)[:, 0:NG]).then_inc(c_dve, 1)
                    dve.wait_ge(c_dve, c.next())
                    steady(dve)
                    dve.max(top8[:, :], lg8[:, :]).then_inc(c_dve, 1)
                    dve.wait_ge(c_dve, c.next())
                    dve.wait_ge(c_lge, it(t) + 1)
                    ts(lgm[:, :], lg8[:, 0:NG], top8[:, 0:1], None, ALU.subtract).then_inc(c_lgm, 1)
                    dve.max_index(gi8[:, :], top8[:, :], lg8[:, :]).then_inc(c_dve, 1)
                    dve.wait_ge(c_dve, c.next())
                    dve.tensor_copy(gf[:, :], gi8[:, 0:1]).then_inc(c_dve, 1)
                    dve.wait_ge(c_dve, c.next())
                    ts(gmask[:, :], iota_e[:, 0:NG], gf[:, 0:1], None, ALU.is_equal).then_inc(c_dve, 1)
                    dve.wait_ge(c_dve, c.next())
                    ts(gbias[:, :], gmask[:, :], -NEG, NEG, ALU.mult, ALU.add).then_inc(c_dve, 1)
                    dve.wait_ge(c_dve, c.next())
                    tt(grouped(le[:, :], NG), grouped(le[:, :], NG), spread(gmask[:, :], PER_G), ALU.mult).then_inc(c_dve, 1)
                    dve.wait_ge(c_dve, c.next())
                    tt(grouped(le[:, :], NG), grouped(le[:, :], NG), spread(gbias[:, :], PER_G), ALU.add).then_inc(c_dve, 1)
                    dve.wait_ge(c_dve, c.next())
                    steady(dve)
                    dve.max(top8e[:, :], le[:, :]).then_inc(c_dve, 1)
                    dve.wait_ge(c_dve, c.next())
                    tt(gap_all[:, ds(t, 1)], top8e[:, 1:2], top8e[:, 0:1], ALU.subtract)
                    dve.max_index(ei8[:, :], top8e[:, :], le[:, :]).then_inc(c_dve, 1)
                    dve.wait_ge(c_dve, c.next())
                    for k in range(TOPK):
                        last = dve.tensor_copy(ef_all[:, k, ds(t, 1)], ei8[:, k:k + 1])
                    last.then_inc(c_dve, 1)
                    dve.wait_ge(c_dve, c.next())
                    for k in range(TOPK):
                        last = ts(onehot[:, k, ds(t, 1), :].rearrange("p o e -> p (o e)"), iota_e,
                                  ef_all[:, k, ds(t, 1)], None, ALU.is_equal)
                    last.then_inc(c_dve, 1)
                    dve.wait_ge(c_dve, c.next())
                    c.close()
                    c = Count(2, it(t))
                    one = lambda a: a.rearrange("p o e -> p (o e)")
                    tt(one(chosen[:, ds(t, 1), :]), one(onehot[:, 0, ds(t, 1), :]), one(onehot[:, 1, ds(t, 1), :]),
                              ALU.add).then_inc(c_dve2, 1)
                    dve.wait_ge(c_dve2, c.next())
                    tt(one(picks[:, ds(t + 1, 1), :]), one(picks[:, ds(t, 1), :]), one(chosen[:, ds(t, 1), :]),
                              ALU.add).then_inc(c_dve2, 1)
                    dve.wait_ge(c_dve2, c.next())
                    c.close()

                def turn(t, j, first, last):
                    if first:
                        cat(0, 0)
                        cat_ev(0, 0)
                    if not last:
                        cat(t + 1, 1 - j)
                    if not first:
                        tail_ev(t - 1)
                    if not last:
                        cat_ev(t + 1, 1 - j)
                    for i, (y, hs) in enumerate(((c_y0, c_h0), (c_y1, c_h1))):
                        dve.wait_ge(y, it(t) + 1)
                        part = h[:, ds(t * D + i * 512, 512)]
                        tt(part, bank(2 + i), part, ALU.add).then_inc(hs, 1)
                    if not first:
                        route(t - 1)
                    dve.wait_ge(c_rf, it(t) + 1)
                    dve.wait_ge(c_f1, it(t) + 1)
                    dve.wait_ge(c_xst, (it(t) + 1) * 16)
                    stt(xf[:, :], h_t(t), rstd_f[:, 0:1], g_ffn_sb[:, :], ALU.mult, ALU.mult).then_inc(c_xf, 1)
                    if last:
                        tail_ev(t)
                        route(t)

                over_tiles(dve, turn)

                R_LINKS = 20
                c = Count(R_LINKS, layer)
                dve.tensor_copy(rank_k[:, 0:NT], gap_all[:, :]).then_inc(r_dve, 1)
                dve.wait_ge(r_dve, c.next())
                dve.sem_inc(r_gap, 1)
                dve.wait_ge(r_rank, layer + 1)
                dve.tensor_copy(rank_sb[:, :, :], grouped(bank(0)[:, 0:NT * NE], NT))
                cmp7 = cmp_s[:, 0:NE * 7].rearrange("p (e s) -> p e s", s=7)
                tt(cmp7, spread(bank(1)[:, 0:NE], 7), steps[:, 0:7].unsqueeze(1).broadcast_to([P, NE, 7]), ALU.is_gt).then_inc(r_dve, 1)
                dve.wait_ge(r_dve, c.next())
                dve.reduce_sum(over_e[:, :], cmp7, axis=AX_X).then_inc(r_dve, 1)
                dve.wait_ge(r_dve, c.next())
                dve.reduce_sum(nb_f[:, :], over_e[:, :], axis=AX_X).then_inc(r_dve, 1)
                dve.wait_ge(r_dve, c.next())
                dve.sem_inc(r_ovt, 1)
                ts(nb_f[:, :], nb_f[:, :], float(NE), None, ALU.add).then_inc(r_dve, 1)
                dve.wait_ge(r_dve, c.next())
                ts(nb2_f[:, :], nb_f[:, :], -2.0, None, ALU.add).then_inc(r_dve, 1)
                dve.wait_ge(r_dve, c.next())
                dve.tensor_copy(plan[:, 0:1], nb2_f[:, :])
                dve.tensor_copy(plan[:, 1:2], gb_f[:, :])
                tt(gb_f[:, :], gb_f[:, :], nb_f[:, :], ALU.add).then_inc(r_dve, 1)
                dve.wait_ge(r_dve, c.next())
                dve.wait_ge(r_ovsb, layer * 2 + 1)
                dve.tensor_copy(overT[:, :], bank(2)[0:NE, 0:P]).then_inc(r_ovs, 1)
                dve.wait_ge(r_ovsb, layer * 2 + 2)
                dve.tensor_copy(over_s[:, :], bank(3)[:, 0:NE]).then_inc(r_dve, 1)
                dve.wait_ge(r_dve, c.next())
                tt(over_end[:, :], over_s[:, :], over_e[:, :], ALU.add).then_inc(r_dve, 1)
                dve.wait_ge(r_dve, c.next())
                cmp16 = cmp_s[:, :].rearrange("p (b e) -> p b e", e=NE)
                tt(cmp16, over_end[:, :].unsqueeze(1).broadcast_to([P, 16, NE]), spread(over_id, NE), ALU.is_le).then_inc(r_dve, 1)
                dve.wait_ge(r_dve, c.next())
                dve.reduce_sum(ex_f[:, :], cmp16, axis=AX_X).then_inc(r_dve, 1)
                dve.wait_ge(r_dve, c.next())
                ts(ex_f[:, :], ex_f[:, :], float(NE - 1), None, ALU.min).then_inc(r_dve, 1)
                dve.wait_ge(r_dve, c.next())
                dve.tensor_copy(expert_i[:, NE:NE + 16], ex_f[:, :])
                c2 = Count(4 * TOPK, layer)
                for k in range(TOPK):
                    for src, dst in ((rank_sb[:, :, :], rank_k),
                                     (over_s[:, :].unsqueeze(1).broadcast_to([P, NT, NE]), ovs_k)):
                        tt(sel[:, :, :], onehot[:, k, :, :], src, ALU.mult).then_inc(r_sel, 1)
                        dve.wait_ge(r_sel, c2.next())
                        dve.reduce_sum(dst[:, k * NT:(k + 1) * NT], sel[:, :, :], axis=AX_X).then_inc(r_sel, 1)
                        dve.wait_ge(r_sel, c2.next())
                ef = ef_all[:, :, :].rearrange("p k t -> p (k t)")
                cmpr = cmp_s[:, 0:16 * 7].rearrange("p (t s) -> p t s", s=7)
                tt(cmpr, spread(rank_k[:, :], 7), steps[:, 0:7].unsqueeze(1).broadcast_to([P, 16, 7]), ALU.is_ge).then_inc(r_dve, 1)
                dve.wait_ge(r_dve, c.next())
                dve.reduce_sum(q_k[:, :], cmpr, axis=AX_X).then_inc(r_dve, 1)
                dve.wait_ge(r_dve, c.next())
                ts(ge_k[:, :], q_k[:, :], 1.0, None, ALU.is_ge)
                tt(blk_k[:, :], q_k[:, :], ovs_k[:, :], ALU.add).then_inc(r_dve, 1)
                dve.wait_ge(r_dve, c.next())
                stt(row_k[:, :], q_k[:, :], -float(P), rank_k[:, :], ALU.mult, ALU.add)
                stt(blk_k[:, :], blk_k[:, :], float(NE - 1), ef, ALU.add, ALU.subtract).then_inc(r_dve, 1)
                dve.wait_ge(r_dve, c.next())
                tt(blk_k[:, :], blk_k[:, :], ge_k[:, :], ALU.mult).then_inc(r_dve, 1)
                dve.wait_ge(r_dve, c.next())
                tt(blk_k[:, :], blk_k[:, :], ef, ALU.add).then_inc(r_dve, 1)
                dve.wait_ge(r_dve, c.next())
                stt(rank_k[:, :], blk_k[:, :], float(P), row_k[:, :], ALU.mult, ALU.add).then_inc(r_dve, 1)
                dve.wait_ge(r_dve, c.next())
                dve.tensor_copy(dest_u[:, :], rank_k[:, :]).then_inc(r_dve, 1)
                dve.wait_ge(r_dve, c.next())
                c.close()
                for n in range(TOPK * NT):
                    t = n % NT
                    dve.wait_ge(r_idx, layer * 16 + n + 1)
                    ts(oh_row[n % 2][:, :], iota_r, row_k[:, n:n + 1], None, ALU.is_equal)
                    ts(oh_blk[n % 2][:, :], blk_iota, blk_k[:, n:n + 1], tok_id[:, t:t + 1], ALU.is_equal, ALU.mult)\
                        .then_inc(r_oh, 1)
                c = Count(5, layer)
                dve.wait_ge(r_exp, layer + 1)
                ts(gates[:, 0:NT], exp_g[:, :], 1.0, None, ALU.add).then_inc(r_gates, 1)
                dve.wait_ge(r_gates, c.next())
                tt(gates[:, 0:NT], gates[:, 0:NT], sum_all[:, :], ALU.mult).then_inc(r_gates, 1)
                dve.wait_ge(r_gates, c.next())
                dve.reciprocal(gates[:, 0:NT], gates[:, 0:NT]).then_inc(r_gates, 1)
                dve.wait_ge(r_gates, c.next())
                tt(gates[:, NT:2 * NT], gates[:, 0:NT], exp_g[:, :], ALU.mult).then_inc(r_gates, 1)
                dve.wait_ge(r_gates, c.next())
                dve.wait_ge(r_idx, layer * 16 + 18)
                dve.tensor_copy(slot_tok[:, :], bank(4)[:, 0:NBLK + 1]).then_inc(r_gates, 1)
                dve.wait_ge(r_gates, c.next())
                c.close()
                dve.tensor_copy(next_gb[:, ds(layer + 1, 1)], gb_f[:, :]).then_inc(r_plan, 1)
                next_phase(dve, DVE_E, layer, PH_C)

                steady(dve)
                nb2 = dve.value_load(plan[0:1, 0:1], min_val=NE - 2, max_val=NBLK - 2)
                nb = nb2 + 2
                gb = dve.value_load(plan[0:1, 1:2], min_val=0, max_val=DEPTH * NBLK)

                def lo(s, turns):
                    dve.wait_ge(d_hi, gb * 6 + turns * 6 + s + 1)
                    tt(ring_lo[:, s % 3, :], ring_raw[:, s % 6, :], ring_hi[:, s % 3, :], ALU.subtract)\
                        .then_inc(d_lo, 1)

                def x_lo(b):
                    for i, (hi_s, lo_s) in enumerate(((d_xhi0, d_xlo0), (d_xhi1, d_xlo1))):
                        dve.wait_ge(hi_s, gb + b + 1)
                        tt(xg_lo[:, 4 * i:4 * i + 4, :], grouped(bank(i), 4), xg_hi[:, 4 * i:4 * i + 4, :], ALU.subtract)\
                            .then_inc(lo_s, 1)

                def g_mul(b, chunks):
                    dve.wait_ge(d_silu, gb + b + 2)
                    dve.wait_ge(d_mm, gb * 6 + chunks + 3)
                    dve.wait_ge(d_tg, gb + b + 1)
                    tt(gate_sb[:, :], bank(4), silu_sb[:, :], ALU.mult).then_inc(d_gm, 1)

                def g_lo(b):
                    dve.wait_ge(d_ghi, gb + b + 1)
                    tt(gT_lo[:, :, :], grouped(bank(2), 4), gT_hi[:, :, :], ALU.subtract).then_inc(d_glo, 1)

                x_lo(0)
                for s in range(4):
                    lo(s, 0)
                g_mul(0, 4)
                x_lo(1)
                for s in (4, 5):
                    lo(s, 0)
                g_lo(0)
                for s in (6, 7, 8, 9):
                    lo(s, 0)

                def turn(b):
                    g_mul(b - 1, (b - 2) * 6 + 8)
                    x_lo(b)
                    lo(10, b - 2)
                    lo(11, b - 2)
                    g_lo(b - 1)
                    for s in (12, 13, 14, 15):
                        lo(s, b - 2)

                steady(dve)
                with dve.Fori(2, NE) as b:
                    turn(b)
                steady(dve)
                with dve.Fori(NE, NBLK) as b:
                    with dve.If(b < nb):
                        turn(b)
                g_mul(nb2 + 1, (nb2) * 6 + 8)
                g_lo(nb2 + 1)
                for s in (10, 11):
                    lo(s, nb2)
                next_phase(dve, DVE_E, layer, PH_D)

                dve.wait_ge(e_par_in, 32 * (layer + 1))

                def front(t, j, pair):
                    dve.wait_ge(e_yg[j], (layer * (NT // 2) + pair + 1) * 32)
                    stt(h_t(t), yg[j][0][:, :], gates[:, ds(t, 1)], h_t(t), ALU.mult, ALU.add).then_inc(e_dve, 1)
                    dve.wait_ge(e_dve, it(t) + 1)
                    stt(h_t(t), yg[j][1][:, :], gates[:, ds(t + NT, 1)], h_t(t), ALU.mult, ALU.add)\
                        .then_inc(e_comb, 1)
                    dve.wait_ge(f_rstd, ft(2, t) + 1)
                    stt(xn[j][:, :], h_t(t), rstd_x[:, j:j + 1], g_ple_sb[:, :], ALU.mult, ALU.mult)\
                        .then_inc(f_xn, 1)
                    dve.wait_ge(f_tp1, ft(2, t) + 1)
                    dve.tensor_copy(xT[j][:, 4:8, :], grouped(bank(1), 4)).then_inc(f_ev1, 1)

                def gate(t):
                    for i, (g, b_) in enumerate(((e_g0, e_b0), (e_g1, e_b1))):
                        dve.wait_ge(g, it(t) + 1)
                        tt(gs[:, i * 512:(i + 1) * 512], bank(2 + i), b_gate_sb[:, i * 512:(i + 1) * 512], ALU.add)\
                            .then_inc(b_, 1)

                def finish(t):
                    dve.wait_ge(e_sg, it(t) + 1)
                    dve.wait_ge(e_pl, it(t) + 1)
                    tt(gs[:, :], bank(4, 2), gs[:, :], ALU.mult).then_inc(e_fin, 1)
                    dve.wait_ge(e_fin, it(t) + 1)
                    tt(h_t(t), h_t(t), gs[:, :], ALU.add).then_inc(e_h, 1)
                    dve.wait_ge(e_h, it(t) + 2)

                def turn(t, j, first, last, pair=None):
                    if first:
                        front(0, 0, 0)
                    if not last:
                        front(t + 1, 1 - j, pair)
                    gate(t)
                    finish(t)

                turn(0, 0, True, False, 0)
                steady(dve)
                with dve.Fori(0, NT // 2 - 1) as i:
                    turn(i * 2 + 1, 1, False, False, i + 1)
                    turn(i * 2 + 2, 0, False, False, i + 1)
                turn(NT - 1, 1, False, True)
                next_phase(dve, DVE_E, layer, PH_E)

        @block.tensor
        def _(pe):
            credit(pe, 1, a_tc, a_s, c_f1, d_tx, d_tg)
            credit(pe, 2, r_idx, e_tpp)
            credit(pe, 3, d_mm)
            credit(pe, 12, b_pt)
            pe.wait_ge(consts_in, 16)
            mm = pe.matmul

            def transposes(dst, src, n0, n, raises, rows=P):
                for i in range(n):
                    last = pe.transpose(dst[:, i * P:(i + 1) * P], src[:, (n0 + i) * P:(n0 + i + 1) * P], ident)
                last.then_inc(raises, 1)

            def product(dst, lhs, rhs, kn, raises=None):
                for k in range(kn):
                    last = mm(dst, lhs(k), rhs(k), start=(k == 0), stop=(k == kn - 1))
                if raises:
                    last.then_inc(raises, 1)

            with pe.Fori(0, DEPTH) as layer:
                it = lambda t: layer * NT + t
                ft = lambda phase, t: (layer * 3 + phase) * NT + t
                pe.wait_ge(ab_in, 16 * AB_LOADS * (layer + 1))
                for i in range(2):
                    for g in range(4 * i, 4 * i + 4):
                        src = ws_nat[g // 6][:, g % 6 * P:(g % 6 + 1) * P]
                        last = pe.transpose(bank(i)[:, (g - 4 * i) * P:(g - 4 * i + 1) * P], src, ident)
                    last.then_inc(ws_t, 1)
                next_phase(pe, PE_E, layer, PH_WS)

                def front(t, j):
                    pe.wait_ge(f_xn, ft(0, t) + 2)
                    pe.wait_ge(f_ev0, ft(0, t) + 1)
                    transposes(bank(0), xn[j], 0, 4, f_tp0)
                    pe.wait_ge(f_ev1, ft(0, t) + 1)
                    transposes(bank(1), xn[j], 4, 4, f_tp1)

                def turn(t, j, first, last):
                    if first:
                        front(0, 0)
                        pe.wait_ge(w_in_in, 16 * (layer + 1))
                    pe.wait_ge(f_ev0, ft(0, t) + 2)
                    pe.wait_ge(f_ev1, ft(0, t) + 2)
                    pe.wait_ge(a_gv, it(t) + 1)
                    lhs = lambda k: xT[j][:, k, :]
                    product(bank(4), lhs, lambda k: w_in_sb[:, k, V0:IN_W], KD, a_mv)
                    if not last:
                        front(t + 1, 1 - j)
                    pe.wait_ge(a_cn, it(t) + 1)
                    product(bank(2)[:, 0:W_C], lhs, lambda k: w_in_sb[:, k, 0:W_C], KD, a_mc)
                    pe.wait_ge(a_gu, it(t) + 1)
                    product(bank(3), lhs, lambda k: w_in_sb[:, k, U0:V0], KD, a_mu)
                    pe.wait_ge(a_cn, it(t) + 2)
                    pe.wait_ge(a_ce, it(t) + 1)
                    transposes(bank(5), cn, 0, 3, a_tc)
                    pe.wait_ge(a_vn, it(t) + 1)
                    pe.wait_ge(a_m, it(t) + 1)
                    for g in range(GROUPS):
                        last_mm = mm(bank(6)[:, g * GDIM:(g + 1) * GDIM], wsT[:, g, :], vn[:, g * GDIM:(g + 1) * GDIM],
                                     start=True, stop=True)
                    last_mm.then_inc(a_s, 1)

                over_tiles(pe, turn)
                next_phase(pe, PE_E, layer, PH_A)

                def front(step, hd, j):
                    if step < 4:
                        lo_t = 4 * (step % 2)
                        prev = (b_tev[1], b_pev[0], b_pev[1], b_pev[2])[step]
                        pe.wait_ge(prev, it(hd) + (1 if step else 0) + 1)
                        if step == 0:
                            pe.wait_ge(b_tev[0], it(hd) + 1)
                        for i in range(4):
                            cols = slice((lo_t + i) * P, (lo_t + i + 1) * P)
                            if step < 2:
                                for k in range(2):
                                    last = mm(bank(0)[:, i * QK:(i + 1) * QK], cT[:, k, cols],
                                              w_uq_sb[:, k, ds(hd * QK, QK)], start=(k == 0), stop=(k == 1))
                            else:
                                last = mm(bank(0)[:, i * P:(i + 1) * P], cT[:, 2, cols],
                                          w_ukv_sb[:, ds(hd * P, P)], start=True, stop=True)
                        last.then_inc(b_proj[step], 1)
                    elif step >= 6:
                        for n in {6: (0,), 7: (1,), 8: (2, 3)}[step]:
                            if n == 0:
                                pe.wait_ge(b_qk, it(hd) + 1)
                            if n == 1:
                                pe.wait_ge(b_tev[0], it(hd) + 2)
                            b = (0, 0, 2, 3)[n]
                            for i in range(4):
                                last = pe.transpose(bank(b)[0:QK, i * P:(i + 1) * P],
                                                    qkb[:, n // 2, 4 * (n % 2) + i, :], ident)
                            last.then_inc(b_t[n], 1)

                def scores(hd, j, i):
                    pe.wait_ge(b_exp, it(hd) * 8 + i + 1)
                    w = (i + 1) * P
                    for c0_ in range(0, w, BANK):
                        n = min(BANK, w - c0_)
                        last = mm(bank(2 + 2 * (i % 2), 2)[:, c0_:c0_ + n], qkT[j][:, 0, i * P:(i + 1) * P],
                                  qkT[j][:, 1, c0_:c0_ + n], start=True, stop=True)
                    last.then_inc(b_s, 1)

                def turn(hd, j, first, last):
                    if first:
                        for step in range(9):
                            front(step, 0, 0)
                    for n in range(4):
                        pe.wait_ge(b_tev[n], it(hd) + 2)
                    scores(hd, j, 0)
                    g = 0
                    ev = [0, 0]
                    for i in range(NT):
                        if i + 1 < NT:
                            scores(hd, j, i + 1)
                        pe.wait_ge(b_exp, it(hd) * 8 + i + 3)
                        for gi in range(1 + (i >= 4)):
                            pe.wait_ge((b_pte_a, b_pte_d)[g % 2], it(hd) * 6 + ev[g % 2] + 1)
                            ev[g % 2] += 1
                            n = min(4, i + 1 - 4 * gi)
                            transposes(bank(1 if g % 2 == 0 else 6), prob[i % 2], 4 * gi, n, b_pt)
                            g += 1
                        if not last:
                            front(i, hd + 1, 1 - j)
                        for s, sg in enumerate((b_pte_a, b_pte_d)):
                            pe.wait_ge(sg, it(hd) * 6 + ev[s] + 1)
                        if i == 0:
                            pe.wait_ge(b_o, it(hd) + 1)
                        for k in range(i + 1):
                            last_mm = mm(bank(7)[:, i * VDIM:(i + 1) * VDIM], probT[:, k, :], v_sb[j][:, k, :],
                                         start=(k == 0), stop=(k == i))
                    last_mm.then_inc(b_pv, 1)
                    if not last:
                        pe.wait_ge(b_exp, it(hd) * 8 + 10)
                        front(8, hd + 1, 1 - j)

                over_tiles(pe, turn)
                next_phase(pe, PE_E, layer, PH_B)

                def front(t, j):
                    pe.wait_ge(f_xn, ft(1, t) + 2)
                    pe.wait_ge(f_ev0, ft(1, t) + 1)
                    transposes(bank(0), xn[j], 0, 4, f_tp0)
                    pe.wait_ge(f_ev1, ft(1, t) + 1)
                    transposes(bank(1), xn[j], 4, 4, f_tp1)

                def tail_t(t):
                    pe.wait_ge(c_xf, it(t) + 1)
                    pe.wait_ge(c_fe0, it(t) + 1)
                    transposes(bank(4), xf, 0, 4, c_f0)
                    pe.wait_ge(c_fe1, it(t) + 1)
                    transposes(bank(5), xf, 4, 4, c_f1)

                def router(t):
                    pe.wait_ge(c_fe0, it(t) + 2)
                    pe.wait_ge(c_fe1, it(t) + 2)
                    pe.wait_ge(c_lge, it(t) + 1)
                    product(bank(6)[:, 0:NROUTE], lambda k: xfT[:, k, :], lambda k: w_router[:, k, :], KD, c_rt)

                def turn(t, j, first, last):
                    if first:
                        pe.wait_ge(wout_in, 16 * (layer + 1))
                        front(0, 0)
                    lhs = lambda k: xT[j][:, k, :]
                    pe.wait_ge(f_ev0, ft(1, t) + 2)
                    pe.wait_ge(f_ev1, ft(1, t) + 2)
                    pe.wait_ge(c_h0, it(t) + 1)
                    product(bank(2), lhs, lambda k: w_out_sb[:, k, 0:512], KD, c_y0)
                    if not first:
                        tail_t(t - 1)
                    if not last:
                        front(t + 1, 1 - j)
                    pe.wait_ge(c_h1, it(t) + 1)
                    product(bank(3), lhs, lambda k: w_out_sb[:, k, 512:1024], KD, c_y1)
                    if not first:
                        router(t - 1)
                    if last:
                        tail_t(t)
                        router(t)

                over_tiles(pe, turn)
                pe.wait_ge(r_gap, layer + 1)
                for t in range(NT):
                    dst = bank(0)[:, t * NE:(t + 1) * NE]
                    mm(dst, before, chosen[:, t, :], start=True, stop=False)
                    mm(dst, ones, picks[:, t, :], start=False, stop=True)
                mm(bank(1)[:, 0:NE], ones, picks[:, NT, :], start=True, stop=True).then_inc(r_rank, 1)
                pe.wait_ge(r_ovt, layer + 1)
                pe.transpose(bank(2)[0:NE, 0:P], over_e[:, :], ident).then_inc(r_ovsb, 1)
                pe.wait_ge(r_ovs, layer + 1)
                mm(bank(3)[:, 0:NE], overT[:, :], before[0:NE, 0:NE], start=True, stop=True).then_inc(r_ovsb, 1)
                for n in range(TOPK * NT):
                    pe.wait_ge(r_oh, layer * 16 + n + 1)
                    mm(bank(4)[:, 0:NBLK + 1], oh_row[n % 2][:, :], oh_blk[n % 2][:, :],
                       start=(n == 0), stop=(n == TOPK * NT - 1)).then_inc(r_idx, 1)
                next_phase(pe, PE_E, layer, PH_C)

                steady(pe)
                nb2 = pe.value_load(plan[0:1, 0:1], min_val=NE - 2, max_val=NBLK - 2)
                nb = nb2 + 2
                gb = pe.value_load(plan[0:1, 1:2], min_val=0, max_val=DEPTH * NBLK)

                def x_t(b):
                    pe.wait_ge(d_xg, (gb + b + 1) * 16)
                    pe.wait_ge(d_xlo0, gb + b + 1)
                    pe.wait_ge(d_xlo1, gb + b + 1)
                    for i in range(KD):
                        last = pe.transpose(ps[:, i * P:(i + 1) * P], xg[:, i * P:(i + 1) * P], ident)
                    last.then_inc(d_tx, 1)

                def split_mm(dst, x_hi, x_lo, w_hi, w_lo, start, stop):
                    mm(dst, x_hi, w_hi, start=start, stop=False)
                    mm(dst, x_hi, w_lo, start=False, stop=False)
                    return mm(dst, x_lo, w_hi, start=False, stop=stop)

                def up(s, turns, dst):
                    pe.wait_ge(d_lo, gb * 6 + turns * 6 + s + 7)
                    part = s % 2
                    for k in range(4):
                        w = slice(k * FE, (k + 1) * FE)
                        last = split_mm(dst, xg_hi[:, 4 * part + k, :], xg_lo[:, 4 * part + k, :],
                                        ring_hi[:, s % 3, w], ring_lo[:, s % 3, w], part == 0 and k == 0,
                                        part == 1 and k == 3)
                    last.then_inc(d_mm, 1)

                def ups(b, s, turns):
                    pe.wait_ge(d_xlo0, gb + b + 2)
                    pe.wait_ge(d_xlo1, gb + b + 2)
                    pe.wait_ge(d_silu, gb + b + 1)
                    up(s, turns, bank(3))
                    up(s + 1, turns, bank(3))
                    pe.wait_ge(d_gm, gb + b + 1)
                    up(s + 2, turns, bank(4))
                    up(s + 3, turns, bank(4))

                def down(b, s, turns):
                    pe.wait_ge(d_glo, gb + b + 2)
                    pe.wait_ge(d_yev, gb + b + 1)
                    for part in range(2):
                        pe.wait_ge(d_lo, gb * 6 + turns * 6 + s + part + 7)
                        for k in range(2):
                            for i in range(2):
                                w = slice(k * D + i * 512, k * D + (i + 1) * 512)
                                last = split_mm(bank(5 + i), gT_hi[:, 2 * part + k, :], gT_lo[:, 2 * part + k, :],
                                                ring_hi[:, (s + part) % 3, w], ring_lo[:, (s + part) % 3, w],
                                                part == 0 and k == 0, part == 1 and k == 1)
                        last.then_inc(d_mm, 1)

                def g_t(b):
                    pe.wait_ge(d_gm, gb + b + 2)
                    pe.wait_ge(d_glo, gb + b + 1)
                    transposes(bank(2), gate_sb, 0, 4, d_tg)

                x_t(0)
                ups(0, 0, 0)
                x_t(1)
                g_t(0)
                ups(1, 4, 0)

                def turn(b):
                    x_t(b)
                    down(b - 2, 8, b - 2)
                    g_t(b - 1)
                    ups(b, 10, b - 2)

                steady(pe)
                with pe.Fori(2, NE) as b:
                    turn(b)
                steady(pe)
                with pe.Fori(NE, NBLK) as b:
                    with pe.If(b < nb):
                        turn(b)
                down(nb2, 8, nb2)
                g_t(nb2 + 1)
                down(nb2 + 1, 10, nb2)
                next_phase(pe, PE_E, layer, PH_D)

                def front(t, j, pair):
                    pe.wait_ge(f_xn, ft(2, t) + 2)
                    pe.wait_ge(f_ev0, ft(2, t) + 1)
                    transposes(bank(0), xn[j], 0, 4, f_tp0)
                    pe.wait_ge(f_ev1, ft(2, t) + 1)
                    transposes(bank(1), xn[j], 4, 4, f_tp1)
                    pe.wait_ge(p_in[j], (layer * (NT // 2) + pair + 1) * 16)
                    pe.wait_ge(e_evp, it(t) + 1)
                    transposes(bank(6), p_sb[j], 0, 2, e_tpp)

                def turn(t, j, first, last, pair=None):
                    if first:
                        pe.wait_ge(ple_w_in, 32 * (layer + 1))
                        front(0, 0, 0)
                    lhs = lambda k: xT[j][:, k, :]
                    pe.wait_ge(f_ev0, ft(2, t) + 2)
                    pe.wait_ge(f_ev1, ft(2, t) + 2)
                    pe.wait_ge(e_evp, it(t) + 2)
                    pe.wait_ge(e_b0, it(t) + 1)
                    product(bank(2), lhs, lambda k: w_gate_sb[:, k, 0:512], KD, e_g0)
                    pe.wait_ge(e_b1, it(t) + 1)
                    product(bank(3), lhs, lambda k: w_gate_sb[:, k, 512:1024], KD, e_g1)
                    if not last:
                        front(t + 1, 1 - j, pair)
                    pe.wait_ge(e_h, it(t) + 1)
                    for i in range(2):
                        product(bank(4 + i), lambda k: pT[j][:, k, :], lambda k: w_ple_sb[:, k, i * 512:(i + 1) * 512], 2,
                                e_pl if i == 1 else None)

                turn(0, 0, True, False, 0)
                steady(pe)
                with pe.Fori(0, NT // 2 - 1) as i:
                    turn(i * 2 + 1, 1, False, False, i + 1)
                    turn(i * 2 + 2, 0, False, False, i + 1)
                turn(NT - 1, 1, False, True)
                next_phase(pe, PE_E, layer, PH_E)


_INS = ["x", "p", "g_mix_norm", "w_in", "g_cq", "g_ckv", "w_uq", "w_ukv", "g_qn", "g_kn", "g_v", "w_s", "b_s",
        "g_out_mla", "g_out_gmlp", "w_out", "g_ffn_norm", "w_router_group", "w_router_expert",
        "w1", "w3", "w2", "g_ple", "w_ple_gate", "b_ple_gate", "w_ple"]


def shape_constants(seq):
    import numpy as np

    f = np.float32
    part = np.arange(P, dtype=f)
    inv = (f(10000.0) ** (-np.arange(0, ROPE, 2, dtype=f) / f(ROPE))).astype(f)
    ang = (np.arange(seq, dtype=f)[:, None] * inv[None, :]).astype(f)
    tiled = lambda a: np.concatenate([a, a], axis=1).reshape(seq // P, P, ROPE).transpose(1, 0, 2).reshape(P, -1)
    row = lambda a: np.broadcast_to(np.asarray(a, f), (P, len(a)))
    return np.ascontiguousarray(np.concatenate([
        np.eye(P, dtype=f),
        (part[:, None] < part[None, :]).astype(f),
        np.ones((P, P), f),
        tiled(np.cos(ang)), tiled(np.sin(ang)),
        row(part),
        row(P * np.arange(NE)),
        row(P * np.arange(1, 9)),
        np.stack([P * t + part for t in range(8)], axis=1),
        row(np.arange(16)),
    ], axis=1).astype(f))


def kernel(**inputs):
    import numpy as _np
    import concourse.bacc as _bacc
    from concourse import mybir as _mybir
    from concourse.bass_utils import run_bass_kernel_spmd as _run

    nc = _bacc.Bacc("TRN2", target_bir_lowering=False, num_devices=1)
    arrays, args = {}, []
    for name in _INS:
        a = _np.ascontiguousarray(inputs[name])
        arrays[f"in_{name}"] = a
        args.append(nc.dram_tensor(f"in_{name}", a.shape, _mybir.dt.from_np(a.dtype), kind="ExternalInput").ap())
    shape = inputs["x"].shape
    a = shape_constants(shape[1])
    arrays["shape_consts"] = a
    args.append(nc.dram_tensor("shape_consts", a.shape, _mybir.dt.float32, kind="ExternalInput").ap())
    args.append(nc.dram_tensor("out_0", shape, _mybir.dt.float32, kind="ExternalOutput").ap())
    hybrid_trunk(nc, *args)
    r = _run(nc, [arrays], core_ids=[0])
    return r.results[0]["out_0"]
```

```python
from contextlib import ExitStack

import concourse.bass as bass
from concourse import mybir

P = 128
BANK = 512
F32 = mybir.dt.float32
F32R = mybir.dt.float32r
I32 = mybir.dt.int32
U32 = mybir.dt.uint32
ALU = mybir.AluOpType
ACT = mybir.ActivationFunctionType
AX_X = mybir.AxisListType.X
ds = bass.ds

EPS = 1e-6
NEG = -3.0e38
HEADS, NOPE, ROPE, VDIM = 8, 64, 32, 64
QK = NOPE + ROPE
Q_RANK, KV_RANK = 256, 128
GROUPS, GDIM = 8, 64
CHUNK = 64
NG, PER_G, NE, TOPK = 4, 8, 32, 2
FE = 512
PLE = 256
CONSTS = 4 * P + 8 * ROPE * 2 + 32 + 8 + 8 + 16


class Count:

    def __init__(self, per, turn):
        self.per, self.base, self.n = per, turn * per, 0

    def next(self):
        self.n += 1
        return self.base + self.n

    def close(self):
        assert self.n == self.per, (self.n, self.per)


def hybrid_trunk(nc, x, p, g_mix_norm, w_in, g_cq, g_ckv, w_uq, w_ukv, g_qn, g_kn, g_v, w_s, b_s,
                 g_out_mla, g_out_gmlp, w_out, g_ffn_norm, w_router_group, w_router_expert,
                 w1, w3, w2, g_ple, w_ple_gate, b_ple_gate, w_ple, shape_consts, out):
    DEPTH, D, IN_W = w_in.shape
    SEQ = x.shape[1]
    NT = SEQ // P
    KD = D // P
    KF = FE // P
    MIXW = HEADS * VDIM
    CQKV = Q_RANK + KV_RANK
    W_C = CQKV + ROPE
    U0, V0 = W_C, W_C + GROUPS * GDIM
    MAX_OVER = (TOPK * SEQ - 1) // P
    NBLK = NE + MAX_OVER
    NROUTE = NG + NE
    SCALE = float(QK) ** -0.5
    GROUP_OF = [0]
    GROUP_N = []
    for i in range(NT):
        GROUP_N += [min(4, i + 1 - g) for g in range(0, i + 1, 4)]
        GROUP_OF.append(len(GROUP_N))
    N_PT, PT_BACK = len(GROUP_N), 3
    PHASES = 6
    AB_LOADS = 11
    PH_WS, PH_A, PH_B, PH_C, PH_D, PH_E = range(PHASES)

    with ExitStack() as ctx:
        sem = lambda name: ctx.enter_context(nc.semaphore(name))

        arena = ctx.enter_context(nc.sbuf_tensor("arena", [P, 212832 // 4], F32))
        ARENA0 = 16512

        def at(name, shape, dt, offset):
            size = 4
            for n in shape[1:]:
                size *= n
            assert offset + size <= 212832, (name, offset, size)
            return nc.alloc_sbuf_tensor_at(name, shape, dt, offset=ARENA0 + offset)

        K = 1024
        h = at("h", [P, NT * D], F32, 0)
        RAW = NT * D * 4
        ring_raw = at("ring_raw", [P, 6, 2048], F32, RAW)
        w_in_sb = at("w_in_sb", [P, KD, IN_W], F32, RAW)
        w_out_sb = at("w_out_sb", [P, KD, D], F32, RAW)
        g_out_sb = at("g_out_sb", [P, D], F32, RAW + 32 * K)
        g_ffn_sb = at("g_ffn_sb", [P, D], F32, RAW + 36 * K)
        w_router = at("w_router", [P, KD, NROUTE], F32, RAW + 40 * K)
        R = RAW + 48 * K
        ring_hi = at("ring_hi", [P, 3, 2048], F32R, R)
        ring_lo = at("ring_lo", [P, 3, 2048], F32R, R + 24 * K)
        xg = at("xg", [P, D], F32, R + 48 * K)
        xg_hi = at("xg_hi", [P, KD, P], F32R, R + 52 * K)
        xg_lo = at("xg_lo", [P, KD, P], F32R, R + 56 * K)
        silu_sb = at("silu_sb", [P, FE], F32, R + 60 * K)
        gate_sb = at("gate_sb", [P, FE], F32, R + 62 * K)
        gT_hi = at("gT_hi", [P, KF, P], F32R, R + 64 * K)
        gT_lo = at("gT_lo", [P, KF, P], F32R, R + 66 * K)
        y_sb = at("y_sb", [P, D], F32, R + 68 * K)
        w_gate_sb = at("w_gate_sb", [P, KD, D], F32, R + 76 * K)
        w_ple_sb = at("w_ple_sb", [P, 2, D], F32, R + 108 * K)
        xT = [at(f"xT{j}", [P, KD, P], F32, R + 4 * K * j) for j in range(2)]
        xn = [at(f"xn{j}", [P, D], F32, R + (8 + 4 * j) * K) for j in range(2)]
        junk = at("junk", [P, D], F32, R + 16 * K)
        gv_sb = at("gv_sb", [P, 512], F32, R + 20 * K)
        gu_sb = at("gu_sb", [P, 512], F32, R + 22 * K)
        vsq = at("vsq", [P, 512], F32, R + 24 * K)
        vn = at("vn", [P, 512], F32, R + 26 * K)
        vn1 = at("vn1", [P, 512], F32, R + 28 * K)
        s_sb = at("s_sb", [P, 512], F32, R + 30 * K)
        cn = at("cn", [P, CQKV], F32, R + 32 * K)
        junk_c = at("junk_c", [P, CQKV], F32, R + 34 * K)
        ws_nat = [at("ws_nat0", [P, 6 * P], F32, RAW + 45 * K), at("ws_nat1", [P, 2 * P], F32, R + 116 * K)]
        g_mix_sb = at("g_mix_sb", [P, D], F32, R + 48 * K)
        g_c_sb = at("g_c_sb", [P, CQKV], F32, R + 52 * K)
        g_v_sb = at("g_v_sb", [P, 512], F32, R + 54 * K)
        g_qk_sb = at("g_qk_sb", [P, 2, QK], F32, R + 56 * K)
        bs_sb = at("bs_sb", [P, GROUPS], F32, R + 57 * K)
        w_uq_sb = at("w_uq_sb", [P, 2, HEADS * QK], F32, R + 58 * K)
        w_ukv_sb = at("w_ukv_sb", [P, HEADS * P], F32, R + 64 * K)
        wsT = at("wsT", [P, GROUPS, P], F32, R + 68 * K)
        kr_all = at("kr_all", [P, NT, ROPE], F32, R + 72 * K)
        cT = at("cT", [P, 3, SEQ], F32, R + 73 * K)
        m_all = at("m_all", [P, NT * 512], F32, R + 85 * K)
        a_all = at("a_all", [P, NT, MIXW], F32, R + 101 * K)
        qkb = at("qkb", [P, 2, NT, QK], F32, R)
        qksq = at("qksq", [P, 2, NT, QK], F32, R + 6 * K)
        rope_c, rope_s, kr_c, kr_rot = (at(n, [P, NT, ROPE], F32, R + (12 + i) * K)
                                        for i, n in enumerate(("rope_c", "rope_s", "kr_c", "kr_rot")))
        kr_s = at("kr_s", [P, NT, ROPE], F32, R + 46 * K)
        qkT = [at(f"qkT{j}", [QK, 2, SEQ], F32, R + (16 + 8 * j) * K) for j in range(2)]
        v_sb = [at(f"v_sb{j}", [P, NT, VDIM], F32, R + (32 + 2 * j) * K) for j in range(2)]
        prob = [at(f"prob{j}", [P, SEQ], F32, R + (36 + 4 * j) * K) for j in range(2)]
        probT = [at(f"probT{j}", [P, 4, P], F32, R + (44 + 2 * j) * K) for j in range(2)]
        xf = at("xf", [P, D], F32, R + 20 * K)
        xfT = at("xfT", [P, KD, P], F32, R + 24 * K)
        yg = [[at(f"yg{j}{k}", [P, D], F32, R + (20 + 8 * j + 4 * k) * K) for k in range(2)] for j in range(2)]
        g_ple_sb = at("g_ple_sb", [P, D], F32, R + 36 * K)
        b_gate_sb = at("b_gate_sb", [P, D], F32, R + 40 * K)
        gs = at("gs", [P, D], F32, R + 44 * K)
        p_sb = [at(f"p_sb{j}", [P, PLE], F32, R + (72 + j) * K) for j in range(2)]
        pT = [at(f"pT{j}", [P, 2, P], F32, R + (74 + j) * K) for j in range(2)]

        S0 = R + 117 * K
        off = [S0]

        def small(name, shape, dt=F32):
            n = 4
            for d in shape[1:]:
                n *= d
            off[0] += -off[0] % 32
            o = off[0]
            off[0] += n
            return at(name, shape, dt, o)

        consts = small("consts", [P, CONSTS])
        c0 = [0]

        def const(n):
            a = c0[0]
            c0[0] += n
            return consts[:, a:a + n]

        ident = const(P)
        before = const(P)
        ones = const(P)
        cos2 = const(8 * ROPE).rearrange("p (t r) -> p t r", t=8)
        sin2 = const(8 * ROPE).rearrange("p (t r) -> p t r", t=8)
        iota_r = const(P)
        iota_e = iota_r[:, 0:NE]
        block_e = const(NE)
        steps = const(8)
        tok_id = const(8)
        over_id = const(16)
        assert c0[0] == CONSTS

        half = small("half", [P, 16])
        stat_x = small("stat_x", [P, 2])
        rstd_x = small("rstd_x", [P, 2])
        stat_c = small("stat_c", [P, 2])
        rstd_c = small("rstd_c", [P, 2])
        stat_v = small("stat_v", [P, GROUPS])
        rstd_v = small("rstd_v", [P, GROUPS])
        tmp_p = small("tmp_p", [P, 16])
        stat_qk = small("stat_qk", [P, 16])
        rstd_qk = small("rstd_qk", [P, 16])
        row_max = small("row_max", [P, 2])
        neg_max = small("neg_max", [P, 2])
        row_sum = small("row_sum", [P, 2 * NT])
        ss_kr = small("ss_kr", [P, NT])
        row_inv = small("row_inv", [P, NT])
        stat_f = small("stat_f", [P, 1])
        rstd_f = small("rstd_f", [P, 1])
        lg8 = small("lg8", [P, 8])
        le = small("le", [P, NE])
        top8 = small("top8", [P, 8])
        gi8 = small("gi8", [P, 8], U32)
        gf = small("gf", [P, 1])
        lgm = small("lgm", [P, NG])
        lge = small("lge", [P, NG])
        gmask = small("gmask", [P, NG])
        gbias = small("gbias", [P, NG])
        top8e = small("top8e", [P, 8])
        ei8 = small("ei8", [P, 8], U32)
        sum_all = small("sum_all", [P, NT])
        gap_all = small("gap_all", [P, NT])
        ef_all = small("ef_all", [P, TOPK, NT])
        picks = small("picks", [P, NT + 1, NE])
        rank_k = small("rank_k", [P, TOPK * NT])
        ovs_k = small("ovs_k", [P, TOPK * NT])
        q_k = small("q_k", [P, TOPK * NT])
        ge_k = small("ge_k", [P, TOPK * NT])
        blk_k = small("blk_k", [P, TOPK * NT])
        row_k = small("row_k", [P, TOPK * NT])
        dest_u = small("dest_u", [P, TOPK * NT], U32)
        over_e = small("over_e", [P, NE])
        over_s = small("over_s", [P, NE])
        over_end = small("over_end", [P, NE])
        nb_f = small("nb_f", [P, 1])
        nb2_f = small("nb2_f", [P, 1])
        gb_f = small("gb_f", [P, 1])
        plan = small("plan", [P, 2], I32)
        next_gb = small("next_gb", [P, DEPTH + 1], I32)
        expert_i = small("expert_i", [P, NE + 16], I32)
        ex_f = small("ex_f", [P, 16])
        gates = small("gates", [P, TOPK * NT])
        exp_g = small("exp_g", [P, NT])
        slot_tok = small("slot_tok", [P, NBLK + 1], U32)
        idx_x = small("idx_x", [P, 1], U32)
        idx_y = [[small(f"idx_y{j}{k}", [P, 1], U32) for k in range(2)] for j in range(2)]
        cmp_s = at("cmp_s", [P, NE * 16], F32, R + 52 * K)
        oh_row = [at(f"oh_row{j}", [P, P], F32, R + 60 * K + 512 * j) for j in range(2)]
        oh_blk = [at(f"oh_blk{j}", [P, NBLK + 1], F32, R + 62 * K + 256 * j) for j in range(2)]
        onehot = at("onehot", [P, TOPK, NT, NE], F32, R + 56 * K)
        chosen = at("chosen", [P, NT, NE], F32, R + 58 * K)
        overT = at("overT", [NE, P], F32, R + 70 * K)
        sel = at("sel", [P, NT, NE], F32, R + 68 * K)
        rank_sb = at("rank_sb", [P, NT, NE], F32, R + 64 * K)
        blk_iota = iota_r[:, 0:NBLK + 1]

        ps = ctx.enter_context(nc.psum_tensor("ps", [P, 8 * BANK], F32))

        def bank(b, n=1):
            return ps[:, b * BANK:(b + n) * BANK]

        xn_rows = nc.dram_tensor("xn_rows", (SEQ, D), F32, kind="Internal").ap()
        y_rows = nc.dram_tensor("y_rows", (NBLK * P, D), F32, kind="Internal").ap()
        x_v = x.rearrange("b (t p) d -> p (b t) d", p=P)
        out_v = out.rearrange("b (t p) d -> p (b t) d", p=P)
        p_v = p.rearrange("l b (t p) d -> (l b t) p d", p=P)
        w_in_v = w_in.rearrange("l (k p) n -> l p k n", p=P)
        w_out_v = w_out.rearrange("l (k p) n -> l p k n", p=P)
        w_gate_v = w_ple_gate.rearrange("l (k p) n -> l p k n", p=P)
        w_ple_v = w_ple.rearrange("l (k p) n -> l p k n", p=P)
        w_uq_v = w_uq.rearrange("l (k p) n -> l p k n", p=P)
        w_rg_v = w_router_group.rearrange("l (k p) n -> l p k n", p=P)
        w_re_v = w_router_expert.rearrange("l (k p) n -> l p k n", p=P)
        w_s_v = w_s.rearrange("l g t j -> l t g j")
        b_s_v = b_s.rearrange("l g t -> l t g")
        g_v_v = g_v.rearrange("l g c -> l (g c)")
        w1_v = w1.rearrange("l e (k p) f -> (l e) p k f", p=P)
        w3_v = w3.rearrange("l e (k p) f -> (l e) p k f", p=P)
        w2_v = w2.rearrange("l e (k p) d -> (l e) p k d", p=P)
        xn_v = xn_rows.rearrange("(t p) d -> t p d", p=P)
        y_v = y_rows.rearrange("(b p) d -> b p d", p=P)

        consts_in, x_in = sem("consts_in"), sem("x_in")
        w_in_in, ab_in, wout_in, cpar_in = sem("w_in_in"), sem("ab_in"), sem("wout_in"), sem("cpar_in")
        ple_w_in, e_par_in, out_done = sem("ple_w_in"), sem("e_par_in"), sem("out_done")
        p_in = [sem(f"p_in{j}") for j in range(2)]
        raw_in = [sem(f"raw_in{s}") for s in range(6)]
        ACT_E, DVE_E, PE_E, POOL_E = "act", "dve", "pe", "pool"
        done = {e: sem(f"phase_done_{e}") for e in (ACT_E, DVE_E, PE_E, POOL_E)}
        half_set, y_filled = sem("half_set"), sem("y_filled")
        f_stat, f_pool, f_rstd, f_xn = sem("f_stat"), sem("f_pool"), sem("f_rstd"), sem("f_xn")
        f_tp0, f_tp1, f_ev0, f_ev1 = sem("f_tp0"), sem("f_tp1"), sem("f_ev0"), sem("f_ev1")
        a_mv, a_mc, a_mu = sem("a_mv"), sem("a_mc"), sem("a_mu")
        a_gv, a_gu, a_csq, a_rc = sem("a_gv"), sem("a_gu"), sem("a_csq"), sem("a_rc")
        a_v2, a_rv, a_cn, a_vn, a_m = sem("a_v2"), sem("a_rv"), sem("a_cn"), sem("a_vn"), sem("a_m")
        a_tc, a_ce, a_s = sem("a_tc"), sem("a_ce"), sem("a_s")
        a_pool_c, a_pool_v, a_dve = sem("a_pool_c"), sem("a_pool_v"), sem("a_dve")
        ws_t, ws_e, ws_dve = sem("ws_t"), sem("ws_e"), sem("ws_dve")
        b_proj, b_sq, b_pev, b_ss, b_rs, b_rp, b_qk = (sem(n) for n in
                                                       ("b_proj", "b_sq", "b_pev", "b_ss", "b_rs", "b_rp", "b_qk"))
        b_kr, b_sum, b_rot = sem("b_kr"), sem("b_sum"), sem("b_rot")
        b_t, b_tev_a, b_tev_d = sem("b_t"), sem("b_tev_a"), sem("b_tev_d")
        b_s, b_max, b_exp = sem("b_s"), sem("b_max"), sem("b_exp")
        b_pt, b_pte_a, b_pte_d = sem("b_pt"), sem("b_pte_a"), sem("b_pte_d")
        b_pv, b_o = sem("b_pv"), sem("b_o")
        b_dve, b_pool, b_max_c = (sem(n) for n in ("b_dve", "b_pool", "b_max_c"))
        c_y0, c_y1, c_h0, c_h1 = sem("c_y0"), sem("c_y1"), sem("c_h0"), sem("c_h1")
        c_sf, c_rf, c_xf, c_xst = sem("c_sf"), sem("c_rf"), sem("c_xf"), sem("c_xst")
        c_f0, c_f1, c_fe0, c_fe1 = sem("c_f0"), sem("c_f1"), sem("c_fe0"), sem("c_fe1")
        c_rt, c_lgm, c_lge = sem("c_rt"), sem("c_lgm"), sem("c_lge")
        c_pool2, c_dve, c_dve2 = sem("c_pool2"), sem("c_dve"), sem("c_dve2")
        r_rank, r_dve, r_ovt, r_ovsb, r_ovs, r_exp, r_gap = (sem("r_rank"), sem("r_dve"), sem("r_ovt"), sem("r_ovsb"),
                                                     sem("r_ovs"), sem("r_exp"), sem("r_gap"))
        r_oh, r_idx = sem("r_oh"), sem("r_idx")
        r_plan = sem("r_plan")
        d_idx, d_xg = sem("d_idx"), sem("d_xg")
        d_tx, d_xhi0, d_xhi1, d_xlo0, d_xlo1 = sem("d_tx"), sem("d_xhi0"), sem("d_xhi1"), sem("d_xlo0"), sem("d_xlo1")
        d_hi, d_lo, d_mm = sem("d_hi"), sem("d_lo"), sem("d_mm")
        d_silu, d_gm, d_tg, d_ghi, d_glo = sem("d_silu"), sem("d_gm"), sem("d_tg"), sem("d_ghi"), sem("d_glo")
        d_yev, d_yst = sem("d_yev"), sem("d_yst")
        e_idx, e_yg = sem("e_idx"), [sem(f"e_yg{j}") for j in range(2)]
        e_comb = sem("e_comb")
        e_tpp, e_evp = sem("e_tpp"), sem("e_evp")
        e_g0, e_g1, e_pl = sem("e_g0"), sem("e_g1"), sem("e_pl")
        e_b0, e_b1, e_sg, e_h = sem("e_b0"), sem("e_b1"), sem("e_sg"), sem("e_h")
        e_dve, e_fin = sem("e_dve"), sem("e_fin")
        r_gates, r_sel = sem("r_gates"), sem("r_sel")

        def steady(eng):
            eng.nop(nofuse=True)

        def next_phase(eng, me, layer, phase):
            steady(eng)
            eng.drain().then_inc(done[me], 1)
            for other in done:
                eng.wait_ge(done[other], layer * PHASES + phase + 1)

        def over_tiles(eng, turn):
            turn(0, 0, True, False)
            steady(eng)
            with eng.Fori(0, NT // 2 - 1) as i:
                turn(i * 2 + 1, 1, False, False)
                turn(i * 2 + 2, 0, False, False)
            turn(NT - 1, 1, False, True)

        def credit(eng, n, *signals):
            for s in signals:
                eng.sem_inc(s, n)

        def grouped(ap, g):
            return ap.rearrange("p (g c) -> p g c", g=g)

        def spread(ap, n):
            return ap.unsqueeze(2).broadcast_to([ap.shape[0], ap.shape[1], n])

        block = ctx.enter_context(nc.Block())

        @block.sync
        def _(sp):
            def load_ab(layer):
                one = lambda v: v[ds(layer, 1)]
                sp.dma_start(w_in_sb[:, :, :], one(w_in_v).rearrange("o p k n -> p (o k) n")).then_inc(w_in_in, 16)
                sp.dma_start(g_mix_sb[:, :], one(g_mix_norm).broadcast_to([P, D])).then_inc(ab_in, 16)
                sp.dma_start(g_c_sb[:, 0:Q_RANK], one(g_cq).broadcast_to([P, Q_RANK])).then_inc(ab_in, 16)
                sp.dma_start(g_c_sb[:, Q_RANK:CQKV], one(g_ckv).broadcast_to([P, KV_RANK])).then_inc(ab_in, 16)
                sp.dma_start(g_v_sb[:, :], one(g_v_v).broadcast_to([P, 512])).then_inc(ab_in, 16)
                sp.dma_start(g_qk_sb[:, 0, :], one(g_qn).broadcast_to([P, QK])).then_inc(ab_in, 16)
                sp.dma_start(g_qk_sb[:, 1, :], one(g_kn).broadcast_to([P, QK])).then_inc(ab_in, 16)
                sp.dma_start(bs_sb[:, :], one(b_s_v).rearrange("o t g -> (o t) g"),
                             allow_slow_non_contiguous=True).then_inc(ab_in, 16)
                for dst, g0, g1 in ((ws_nat[0], 0, 6), (ws_nat[1], 6, GROUPS)):
                    sp.dma_start(grouped(dst[:, :], g1 - g0),
                                 one(w_s_v)[:, :, g0:g1, :].rearrange("o t g j -> t (o g) j")).then_inc(ab_in, 16)
                sp.dma_start(w_uq_sb[:, :, :], one(w_uq_v).rearrange("o p k n -> p (o k) n")).then_inc(ab_in, 16)
                sp.dma_start(w_ukv_sb[:, :], one(w_ukv).rearrange("o p n -> (o p) n")).then_inc(ab_in, 16)

            def chunk(layer, expert, which, part, slot):
                if which == 2:
                    src = w2_v[ds(layer * NE + expert, 1)][:, :, 2 * part:2 * part + 2, :]
                    dst = ring_raw[:, slot, :].rearrange("p (k n) -> p k n", k=2)
                else:
                    src = (w1_v if which == 1 else w3_v)[ds(layer * NE + expert, 1)][:, :, 4 * part:4 * part + 4, :]
                    dst = ring_raw[:, slot, :].rearrange("p (k n) -> p k n", k=4)
                sp.dma_start(dst, src.rearrange("o p k n -> p (o k) n")).then_inc(raw_in[slot], 16)

            sp.sem_inc(c_xst, 16)
            sp.dma_start(consts[:, :], shape_consts).then_inc(consts_in, 16)
            sp.dma_start(h[:, :].rearrange("p (t d) -> p t d", t=NT), x_v).then_inc(x_in, 16)
            load_ab(0)
            x_rows = x.rearrange("b s d -> (b s) d")
            for row in range(NE * P, NBLK * P, SEQ):
                n = min(SEQ, NBLK * P - row)
                sp.dma_start(y_rows[row:row + n, :], x_rows[0:n, :]).then_inc(y_filled, 16)
            with sp.Fori(0, DEPTH) as layer:
                ph = lambda e, phase: sp.wait_ge(done[e], layer * PHASES + phase + 1)
                ph(PE_E, PH_A)
                one = lambda v: v[ds(layer, 1)]
                sp.dma_start(w_out_sb[:, :, :], one(w_out_v).rearrange("o p k n -> p (o k) n")).then_inc(wout_in, 16)
                sp.dma_start(g_out_sb[:, 0:MIXW], one(g_out_mla).broadcast_to([P, MIXW])).then_inc(cpar_in, 16)
                sp.dma_start(g_out_sb[:, MIXW:D], one(g_out_gmlp).broadcast_to([P, MIXW])).then_inc(cpar_in, 16)
                sp.dma_start(g_ffn_sb[:, :], one(g_ffn_norm).broadcast_to([P, D])).then_inc(cpar_in, 16)
                sp.dma_start(w_router[:, :, 0:NG], one(w_rg_v).rearrange("o p k n -> p (o k) n")).then_inc(cpar_in, 16)
                sp.dma_start(w_router[:, :, NG:NROUTE], one(w_re_v).rearrange("o p k n -> p (o k) n")).then_inc(cpar_in, 16)
                steady(sp)
                with sp.Fori(0, NT) as t:
                    sp.wait_ge(c_xf, layer * NT + t + 1)
                    sp.dma_start(xn_v[ds(t, 1)].rearrange("o p d -> (o p) d"), xf[:, :]).then_inc(c_xst, 16)
                sp.wait_ge(c_rt, (layer + 1) * NT)
                steady(sp)
                before_here = sp.value_load(next_gb[0:1, ds(layer, 1)], min_val=0, max_val=DEPTH * NBLK)
                n = [0]

                def stream(expert, which, part, turn):
                    s = n[0]
                    n[0] += 1
                    sp.wait_ge(d_lo, before_here * 6 + turn * 6 + s + 1)
                    chunk(layer, expert, which, part, s % 6)

                for b in range(2):
                    for which in (1, 3):
                        for part in range(2):
                            stream(b, which, part, 0)

                def turn(b, before_last, this):
                    n[0] = 8
                    for part in range(2):
                        stream(before_last, 2, part, b - 2)
                    for which in (1, 3):
                        for part in range(2):
                            stream(this, which, part, b - 2)

                steady(sp)
                with sp.Fori(2, NE) as b:
                    turn(b, b - 2, b)
                sp.dma_start(w_gate_sb[:, :, :], one(w_gate_v).rearrange("o p k n -> p (o k) n")).then_inc(ple_w_in, 16)
                sp.dma_start(w_ple_sb[:, :, :], one(w_ple_v).rearrange("o p k n -> p (o k) n")).then_inc(ple_w_in, 16)
                sp.wait_ge(r_plan, layer + 1)
                steady(sp)
                nb2 = sp.value_load(plan[0:1, 0:1], min_val=NE - 2, max_val=NBLK - 2)
                nb = nb2 + 2
                expert_of = lambda b: sp.value_load(expert_i[0:1, ds(b, 1)], min_val=0, max_val=NE - 1)
                steady(sp)
                with sp.Fori(NE, NBLK) as b:
                    with sp.If(b < nb):
                        steady(sp)
                        turn(b, expert_of(b - 2), expert_of(b))
                n[0] = 8
                for back in (2, 1):
                    steady(sp)
                    e = expert_of(nb2 + 2 - back)
                    for part in range(2):
                        stream(e, 2, part, nb2)
                for e in (PE_E, DVE_E, ACT_E):
                    ph(e, PH_D)
                sp.dma_start(g_ple_sb[:, :], one(g_ple).broadcast_to([P, D])).then_inc(e_par_in, 16)
                sp.dma_start(b_gate_sb[:, :], one(b_ple_gate).broadcast_to([P, D])).then_inc(e_par_in, 16)

                def load_p(t, j):
                    sp.wait_ge(e_tpp, layer * NT + t + 1)
                    sp.dma_start(p_sb[j][:, :], p_v[ds(layer * NT + t, 1)].rearrange("o p d -> (o p) d"))\
                      .then_inc(p_in[j], 16)

                load_p(0, 0)
                load_p(1, 1)
                with sp.If(layer < DEPTH - 1):
                    load_ab(nc.s_assert_within(
                        layer + 1, min_val=1, max_val=DEPTH - 1,
                        skip_runtime_bounds_check_because="only where layer < DEPTH - 1"))
                steady(sp)
                with sp.Fori(1, NT // 2) as i:
                    load_p(i * 2, 0)
                    load_p(i * 2 + 1, 1)
            for t in range(NT):
                sp.wait_ge(e_h, (DEPTH - 1) * NT + t + 2)
                sp.dma_start(out_v[:, t, :], h[:, t * D:(t + 1) * D]).then_inc(out_done, 16)
            sp.wait_ge(out_done, 16 * NT)

        @block.gpsimd
        def _(pool):
            def rsqrt(out_ap, in_ap, scale, order, done, raises):
                n = in_ap.shape[1]
                steady(pool)
                pool.tensor_scalar(tmp_p[:, 0:n], in_ap, scale, EPS, ALU.mult, ALU.add).then_inc(order, 1)
                pool.wait_ge(order, done)
                pool.tensor_tensor(out_ap, tmp_p[:, 0:n], half[:, 0:n], ALU.pow).then_inc(raises, 1)

            pool.memset(half[:, :], -0.5).then_inc(half_set, 1)
            pool.wait_ge(half_set, 1)
            pool.wait_ge(consts_in, 16)
            with pool.Fori(0, DEPTH) as layer:
                it = lambda t: layer * NT + t
                ft = lambda phase, t: (layer * 3 + phase) * NT + t
                next_phase(pool, POOL_E, layer, PH_WS)

                def rstd_x_of(t, j):
                    pool.wait_ge(f_stat, ft(0, t) + 1)
                    rsqrt(rstd_x[:, j:j + 1], stat_x[:, j:j + 1], 1.0, f_pool, ft(0, t) + 1, f_rstd)
                    pool.wait_ge(f_rstd, ft(0, t) + 1)

                def turn(t, j, first, last):
                    if first:
                        rstd_x_of(0, 0)
                    if not last:
                        rstd_x_of(t + 1, 1 - j)
                    pool.wait_ge(a_csq, it(t) + 1)
                    rsqrt(rstd_c[:, :], stat_c[:, :], 1.0, a_pool_c, it(t) + 1, a_rc)
                    pool.wait_ge(a_rc, it(t) + 1)
                    pool.wait_ge(a_v2, it(t) + 1)
                    rsqrt(rstd_v[:, :], stat_v[:, :], 1.0 / GDIM, a_pool_v, it(t) + 1, a_rv)
                    pool.wait_ge(a_rv, it(t) + 1)

                over_tiles(pool, turn)
                next_phase(pool, POOL_E, layer, PH_A)

                def normalise(hd):
                    steady(pool)
                    pool.wait_ge(b_pev, it(hd) * 4 + 2)
                    pool.wait_ge(b_qk, it(hd) * 2 + 1)
                    steady(pool)
                    pool.tensor_tensor(rope_c[:, :, :], qkb[:, 0, :, NOPE:QK], cos2, ALU.mult)
                    pool.tensor_tensor(rope_s[:, :, :], qkb[:, 0, :, NOPE:QK], sin2, ALU.mult).then_inc(b_rp, 1)
                    for i in range(2):
                        pool.wait_ge(b_ss, it(hd) * 2 + i + 1)
                        v = slice(i * NT, (i + 1) * NT)
                        rsqrt(rstd_qk[:, v], stat_qk[:, v], 1.0, b_pool, it(hd) * 2 + i + 1, b_rs)
                        pool.wait_ge(b_rs, it(hd) * 2 + i + 1)

                def turn(hd, j, first, last):
                    if first:
                        normalise(0)
                    if not last:
                        normalise(hd + 1)

                over_tiles(pool, turn)
                next_phase(pool, POOL_E, layer, PH_B)

                def rstd_c_of(t):
                    pool.wait_ge(f_stat, ft(1, t) + 1)
                    rsqrt(rstd_c[:, :], stat_c[:, :], 1.0, f_pool, ft(1, t) + 1, f_rstd)
                    pool.wait_ge(f_rstd, ft(1, t) + 1)

                def turn(t, j, first, last):
                    if first:
                        rstd_c_of(0)
                    if not last:
                        rstd_c_of(t + 1)
                    pool.wait_ge(c_sf, it(t) + 2)
                    rsqrt(rstd_f[:, :], stat_f[:, :], 1.0, c_pool2, it(t) + 1, c_rf)
                    pool.wait_ge(c_rf, it(t) + 1)

                over_tiles(pool, turn)
                next_phase(pool, POOL_E, layer, PH_C)

                pool.wait_ge(c_xst, (layer * NT + NT + 1) * 16)
                pool.wait_ge(r_plan, layer + 1)
                steady(pool)
                nb2 = pool.value_load(plan[0:1, 0:1], min_val=NE - 2, max_val=NBLK - 2)
                nb = nb2 + 2
                gb = pool.value_load(plan[0:1, 1:2], min_val=0, max_val=DEPTH * NBLK)

                def gather(b):
                    pool.wait_ge(d_tx, gb + b + 1)
                    steady(pool)
                    pool.tensor_copy(idx_x[:, :], slot_tok[:, ds(b, 1)]).then_inc(d_idx, 1)
                    pool.wait_ge(d_idx, gb + b + 1)
                    steady(pool)
                    pool.indirect_dma_start(xg[:, :], None, xn_rows,
                                            bass.IndirectOffsetOnAxis(ap=idx_x[:, :], axis=0)).then_inc(d_xg, 16)

                steady(pool)
                with pool.Fori(0, NE) as b:
                    gather(b)
                steady(pool)
                with pool.Fori(NE, NBLK) as b:
                    with pool.If(b < nb):
                        gather(b)
                next_phase(pool, POOL_E, layer, PH_D)

                pool.wait_ge(d_yst, (gb + nb + 1) * 16)

                def gather2(t, j):
                    pool.wait_ge(e_comb, it(t) + 1)
                    steady(pool)
                    for k in range(TOPK):
                        pool.tensor_copy(idx_y[j][k][:, :], dest_u[:, ds(t + k * NT, 1)]).then_inc(e_idx, 1)
                    pool.wait_ge(e_idx, (it(t) + 1) * 2)
                    steady(pool)
                    for k in range(TOPK):
                        pool.indirect_dma_start(yg[j][k][:, :], None, y_rows,
                                                bass.IndirectOffsetOnAxis(ap=idx_y[j][k][:, :], axis=0))\
                            .then_inc(e_yg[j], 16)

                def rstd_e(t, j):
                    pool.wait_ge(f_stat, ft(2, t) + 1)
                    rsqrt(rstd_x[:, j:j + 1], stat_x[:, j:j + 1], 1.0, f_pool, ft(2, t) + 1, f_rstd)
                    pool.wait_ge(f_rstd, ft(2, t) + 1)

                def turn(t, j, first, last):
                    if first:
                        gather2(0, 0)
                        rstd_e(0, 0)
                    if not last:
                        gather2(t + 1, 1 - j)
                        rstd_e(t + 1, 1 - j)

                over_tiles(pool, turn)
                next_phase(pool, POOL_E, layer, PH_E)

        @block.scalar
        def _(act):
            credit(act, 1, c_sf, f_ev0, a_gv, a_gu, a_ce, b_pte_a,
                   c_fe0, c_lge, d_silu, d_yev, e_evp)
            credit(act, 2, b_exp)
            act.sem_inc(d_yst, 16)
            act.wait_ge(consts_in, 16)
            act.wait_ge(x_in, 16)

            def copy(out_ap, in_ap):
                return act.activation(out_ap, in_ap, ACT.Copy)

            with act.Fori(0, DEPTH) as layer:
                it = lambda t: layer * NT + t
                ft = lambda phase, t: (layer * 3 + phase) * NT + t
                h_t = lambda t: h[:, ds(t * D, D)]
                next_phase(act, ACT_E, layer, PH_WS)

                def front(t, j):
                    steady(act)
                    act.activation(junk[:, :], h_t(t), ACT.Square, scale=float(D) ** -0.5,
                                   accum_out=stat_x[:, j:j + 1]).then_inc(f_stat, 1)
                    act.wait_ge(f_tp0, ft(0, t) + 1)
                    copy(xT[j][:, 0:4, :], grouped(bank(0), 4)).then_inc(f_ev0, 1)

                def turn(t, j, first, last):
                    if first:
                        front(0, 0)
                    if not last:
                        front(t + 1, 1 - j)
                    act.wait_ge(a_mv, it(t) + 1)
                    act.wait_ge(a_m, it(t) + 1)
                    act.activation(gv_sb[:, :], bank(4), ACT.Gelu_apprx_tanh).then_inc(a_gv, 1)
                    act.wait_ge(a_mc, it(t) + 1)
                    act.activation(junk_c[:, 0:Q_RANK], bank(2)[:, 0:Q_RANK], ACT.Square, scale=float(Q_RANK) ** -0.5,
                                   accum_out=stat_c[:, 0:1])
                    act.activation(junk_c[:, Q_RANK:CQKV], bank(2)[:, Q_RANK:CQKV], ACT.Square,
                                   scale=float(KV_RANK) ** -0.5, accum_out=stat_c[:, 1:2]).then_inc(a_csq, 1)
                    act.wait_ge(a_mu, it(t) + 1)
                    act.activation(gu_sb[:, :], bank(3), ACT.Gelu_apprx_tanh).then_inc(a_gu, 1)
                    act.wait_ge(a_tc, it(t) + 2)
                    steady(act)
                    copy(cT[:, :, ds(t * P, P)], grouped(bank(5)[:, 0:CQKV], 3)).then_inc(a_ce, 1)

                over_tiles(act, turn)
                next_phase(act, ACT_E, layer, PH_A)

                def squares(hd, j, n, first=False):
                    act.wait_ge(b_proj, it(hd) * 4 + n + 1)
                    if not first:
                        act.wait_ge(b_ss, it(hd) * 2)
                    four = slice(4 * (n % 2), 4 * (n % 2) + 4)
                    if n < 2:
                        act.activation(qksq[:, 0, four, :], grouped(bank(0)[:, 0:4 * QK], 4), ACT.Square,
                                       scale=SCALE).then_inc(b_sq, 1)
                    else:
                        kv = grouped(bank(0), 4)
                        act.activation(qksq[:, 1, four, 0:NOPE], kv[:, :, 0:NOPE], ACT.Square, scale=SCALE)
                        copy(v_sb[j][:, four, :], kv[:, :, NOPE:P]).then_inc(b_sq, 1)

                def tr_ev(hd, j, n):
                    act.wait_ge(b_t, it(hd) * 4 + 2 + n + 1)
                    copy(qkT[j][:, n, 512:1024], bank(0)[0:QK, :]).then_inc(b_tev_a, 1)

                def exp_of(hd, j, i):
                    act.wait_ge(b_max, it(hd) * 8 + i + 1)
                    act.wait_ge(b_pt, it(hd) * N_PT + (GROUP_OF[i - 1] if i >= 1 else GROUP_OF[-2] - N_PT) + PT_BACK)
                    w = (i + 1) * P
                    act.activation(prob[i % 2][:, 0:w], bank(2 + 2 * (i % 2), 2)[:, 0:w], ACT.Exp,
                                   bias=neg_max[:, i % 2:i % 2 + 1], scale=SCALE,
                                   accum_out=row_sum[:, j * NT + i:j * NT + i + 1]).then_inc(b_exp, 1)

                def probs_ev(hd, i):
                    for g in range(GROUP_OF[i], GROUP_OF[i + 1]):
                        if g % 2 == 0:
                            n = GROUP_N[g]
                            act.wait_ge(b_pt, it(hd) * N_PT + g + 1 + PT_BACK)
                            copy(probT[g % 2][:, 0:n, :], grouped(bank(1)[:, 0:n * P], n)).then_inc(b_pte_a, 1)

                def turn(hd, j, first, last):
                    if first:
                        for n in range(4):
                            squares(0, 0, n, True)
                        for n in range(2):
                            tr_ev(0, 0, n)
                        exp_of(0, 0, 0)
                    for i in range(NT):
                        probs_ev(hd, i)
                        if i + 1 < NT:
                            exp_of(hd, j, i + 1)
                        elif not last:
                            act.wait_ge(b_o, it(hd) + 1)
                            exp_of(hd + 1, 1 - j, 0)
                        if not last:
                            if i < 4:
                                squares(hd + 1, 1 - j, i)
                            if i == NT - 1:
                                for n in range(2):
                                    tr_ev(hd + 1, 1 - j, n)

                over_tiles(act, turn)
                next_phase(act, ACT_E, layer, PH_B)

                def stats(t):
                    act.wait_ge(f_xn, ft(1, t) + 1)
                    steady(act)
                    act.activation(junk[:, 0:MIXW], a_all[:, ds(t, 1), :].rearrange("p o c -> p (o c)"), ACT.Square,
                                   scale=float(MIXW) ** -0.5, accum_out=stat_c[:, 0:1])
                    act.activation(junk[:, MIXW:D], m_all[:, ds(t * MIXW, MIXW)], ACT.Square,
                                   scale=float(MIXW) ** -0.5, accum_out=stat_c[:, 1:2]).then_inc(f_stat, 1)

                def front(t, j):
                    act.wait_ge(f_tp0, ft(1, t) + 1)
                    copy(xT[j][:, 0:4, :], grouped(bank(0), 4)).then_inc(f_ev0, 1)

                def tail_ev(t):
                    act.wait_ge(c_f0, it(t) + 1)
                    copy(xfT[:, 0:4, :], grouped(bank(4), 4)).then_inc(c_fe0, 1)

                def tail_exp(t):
                    act.wait_ge(c_lgm, it(t) + 1)
                    steady(act)
                    act.activation(lge[:, :], lgm[:, :], ACT.Exp, accum_out=sum_all[:, ds(t, 1)]).then_inc(c_lge, 1)

                def turn(t, j, first, last):
                    if first:
                        stats(0)
                        front(0, 0)
                    if not last:
                        act.wait_ge(c_sf, it(t) + 1)
                        stats(t + 1)
                    if not first:
                        tail_ev(t - 1)
                    if not last:
                        front(t + 1, 1 - j)
                    act.wait_ge(c_h1, it(t) + 2)
                    steady(act)
                    act.activation(junk[:, :], h_t(t), ACT.Square, scale=float(D) ** -0.5,
                                   accum_out=stat_f[:, :]).then_inc(c_sf, 1)
                    if not first:
                        tail_exp(t - 1)
                    if last:
                        tail_ev(t)
                        tail_exp(t)

                over_tiles(act, turn)
                act.wait_ge(r_gap, layer + 1)
                act.activation(exp_g[:, :], gap_all[:, :], ACT.Exp).then_inc(r_exp, 1)
                next_phase(act, ACT_E, layer, PH_C)

                steady(act)
                nb2 = act.value_load(plan[0:1, 0:1], min_val=NE - 2, max_val=NBLK - 2)
                nb = nb2 + 2
                gb = act.value_load(plan[0:1, 1:2], min_val=0, max_val=DEPTH * NBLK)

                def hi(s, turns):
                    q = s % 6
                    act.wait_ge(raw_in[q], (gb + turns + (s // 6 + 1)) * 16)
                    act.wait_ge(d_mm, gb * 6 + turns * 6 + s + 1)
                    copy(ring_hi[:, s % 3, :], ring_raw[:, q, :]).then_inc(d_hi, 1)

                def x_hi(b):
                    for i, s in enumerate((d_xhi0, d_xhi1)):
                        act.wait_ge(d_tx, gb + b + 2)
                        copy(xg_hi[:, 4 * i:4 * i + 4, :], grouped(bank(i), 4)).then_inc(s, 1)

                def silu_of(b, chunks):
                    act.wait_ge(d_mm, gb * 6 + chunks + 3)
                    act.wait_ge(d_gm, gb + b + 1)
                    act.activation(silu_sb[:, :], bank(3), ACT.Silu).then_inc(d_silu, 1)

                def g_hi(b):
                    act.wait_ge(d_tg, gb + b + 2)
                    copy(gT_hi[:, :, :], grouped(bank(2), 4)).then_inc(d_ghi, 1)

                def y_out(b, chunks):
                    act.wait_ge(d_mm, gb * 6 + chunks + 3)
                    act.wait_ge(d_yst, (gb + b + 1) * 16)
                    for i in range(2):
                        last = copy(y_sb[:, i * 512:(i + 1) * 512], bank(5 + i))
                    last.then_inc(d_yev, 1)
                    act.wait_ge(d_yev, gb + b + 2)
                    steady(act)
                    act.dma_start(y_v[ds(b, 1)].rearrange("o p d -> (o p) d"), y_sb[:, :]).then_inc(d_yst, 16)

                act.wait_ge(y_filled, 16 * -(-MAX_OVER * P // SEQ))
                x_hi(0)
                for s in range(3):
                    hi(s, 0)
                hi(3, 0)
                silu_of(0, 2)
                x_hi(1)
                for s in (4, 5):
                    hi(s, 0)
                g_hi(0)
                for s in (6, 7, 8, 9):
                    hi(s, 0)

                def turn(b):
                    silu_of(b - 1, (b - 2) * 6 + 6)
                    x_hi(b)
                    hi(10, b - 2)
                    hi(11, b - 2)
                    y_out(b - 2, (b - 2) * 6 + 10)
                    g_hi(b - 1)
                    for s in (12, 13, 14, 15):
                        hi(s, b - 2)

                steady(act)
                with act.Fori(2, NE) as b:
                    turn(b)
                steady(act)
                with act.Fori(NE, NBLK) as b:
                    with act.If(b < nb):
                        turn(b)
                silu_of(nb2 + 1, (nb2) * 6 + 6)
                y_out(nb2, (nb2) * 6 + 10)
                g_hi(nb2 + 1)
                for s in (10, 11):
                    hi(s, nb2)
                y_out(nb2 + 1, (nb2) * 6 + 12)
                next_phase(act, ACT_E, layer, PH_D)

                def front(t, j):
                    act.wait_ge(e_comb, it(t) + 3)
                    steady(act)
                    act.activation(junk[:, :], h_t(t), ACT.Square, scale=float(D) ** -0.5,
                                   accum_out=stat_x[:, j:j + 1]).then_inc(f_stat, 1)
                    act.wait_ge(f_tp0, ft(2, t) + 1)
                    copy(xT[j][:, 0:4, :], grouped(bank(0), 4)).then_inc(f_ev0, 1)
                    act.wait_ge(e_tpp, it(t) + 3)
                    copy(pT[j][:, :, :], grouped(bank(6)[:, 0:PLE], 2)).then_inc(e_evp, 1)

                def turn(t, j, first, last):
                    if first:
                        front(0, 0)
                    if not last:
                        front(t + 1, 1 - j)
                    act.wait_ge(e_b1, it(t) + 2)
                    act.activation(gs[:, :], gs[:, :], ACT.Sigmoid).then_inc(e_sg, 1)

                over_tiles(act, turn)
                next_phase(act, ACT_E, layer, PH_E)

        @block.vector
        def _(dve):
            credit(dve, 1, f_xn, f_ev1, a_cn, a_m, b_pte_d, b_o, c_h0,
                   c_h1, c_fe1, d_xlo0, d_xlo1, d_gm, d_glo, e_b0, e_b1, e_h)
            credit(dve, 1, b_qk)
            credit(dve, 2, e_comb)
            credit(dve, 6, d_lo)
            dve.memset(next_gb[:, :], 0)
            dve.memset(gb_f[:, :], 0.0)
            dve.memset(lg8[:, :], NEG)
            dve.memset(picks[:, 0, :], 0.0)
            dve.wait_ge(consts_in, 16)
            dve.wait_ge(x_in, 16)
            dve.tensor_copy(expert_i[:, 0:NE], iota_e)
            stt = dve.scalar_tensor_tensor
            tt = dve.tensor_tensor
            ts = dve.tensor_scalar

            with dve.Fori(0, DEPTH) as layer:
                it = lambda t: layer * NT + t
                ft = lambda phase, t: (layer * 3 + phase) * NT + t
                h_t = lambda t: h[:, ds(t * D, D)]

                c = Count(2, layer)
                for i in range(2):
                    dve.wait_ge(ws_t, layer * 2 + i + 1)
                    dve.tensor_copy(wsT[:, 4 * i:4 * i + 4, :], grouped(bank(i), 4)).then_inc(ws_dve, 1)
                    dve.wait_ge(ws_dve, c.next())
                c.close()
                dve.memset(wsT[CHUNK:P, :, 0:CHUNK], 0.0).then_inc(ws_e, 1)
                dve.wait_ge(ab_in, 16 * AB_LOADS * (layer + 1))
                next_phase(dve, DVE_E, layer, PH_WS)

                def front(t, j):
                    dve.wait_ge(f_rstd, ft(0, t) + 1)
                    stt(xn[j][:, :], h_t(t), rstd_x[:, j:j + 1], g_mix_sb[:, :], ALU.mult, ALU.mult)\
                        .then_inc(f_xn, 1)
                    dve.wait_ge(f_tp1, ft(0, t) + 1)
                    dve.tensor_copy(xT[j][:, 4:8, :], grouped(bank(1), 4)).then_inc(f_ev1, 1)

                def turn(t, j, first, last):
                    if first:
                        front(0, 0)
                    if not last:
                        front(t + 1, 1 - j)
                    c = Count(3, it(t))
                    dve.wait_ge(a_gv, it(t) + 2)
                    tt(vsq[:, :], gv_sb[:, :], gv_sb[:, :], ALU.mult).then_inc(a_dve, 1)
                    dve.wait_ge(a_dve, c.next())
                    dve.reduce_sum(stat_v[:, :], grouped(vsq[:, :], GROUPS), axis=AX_X).then_inc(a_v2, 1)
                    dve.wait_ge(a_rc, it(t) + 1)
                    dve.wait_ge(a_tc, it(t) + 1)
                    stt(cn[:, 0:Q_RANK], bank(2)[:, 0:Q_RANK], rstd_c[:, 0:1], g_c_sb[:, 0:Q_RANK], ALU.mult, ALU.mult)
                    stt(cn[:, Q_RANK:CQKV], bank(2)[:, Q_RANK:CQKV], rstd_c[:, 1:2], g_c_sb[:, Q_RANK:CQKV],
                        ALU.mult, ALU.mult)
                    dve.tensor_copy(kr_all[:, ds(t, 1), :].rearrange("p o r -> p (o r)"), bank(2)[:, CQKV:W_C])\
                        .then_inc(a_cn, 1)
                    dve.wait_ge(a_rv, it(t) + 1)
                    dve.wait_ge(a_s, it(t) + 1)
                    tt(grouped(vn1[:, :], GROUPS), grouped(gv_sb[:, :], GROUPS), spread(rstd_v[:, :], GDIM), ALU.mult).then_inc(a_dve, 1)
                    dve.wait_ge(a_dve, c.next())
                    tt(vn[:, :], vn1[:, :], g_v_sb[:, :], ALU.mult).then_inc(a_vn, 1)
                    dve.wait_ge(a_s, it(t) + 2)
                    tt(grouped(s_sb[:, :], GROUPS), grouped(bank(6), GROUPS), spread(bs_sb[:, :], GDIM), ALU.add).then_inc(a_dve, 1)
                    dve.wait_ge(a_dve, c.next())
                    c.close()
                    dve.wait_ge(a_gu, it(t) + 2)
                    tt(m_all[:, ds(t * 512, 512)], s_sb[:, :], gu_sb[:, :], ALU.mult).then_inc(a_m, 1)

                over_tiles(dve, turn)
                next_phase(dve, DVE_E, layer, PH_A)

                c = Count(6, layer)
                tt(kr_rot[:, :, :], kr_all[:, :, :], kr_all[:, :, :], ALU.mult).then_inc(b_kr, 1)
                dve.wait_ge(b_kr, c.next())
                dve.reduce_sum(ss_kr[:, :], kr_rot[:, :, :], axis=AX_X).then_inc(b_kr, 1)
                dve.wait_ge(b_kr, c.next())
                tt(kr_all[:, :, :], kr_all[:, :, :], g_qk_sb[:, 1:2, NOPE:QK].broadcast_to([P, NT, ROPE]), ALU.mult)\
                    .then_inc(b_kr, 1)
                dve.wait_ge(b_kr, c.next())
                tt(kr_c[:, :, :], kr_all[:, :, :], cos2, ALU.mult).then_inc(b_kr, 1)
                dve.wait_ge(b_kr, c.next())
                tt(kr_s[:, :, :], kr_all[:, :, :], sin2, ALU.mult).then_inc(b_kr, 1)
                dve.wait_ge(b_kr, c.next())
                hf = ROPE // 2
                tt(kr_rot[:, :, 0:hf], kr_c[:, :, 0:hf], kr_s[:, :, hf:ROPE], ALU.subtract)
                tt(kr_rot[:, :, hf:ROPE], kr_c[:, :, hf:ROPE], kr_s[:, :, 0:hf], ALU.add).then_inc(b_kr, 1)
                dve.wait_ge(b_kr, c.next())
                c.close()

                def proj_ev(hd, n, first=False):
                    dve.wait_ge(b_sq, it(hd) * 4 + n + 1)
                    if not first:
                        dve.wait_ge(b_t, it(hd) * 4)
                    four = slice(4 * (n % 2), 4 * (n % 2) + 4)
                    if n < 2:
                        tt(qkb[:, 0, four, :], grouped(bank(0)[:, 0:4 * QK], 4),
                           g_qk_sb[:, 0:1, :].broadcast_to([P, 4, QK]), ALU.mult).then_inc(b_pev, 1)
                    else:
                        tt(qkb[:, 1, four, 0:NOPE], grouped(bank(0), 4)[:, :, 0:NOPE],
                           g_qk_sb[:, 1:2, 0:NOPE].broadcast_to([P, 4, NOPE]), ALU.mult).then_inc(b_pev, 1)

                def sum_q(hd):
                    dve.wait_ge(b_sq, it(hd) * 4 + 2)
                    dve.reduce_sum(stat_qk[:, 0:NT], qksq[:, 0, :, :], axis=AX_X).then_inc(b_ss, 1)

                def sum_k(hd):
                    dve.wait_ge(b_sq, it(hd) * 4 + 4)
                    dve.reduce_sum(stat_qk[:, NT:2 * NT], qksq[:, 1, :, 0:NOPE], axis=AX_X).then_inc(b_sum, 1)
                    dve.wait_ge(b_sum, it(hd) + 1)
                    stt(stat_qk[:, NT:2 * NT], ss_kr[:, :], 1.0 / QK, stat_qk[:, NT:2 * NT], ALU.mult, ALU.add)\
                        .then_inc(b_ss, 1)

                def norm_q(hd):
                    dve.wait_ge(b_rp, it(hd) + 1)
                    dve.wait_ge(b_pev, it(hd) * 4 + 2)
                    tt(qkb[:, 0, :, NOPE:NOPE + hf], rope_c[:, :, 0:hf], rope_s[:, :, hf:ROPE], ALU.subtract)
                    tt(qkb[:, 0, :, NOPE + hf:QK], rope_c[:, :, hf:ROPE], rope_s[:, :, 0:hf], ALU.add).then_inc(b_rot, 1)
                    dve.wait_ge(b_rot, it(hd) + 1)
                    dve.wait_ge(b_rs, it(hd) * 2 + 1)
                    tt(qkb[:, 0, :, :], qkb[:, 0, :, :], spread(rstd_qk[:, 0:NT], QK), ALU.mult).then_inc(b_qk, 1)

                def norm_k(hd):
                    dve.wait_ge(b_rs, it(hd) * 2 + 2)
                    dve.wait_ge(b_pev, it(hd) * 4 + 4)
                    r = rstd_qk[:, NT:2 * NT]
                    tt(qkb[:, 1, :, 0:NOPE], qkb[:, 1, :, 0:NOPE], spread(r, NOPE), ALU.mult)
                    tt(qkb[:, 1, :, NOPE:QK], kr_rot[:, :, :], spread(r, ROPE), ALU.mult).then_inc(b_qk, 1)

                def tr_ev(hd, j, n):
                    dve.wait_ge(b_t, it(hd) * 4 + n + 1)
                    dve.tensor_copy(qkT[j][:, n, 0:512], bank(0)[0:QK, :]).then_inc(b_tev_d, 1)

                def max_of(hd, i):
                    w = (i + 1) * P
                    s = bank(2 + 2 * (i % 2), 2)
                    c = Count(2, it(hd) * 8 + i)
                    dve.wait_ge(b_s, it(hd) * 8 + i + 1)
                    dve.memset(s[0:CHUNK, w - CHUNK:w], NEG).then_inc(b_max_c, 1)
                    dve.wait_ge(b_max_c, c.next())
                    dve.reduce_max(row_max[:, i % 2:i % 2 + 1], s[:, 0:w], axis=AX_X).then_inc(b_max_c, 1)
                    dve.wait_ge(b_max_c, c.next())
                    dve.wait_ge(b_exp, it(hd) * 8 + i + 1)
                    ts(neg_max[:, i % 2:i % 2 + 1], row_max[:, i % 2:i % 2 + 1], -SCALE, None, ALU.mult)\
                        .then_inc(b_max, 1)

                def probs_ev(hd, i):
                    for g in range(GROUP_OF[i], GROUP_OF[i + 1]):
                        if g % 2 == 1:
                            n = GROUP_N[g]
                            dve.wait_ge(b_pt, it(hd) * N_PT + g + 1 + PT_BACK)
                            dve.tensor_copy(probT[g % 2][:, 0:n, :], grouped(bank(6)[:, 0:n * P], n))\
                                .then_inc(b_pte_d, 1)

                def turn(hd, j, first, last):
                    if first:
                        proj_ev(0, 0, True)
                        proj_ev(0, 1, True)
                        sum_q(0)
                        proj_ev(0, 2, True)
                        proj_ev(0, 3, True)
                        sum_k(0)
                        norm_q(0)
                        norm_k(0)
                        tr_ev(0, 0, 0)
                        tr_ev(0, 0, 1)
                        max_of(0, 0)
                        max_of(0, 1)
                    for i in range(NT):
                        if i == 6 and not last:
                            tr_ev(hd + 1, 1 - j, 1)
                        probs_ev(hd, i)
                        if i + 2 < NT:
                            max_of(hd, i + 2)
                        elif not last:
                            max_of(hd + 1, i + 2 - NT)
                        if not last:
                            if i == 2:
                                sum_q(hd + 1)
                            if i == 3:
                                norm_q(hd + 1)
                            if i < 4:
                                proj_ev(hd + 1, i)
                            if i == 4:
                                sum_k(hd + 1)
                            if i == 5:
                                norm_k(hd + 1)
                                tr_ev(hd + 1, 1 - j, 0)
                    dve.wait_ge(b_exp, it(hd) * 8 + 10)
                    dve.reciprocal(row_inv[:, :], row_sum[:, j * NT:(j + 1) * NT]).then_inc(b_dve, 1)
                    dve.wait_ge(b_dve, it(hd) + 1)
                    dve.wait_ge(b_pv, it(hd) + 1)
                    tt(a_all[:, :, ds(hd * VDIM, VDIM)], grouped(bank(7), NT), spread(row_inv[:, :], VDIM), ALU.mult)\
                        .then_inc(b_o, 1)

                over_tiles(dve, turn)
                dve.wait_ge(cpar_in, 16 * 5 * (layer + 1))
                next_phase(dve, DVE_E, layer, PH_B)

                def cat(t, j):
                    dve.wait_ge(f_rstd, ft(1, t) + 1)
                    stt(xn[j][:, 0:MIXW], a_all[:, ds(t, 1), :].rearrange("p o c -> p (o c)"), rstd_c[:, 0:1],
                        g_out_sb[:, 0:MIXW], ALU.mult, ALU.mult)
                    stt(xn[j][:, MIXW:D], m_all[:, ds(t * MIXW, MIXW)], rstd_c[:, 1:2],
                        g_out_sb[:, MIXW:D], ALU.mult, ALU.mult).then_inc(f_xn, 1)

                def cat_ev(t, j):
                    dve.wait_ge(f_tp1, ft(1, t) + 1)
                    dve.tensor_copy(xT[j][:, 4:8, :], grouped(bank(1), 4)).then_inc(f_ev1, 1)

                def tail_ev(t):
                    dve.wait_ge(c_f1, it(t) + 2)
                    dve.tensor_copy(xfT[:, 4:8, :], grouped(bank(5), 4)).then_inc(c_fe1, 1)

                def route(t):
                    c = Count(12, it(t))
                    dve.wait_ge(c_rt, it(t) + 1)
                    dve.tensor_copy(le[:, :], bank(6)[:, NG:NROUTE])
                    dve.tensor_copy(lg8[:, 0:NG], bank(6)[:, 0:NG]).then_inc(c_dve, 1)
                    dve.wait_ge(c_dve, c.next())
                    steady(dve)
                    dve.max(top8[:, :], lg8[:, :]).then_inc(c_dve, 1)
                    dve.wait_ge(c_dve, c.next())
                    dve.wait_ge(c_lge, it(t) + 1)
                    ts(lgm[:, :], lg8[:, 0:NG], top8[:, 0:1], None, ALU.subtract).then_inc(c_lgm, 1)
                    dve.max_index(gi8[:, :], top8[:, :], lg8[:, :]).then_inc(c_dve, 1)
                    dve.wait_ge(c_dve, c.next())
                    dve.tensor_copy(gf[:, :], gi8[:, 0:1]).then_inc(c_dve, 1)
                    dve.wait_ge(c_dve, c.next())
                    ts(gmask[:, :], iota_e[:, 0:NG], gf[:, 0:1], None, ALU.is_equal).then_inc(c_dve, 1)
                    dve.wait_ge(c_dve, c.next())
                    ts(gbias[:, :], gmask[:, :], -NEG, NEG, ALU.mult, ALU.add).then_inc(c_dve, 1)
                    dve.wait_ge(c_dve, c.next())
                    tt(grouped(le[:, :], NG), grouped(le[:, :], NG), spread(gmask[:, :], PER_G), ALU.mult).then_inc(c_dve, 1)
                    dve.wait_ge(c_dve, c.next())
                    tt(grouped(le[:, :], NG), grouped(le[:, :], NG), spread(gbias[:, :], PER_G), ALU.add).then_inc(c_dve, 1)
                    dve.wait_ge(c_dve, c.next())
                    steady(dve)
                    dve.max(top8e[:, :], le[:, :]).then_inc(c_dve, 1)
                    dve.wait_ge(c_dve, c.next())
                    tt(gap_all[:, ds(t, 1)], top8e[:, 1:2], top8e[:, 0:1], ALU.subtract)
                    dve.max_index(ei8[:, :], top8e[:, :], le[:, :]).then_inc(c_dve, 1)
                    dve.wait_ge(c_dve, c.next())
                    for k in range(TOPK):
                        last = dve.tensor_copy(ef_all[:, k, ds(t, 1)], ei8[:, k:k + 1])
                    last.then_inc(c_dve, 1)
                    dve.wait_ge(c_dve, c.next())
                    for k in range(TOPK):
                        last = ts(onehot[:, k, ds(t, 1), :].rearrange("p o e -> p (o e)"), iota_e,
                                  ef_all[:, k, ds(t, 1)], None, ALU.is_equal)
                    last.then_inc(c_dve, 1)
                    dve.wait_ge(c_dve, c.next())
                    c.close()
                    c = Count(2, it(t))
                    one = lambda a: a.rearrange("p o e -> p (o e)")
                    tt(one(chosen[:, ds(t, 1), :]), one(onehot[:, 0, ds(t, 1), :]), one(onehot[:, 1, ds(t, 1), :]),
                              ALU.add).then_inc(c_dve2, 1)
                    dve.wait_ge(c_dve2, c.next())
                    tt(one(picks[:, ds(t + 1, 1), :]), one(picks[:, ds(t, 1), :]), one(chosen[:, ds(t, 1), :]),
                              ALU.add).then_inc(c_dve2, 1)
                    dve.wait_ge(c_dve2, c.next())
                    c.close()

                def turn(t, j, first, last):
                    if first:
                        cat(0, 0)
                        cat_ev(0, 0)
                    if not last:
                        cat(t + 1, 1 - j)
                    if not first:
                        tail_ev(t - 1)
                    if not last:
                        cat_ev(t + 1, 1 - j)
                    for i, (y, hs) in enumerate(((c_y0, c_h0), (c_y1, c_h1))):
                        dve.wait_ge(y, it(t) + 1)
                        part = h[:, ds(t * D + i * 512, 512)]
                        tt(part, bank(2 + i), part, ALU.add).then_inc(hs, 1)
                    if not first:
                        route(t - 1)
                    dve.wait_ge(c_rf, it(t) + 1)
                    dve.wait_ge(c_f1, it(t) + 1)
                    dve.wait_ge(c_xst, (it(t) + 1) * 16)
                    stt(xf[:, :], h_t(t), rstd_f[:, 0:1], g_ffn_sb[:, :], ALU.mult, ALU.mult).then_inc(c_xf, 1)
                    if last:
                        tail_ev(t)
                        route(t)

                over_tiles(dve, turn)

                R_LINKS = 20
                c = Count(R_LINKS, layer)
                dve.tensor_copy(rank_k[:, 0:NT], gap_all[:, :]).then_inc(r_dve, 1)
                dve.wait_ge(r_dve, c.next())
                dve.sem_inc(r_gap, 1)
                dve.wait_ge(r_rank, layer + 1)
                dve.tensor_copy(rank_sb[:, :, :], grouped(bank(0)[:, 0:NT * NE], NT))
                cmp7 = cmp_s[:, 0:NE * 7].rearrange("p (e s) -> p e s", s=7)
                tt(cmp7, spread(bank(1)[:, 0:NE], 7), steps[:, 0:7].unsqueeze(1).broadcast_to([P, NE, 7]), ALU.is_gt).then_inc(r_dve, 1)
                dve.wait_ge(r_dve, c.next())
                dve.reduce_sum(over_e[:, :], cmp7, axis=AX_X).then_inc(r_dve, 1)
                dve.wait_ge(r_dve, c.next())
                dve.reduce_sum(nb_f[:, :], over_e[:, :], axis=AX_X).then_inc(r_dve, 1)
                dve.wait_ge(r_dve, c.next())
                dve.sem_inc(r_ovt, 1)
                ts(nb_f[:, :], nb_f[:, :], float(NE), None, ALU.add).then_inc(r_dve, 1)
                dve.wait_ge(r_dve, c.next())
                ts(nb2_f[:, :], nb_f[:, :], -2.0, None, ALU.add).then_inc(r_dve, 1)
                dve.wait_ge(r_dve, c.next())
                dve.tensor_copy(plan[:, 0:1], nb2_f[:, :])
                dve.tensor_copy(plan[:, 1:2], gb_f[:, :])
                tt(gb_f[:, :], gb_f[:, :], nb_f[:, :], ALU.add).then_inc(r_dve, 1)
                dve.wait_ge(r_dve, c.next())
                dve.wait_ge(r_ovsb, layer * 2 + 1)
                dve.tensor_copy(overT[:, :], bank(2)[0:NE, 0:P]).then_inc(r_ovs, 1)
                dve.wait_ge(r_ovsb, layer * 2 + 2)
                dve.tensor_copy(over_s[:, :], bank(3)[:, 0:NE]).then_inc(r_dve, 1)
                dve.wait_ge(r_dve, c.next())
                tt(over_end[:, :], over_s[:, :], over_e[:, :], ALU.add).then_inc(r_dve, 1)
                dve.wait_ge(r_dve, c.next())
                cmp16 = cmp_s[:, :].rearrange("p (b e) -> p b e", e=NE)
                tt(cmp16, over_end[:, :].unsqueeze(1).broadcast_to([P, 16, NE]), spread(over_id, NE), ALU.is_le).then_inc(r_dve, 1)
                dve.wait_ge(r_dve, c.next())
                dve.reduce_sum(ex_f[:, :], cmp16, axis=AX_X).then_inc(r_dve, 1)
                dve.wait_ge(r_dve, c.next())
                ts(ex_f[:, :], ex_f[:, :], float(NE - 1), None, ALU.min).then_inc(r_dve, 1)
                dve.wait_ge(r_dve, c.next())
                dve.tensor_copy(expert_i[:, NE:NE + 16], ex_f[:, :])
                c2 = Count(4 * TOPK, layer)
                for k in range(TOPK):
                    for src, dst in ((rank_sb[:, :, :], rank_k),
                                     (over_s[:, :].unsqueeze(1).broadcast_to([P, NT, NE]), ovs_k)):
                        tt(sel[:, :, :], onehot[:, k, :, :], src, ALU.mult).then_inc(r_sel, 1)
                        dve.wait_ge(r_sel, c2.next())
                        dve.reduce_sum(dst[:, k * NT:(k + 1) * NT], sel[:, :, :], axis=AX_X).then_inc(r_sel, 1)
                        dve.wait_ge(r_sel, c2.next())
                ef = ef_all[:, :, :].rearrange("p k t -> p (k t)")
                cmpr = cmp_s[:, 0:16 * 7].rearrange("p (t s) -> p t s", s=7)
                tt(cmpr, spread(rank_k[:, :], 7), steps[:, 0:7].unsqueeze(1).broadcast_to([P, 16, 7]), ALU.is_ge).then_inc(r_dve, 1)
                dve.wait_ge(r_dve, c.next())
                dve.reduce_sum(q_k[:, :], cmpr, axis=AX_X).then_inc(r_dve, 1)
                dve.wait_ge(r_dve, c.next())
                ts(ge_k[:, :], q_k[:, :], 1.0, None, ALU.is_ge)
                tt(blk_k[:, :], q_k[:, :], ovs_k[:, :], ALU.add).then_inc(r_dve, 1)
                dve.wait_ge(r_dve, c.next())
                stt(row_k[:, :], q_k[:, :], -float(P), rank_k[:, :], ALU.mult, ALU.add)
                stt(blk_k[:, :], blk_k[:, :], float(NE - 1), ef, ALU.add, ALU.subtract).then_inc(r_dve, 1)
                dve.wait_ge(r_dve, c.next())
                tt(blk_k[:, :], blk_k[:, :], ge_k[:, :], ALU.mult).then_inc(r_dve, 1)
                dve.wait_ge(r_dve, c.next())
                tt(blk_k[:, :], blk_k[:, :], ef, ALU.add).then_inc(r_dve, 1)
                dve.wait_ge(r_dve, c.next())
                stt(rank_k[:, :], blk_k[:, :], float(P), row_k[:, :], ALU.mult, ALU.add).then_inc(r_dve, 1)
                dve.wait_ge(r_dve, c.next())
                dve.tensor_copy(dest_u[:, :], rank_k[:, :]).then_inc(r_dve, 1)
                dve.wait_ge(r_dve, c.next())
                c.close()
                for n in range(TOPK * NT):
                    t = n % NT
                    dve.wait_ge(r_idx, layer * 16 + n + 1)
                    ts(oh_row[n % 2][:, :], iota_r, row_k[:, n:n + 1], None, ALU.is_equal)
                    ts(oh_blk[n % 2][:, :], blk_iota, blk_k[:, n:n + 1], tok_id[:, t:t + 1], ALU.is_equal, ALU.mult)\
                        .then_inc(r_oh, 1)
                c = Count(5, layer)
                dve.wait_ge(r_exp, layer + 1)
                ts(gates[:, 0:NT], exp_g[:, :], 1.0, None, ALU.add).then_inc(r_gates, 1)
                dve.wait_ge(r_gates, c.next())
                tt(gates[:, 0:NT], gates[:, 0:NT], sum_all[:, :], ALU.mult).then_inc(r_gates, 1)
                dve.wait_ge(r_gates, c.next())
                dve.reciprocal(gates[:, 0:NT], gates[:, 0:NT]).then_inc(r_gates, 1)
                dve.wait_ge(r_gates, c.next())
                tt(gates[:, NT:2 * NT], gates[:, 0:NT], exp_g[:, :], ALU.mult).then_inc(r_gates, 1)
                dve.wait_ge(r_gates, c.next())
                dve.wait_ge(r_idx, layer * 16 + 18)
                dve.tensor_copy(slot_tok[:, :], bank(4)[:, 0:NBLK + 1]).then_inc(r_gates, 1)
                dve.wait_ge(r_gates, c.next())
                c.close()
                dve.tensor_copy(next_gb[:, ds(layer + 1, 1)], gb_f[:, :]).then_inc(r_plan, 1)
                next_phase(dve, DVE_E, layer, PH_C)

                steady(dve)
                nb2 = dve.value_load(plan[0:1, 0:1], min_val=NE - 2, max_val=NBLK - 2)
                nb = nb2 + 2
                gb = dve.value_load(plan[0:1, 1:2], min_val=0, max_val=DEPTH * NBLK)

                def lo(s, turns):
                    dve.wait_ge(d_hi, gb * 6 + turns * 6 + s + 1)
                    tt(ring_lo[:, s % 3, :], ring_raw[:, s % 6, :], ring_hi[:, s % 3, :], ALU.subtract)\
                        .then_inc(d_lo, 1)

                def x_lo(b):
                    for i, (hi_s, lo_s) in enumerate(((d_xhi0, d_xlo0), (d_xhi1, d_xlo1))):
                        dve.wait_ge(hi_s, gb + b + 1)
                        tt(xg_lo[:, 4 * i:4 * i + 4, :], grouped(bank(i), 4), xg_hi[:, 4 * i:4 * i + 4, :], ALU.subtract)\
                            .then_inc(lo_s, 1)

                def g_mul(b, chunks):
                    dve.wait_ge(d_silu, gb + b + 2)
                    dve.wait_ge(d_mm, gb * 6 + chunks + 3)
                    dve.wait_ge(d_tg, gb + b + 1)
                    tt(gate_sb[:, :], bank(4), silu_sb[:, :], ALU.mult).then_inc(d_gm, 1)

                def g_lo(b):
                    dve.wait_ge(d_ghi, gb + b + 1)
                    tt(gT_lo[:, :, :], grouped(bank(2), 4), gT_hi[:, :, :], ALU.subtract).then_inc(d_glo, 1)

                x_lo(0)
                for s in range(4):
                    lo(s, 0)
                g_mul(0, 4)
                x_lo(1)
                for s in (4, 5):
                    lo(s, 0)
                g_lo(0)
                for s in (6, 7, 8, 9):
                    lo(s, 0)

                def turn(b):
                    g_mul(b - 1, (b - 2) * 6 + 8)
                    x_lo(b)
                    lo(10, b - 2)
                    lo(11, b - 2)
                    g_lo(b - 1)
                    for s in (12, 13, 14, 15):
                        lo(s, b - 2)

                steady(dve)
                with dve.Fori(2, NE) as b:
                    turn(b)
                steady(dve)
                with dve.Fori(NE, NBLK) as b:
                    with dve.If(b < nb):
                        turn(b)
                g_mul(nb2 + 1, (nb2) * 6 + 8)
                g_lo(nb2 + 1)
                for s in (10, 11):
                    lo(s, nb2)
                next_phase(dve, DVE_E, layer, PH_D)

                dve.wait_ge(e_par_in, 32 * (layer + 1))

                def front(t, j, pair):
                    dve.wait_ge(e_yg[j], (layer * (NT // 2) + pair + 1) * 32)
                    stt(h_t(t), yg[j][0][:, :], gates[:, ds(t, 1)], h_t(t), ALU.mult, ALU.add).then_inc(e_dve, 1)
                    dve.wait_ge(e_dve, it(t) + 1)
                    stt(h_t(t), yg[j][1][:, :], gates[:, ds(t + NT, 1)], h_t(t), ALU.mult, ALU.add)\
                        .then_inc(e_comb, 1)
                    dve.wait_ge(f_rstd, ft(2, t) + 1)
                    stt(xn[j][:, :], h_t(t), rstd_x[:, j:j + 1], g_ple_sb[:, :], ALU.mult, ALU.mult)\
                        .then_inc(f_xn, 1)
                    dve.wait_ge(f_tp1, ft(2, t) + 1)
                    dve.tensor_copy(xT[j][:, 4:8, :], grouped(bank(1), 4)).then_inc(f_ev1, 1)

                def gate(t):
                    for i, (g, b_) in enumerate(((e_g0, e_b0), (e_g1, e_b1))):
                        dve.wait_ge(g, it(t) + 1)
                        tt(gs[:, i * 512:(i + 1) * 512], bank(2 + i), b_gate_sb[:, i * 512:(i + 1) * 512], ALU.add)\
                            .then_inc(b_, 1)

                def finish(t):
                    dve.wait_ge(e_sg, it(t) + 1)
                    dve.wait_ge(e_pl, it(t) + 1)
                    tt(gs[:, :], bank(4, 2), gs[:, :], ALU.mult).then_inc(e_fin, 1)
                    dve.wait_ge(e_fin, it(t) + 1)
                    tt(h_t(t), h_t(t), gs[:, :], ALU.add).then_inc(e_h, 1)
                    dve.wait_ge(e_h, it(t) + 2)

                def turn(t, j, first, last, pair=None):
                    if first:
                        front(0, 0, 0)
                    if not last:
                        front(t + 1, 1 - j, pair)
                    gate(t)
                    finish(t)

                turn(0, 0, True, False, 0)
                steady(dve)
                with dve.Fori(0, NT // 2 - 1) as i:
                    turn(i * 2 + 1, 1, False, False, i + 1)
                    turn(i * 2 + 2, 0, False, False, i + 1)
                turn(NT - 1, 1, False, True)
                next_phase(dve, DVE_E, layer, PH_E)

        @block.tensor
        def _(pe):
            credit(pe, 1, a_tc, a_s, c_f1, d_tx, d_tg)
            credit(pe, 2, r_idx, e_tpp)
            credit(pe, 3, d_mm)
            credit(pe, PT_BACK, b_pt)
            pe.wait_ge(consts_in, 16)
            mm = pe.matmul

            def transposes(dst, src, n0, n, raises, rows=P):
                for i in range(n):
                    last = pe.transpose(dst[:, i * P:(i + 1) * P], src[:, (n0 + i) * P:(n0 + i + 1) * P], ident)
                last.then_inc(raises, 1)

            def product(dst, lhs, rhs, kn, raises=None):
                for k in range(kn):
                    last = mm(dst, lhs(k), rhs(k), start=(k == 0), stop=(k == kn - 1))
                if raises:
                    last.then_inc(raises, 1)

            with pe.Fori(0, DEPTH) as layer:
                it = lambda t: layer * NT + t
                ft = lambda phase, t: (layer * 3 + phase) * NT + t
                pe.wait_ge(ab_in, 16 * AB_LOADS * (layer + 1))
                for i in range(2):
                    for g in range(4 * i, 4 * i + 4):
                        src = ws_nat[g // 6][:, g % 6 * P:(g % 6 + 1) * P]
                        last = pe.transpose(bank(i)[:, (g - 4 * i) * P:(g - 4 * i + 1) * P], src, ident)
                    last.then_inc(ws_t, 1)
                next_phase(pe, PE_E, layer, PH_WS)

                def front(t, j):
                    pe.wait_ge(f_xn, ft(0, t) + 2)
                    pe.wait_ge(f_ev0, ft(0, t) + 1)
                    transposes(bank(0), xn[j], 0, 4, f_tp0)
                    pe.wait_ge(f_ev1, ft(0, t) + 1)
                    transposes(bank(1), xn[j], 4, 4, f_tp1)

                def turn(t, j, first, last):
                    if first:
                        front(0, 0)
                        pe.wait_ge(w_in_in, 16 * (layer + 1))
                    pe.wait_ge(f_ev0, ft(0, t) + 2)
                    pe.wait_ge(f_ev1, ft(0, t) + 2)
                    pe.wait_ge(a_gv, it(t) + 1)
                    lhs = lambda k: xT[j][:, k, :]
                    product(bank(4), lhs, lambda k: w_in_sb[:, k, V0:IN_W], KD, a_mv)
                    if not last:
                        front(t + 1, 1 - j)
                    pe.wait_ge(a_cn, it(t) + 1)
                    product(bank(2)[:, 0:W_C], lhs, lambda k: w_in_sb[:, k, 0:W_C], KD, a_mc)
                    pe.wait_ge(a_gu, it(t) + 1)
                    product(bank(3), lhs, lambda k: w_in_sb[:, k, U0:V0], KD, a_mu)
                    pe.wait_ge(a_cn, it(t) + 2)
                    pe.wait_ge(a_ce, it(t) + 1)
                    transposes(bank(5), cn, 0, 3, a_tc)
                    pe.wait_ge(a_vn, it(t) + 1)
                    pe.wait_ge(a_m, it(t) + 1)
                    for g in range(GROUPS):
                        last_mm = mm(bank(6)[:, g * GDIM:(g + 1) * GDIM], wsT[:, g, :], vn[:, g * GDIM:(g + 1) * GDIM],
                                     start=True, stop=True)
                    last_mm.then_inc(a_s, 1)

                over_tiles(pe, turn)
                next_phase(pe, PE_E, layer, PH_A)

                def project(hd, n, first=False):
                    if n > 0:
                        pe.wait_ge(b_pev, it(hd) * 4 + n)
                    elif not first:
                        pe.wait_ge(b_tev_a, it(hd) * 2)
                    for i in range(4):
                        cols = slice((4 * (n % 2) + i) * P, (4 * (n % 2) + i + 1) * P)
                        if n < 2:
                            for k in range(2):
                                last = mm(bank(0)[:, i * QK:(i + 1) * QK], cT[:, k, cols],
                                          w_uq_sb[:, k, ds(hd * QK, QK)], start=(k == 0), stop=(k == 1))
                        else:
                            last = mm(bank(0)[:, i * P:(i + 1) * P], cT[:, 2, cols],
                                      w_ukv_sb[:, ds(hd * P, P)], start=True, stop=True)
                    last.then_inc(b_proj, 1)

                def transpose_qk(hd, n):
                    if n == 0:
                        pe.wait_ge(b_pev, it(hd) * 4 + 4)
                        pe.wait_ge(b_qk, it(hd) * 2 + 2)
                    if n == 1:
                        pe.wait_ge(b_qk, it(hd) * 2 + 3)
                        pe.wait_ge(b_tev_d, it(hd) * 2 + 1)
                    if n == 2:
                        pe.wait_ge(b_tev_d, it(hd) * 2 + 2)
                    if n == 3:
                        pe.wait_ge(b_tev_a, it(hd) * 2 + 1)
                    for i in range(4):
                        last = pe.transpose(bank(0)[0:QK, i * P:(i + 1) * P],
                                            qkb[:, n % 2, 4 * (n // 2) + i, :], ident)
                    last.then_inc(b_t, 1)

                def scores(hd, j, i):
                    if i == 0:
                        pe.wait_ge(b_tev_d, it(hd) * 2 + 2)
                    if i == 4:
                        pe.wait_ge(b_tev_a, it(hd) * 2 + 2)
                    pe.wait_ge(b_exp, it(hd) * 8 + i + 1)
                    w = (i + 1) * P
                    for c0_ in range(0, w, BANK):
                        n = min(BANK, w - c0_)
                        last = mm(bank(2 + 2 * (i % 2), 2)[:, c0_:c0_ + n], qkT[j][:, 0, i * P:(i + 1) * P],
                                  qkT[j][:, 1, c0_:c0_ + n], start=True, stop=True)
                    last.then_inc(b_s, 1)

                def weigh(hd, j, i, g):
                    if g % 2 == 0:
                        pe.wait_ge(b_pte_a, it(hd) * 6 + g // 2 + 2)
                    else:
                        pe.wait_ge(b_pte_d, it(hd) * 6 + g // 2 + 2)
                    if g == 0:
                        pe.wait_ge(b_o, it(hd) + 1)
                    k0 = 4 * (g - GROUP_OF[i])
                    for k in range(k0, k0 + GROUP_N[g]):
                        last = mm(bank(7)[:, i * VDIM:(i + 1) * VDIM], probT[g % 2][:, k - k0, :], v_sb[j][:, k, :],
                                  start=(k == 0), stop=(k == i))
                    if g == N_PT - 1:
                        last.then_inc(b_pv, 1)

                def turn(hd, j, first, last):
                    if first:
                        for n in range(4):
                            project(0, n, True)
                        for n in range(4):
                            transpose_qk(0, n)
                        scores(0, 0, 0)
                        scores(0, 0, 1)
                    before_g = None
                    for i in range(NT):
                        pe.wait_ge(b_exp, it(hd) * 8 + i + 3)
                        for g in range(GROUP_OF[i], GROUP_OF[i + 1]):
                            if g % 2 == 0:
                                pe.wait_ge(b_pte_a, it(hd) * 6 + g // 2 + 1)
                            else:
                                pe.wait_ge(b_pte_d, it(hd) * 6 + g // 2 + 1)
                            transposes(bank(1 if g % 2 == 0 else 6), prob[i % 2], 4 * (g - GROUP_OF[i]), GROUP_N[g],
                                       b_pt)
                            if before_g:
                                weigh(hd, j, *before_g)
                            before_g = (i, g)
                            if not last and g == GROUP_OF[6]:
                                transpose_qk(hd + 1, 1)
                            if not last and g == GROUP_OF[7]:
                                transpose_qk(hd + 1, 2)
                        if i + 2 < NT:
                            scores(hd, j, i + 2)
                        elif not last:
                            scores(hd + 1, 1 - j, i + 2 - NT)
                        if not last:
                            if i < 4:
                                project(hd + 1, i)
                            if i == 5:
                                transpose_qk(hd + 1, 0)
                            if i == 7:
                                transpose_qk(hd + 1, 3)
                    weigh(hd, j, *before_g)

                over_tiles(pe, turn)
                next_phase(pe, PE_E, layer, PH_B)

                def front(t, j):
                    pe.wait_ge(f_xn, ft(1, t) + 2)
                    pe.wait_ge(f_ev0, ft(1, t) + 1)
                    transposes(bank(0), xn[j], 0, 4, f_tp0)
                    pe.wait_ge(f_ev1, ft(1, t) + 1)
                    transposes(bank(1), xn[j], 4, 4, f_tp1)

                def tail_t(t):
                    pe.wait_ge(c_xf, it(t) + 1)
                    pe.wait_ge(c_fe0, it(t) + 1)
                    transposes(bank(4), xf, 0, 4, c_f0)
                    pe.wait_ge(c_fe1, it(t) + 1)
                    transposes(bank(5), xf, 4, 4, c_f1)

                def router(t):
                    pe.wait_ge(c_fe0, it(t) + 2)
                    pe.wait_ge(c_fe1, it(t) + 2)
                    pe.wait_ge(c_lge, it(t) + 1)
                    product(bank(6)[:, 0:NROUTE], lambda k: xfT[:, k, :], lambda k: w_router[:, k, :], KD, c_rt)

                def turn(t, j, first, last):
                    if first:
                        pe.wait_ge(wout_in, 16 * (layer + 1))
                        front(0, 0)
                    lhs = lambda k: xT[j][:, k, :]
                    pe.wait_ge(f_ev0, ft(1, t) + 2)
                    pe.wait_ge(f_ev1, ft(1, t) + 2)
                    pe.wait_ge(c_h0, it(t) + 1)
                    product(bank(2), lhs, lambda k: w_out_sb[:, k, 0:512], KD, c_y0)
                    if not first:
                        tail_t(t - 1)
                    if not last:
                        front(t + 1, 1 - j)
                    pe.wait_ge(c_h1, it(t) + 1)
                    product(bank(3), lhs, lambda k: w_out_sb[:, k, 512:1024], KD, c_y1)
                    if not first:
                        router(t - 1)
                    if last:
                        tail_t(t)
                        router(t)

                over_tiles(pe, turn)
                pe.wait_ge(r_gap, layer + 1)
                for t in range(NT):
                    dst = bank(0)[:, t * NE:(t + 1) * NE]
                    mm(dst, before, chosen[:, t, :], start=True, stop=False)
                    mm(dst, ones, picks[:, t, :], start=False, stop=True)
                mm(bank(1)[:, 0:NE], ones, picks[:, NT, :], start=True, stop=True).then_inc(r_rank, 1)
                pe.wait_ge(r_ovt, layer + 1)
                pe.transpose(bank(2)[0:NE, 0:P], over_e[:, :], ident).then_inc(r_ovsb, 1)
                pe.wait_ge(r_ovs, layer + 1)
                mm(bank(3)[:, 0:NE], overT[:, :], before[0:NE, 0:NE], start=True, stop=True).then_inc(r_ovsb, 1)
                for n in range(TOPK * NT):
                    pe.wait_ge(r_oh, layer * 16 + n + 1)
                    mm(bank(4)[:, 0:NBLK + 1], oh_row[n % 2][:, :], oh_blk[n % 2][:, :],
                       start=(n == 0), stop=(n == TOPK * NT - 1)).then_inc(r_idx, 1)
                next_phase(pe, PE_E, layer, PH_C)

                steady(pe)
                nb2 = pe.value_load(plan[0:1, 0:1], min_val=NE - 2, max_val=NBLK - 2)
                nb = nb2 + 2
                gb = pe.value_load(plan[0:1, 1:2], min_val=0, max_val=DEPTH * NBLK)

                def x_t(b):
                    pe.wait_ge(d_xg, (gb + b + 1) * 16)
                    pe.wait_ge(d_xlo0, gb + b + 1)
                    pe.wait_ge(d_xlo1, gb + b + 1)
                    for i in range(KD):
                        last = pe.transpose(ps[:, i * P:(i + 1) * P], xg[:, i * P:(i + 1) * P], ident)
                    last.then_inc(d_tx, 1)

                def split_mm(dst, x_hi, x_lo, w_hi, w_lo, start, stop):
                    mm(dst, x_hi, w_hi, start=start, stop=False)
                    mm(dst, x_hi, w_lo, start=False, stop=False)
                    return mm(dst, x_lo, w_hi, start=False, stop=stop)

                def up(s, turns, dst):
                    pe.wait_ge(d_lo, gb * 6 + turns * 6 + s + 7)
                    part = s % 2
                    for k in range(4):
                        w = slice(k * FE, (k + 1) * FE)
                        last = split_mm(dst, xg_hi[:, 4 * part + k, :], xg_lo[:, 4 * part + k, :],
                                        ring_hi[:, s % 3, w], ring_lo[:, s % 3, w], part == 0 and k == 0,
                                        part == 1 and k == 3)
                    last.then_inc(d_mm, 1)

                def ups(b, s, turns):
                    pe.wait_ge(d_xlo0, gb + b + 2)
                    pe.wait_ge(d_xlo1, gb + b + 2)
                    pe.wait_ge(d_silu, gb + b + 1)
                    up(s, turns, bank(3))
                    up(s + 1, turns, bank(3))
                    pe.wait_ge(d_gm, gb + b + 1)
                    up(s + 2, turns, bank(4))
                    up(s + 3, turns, bank(4))

                def down(b, s, turns):
                    pe.wait_ge(d_glo, gb + b + 2)
                    pe.wait_ge(d_yev, gb + b + 1)
                    for part in range(2):
                        pe.wait_ge(d_lo, gb * 6 + turns * 6 + s + part + 7)
                        for k in range(2):
                            for i in range(2):
                                w = slice(k * D + i * 512, k * D + (i + 1) * 512)
                                last = split_mm(bank(5 + i), gT_hi[:, 2 * part + k, :], gT_lo[:, 2 * part + k, :],
                                                ring_hi[:, (s + part) % 3, w], ring_lo[:, (s + part) % 3, w],
                                                part == 0 and k == 0, part == 1 and k == 1)
                        last.then_inc(d_mm, 1)

                def g_t(b):
                    pe.wait_ge(d_gm, gb + b + 2)
                    pe.wait_ge(d_glo, gb + b + 1)
                    transposes(bank(2), gate_sb, 0, 4, d_tg)

                x_t(0)
                ups(0, 0, 0)
                x_t(1)
                g_t(0)
                ups(1, 4, 0)

                def turn(b):
                    x_t(b)
                    down(b - 2, 8, b - 2)
                    g_t(b - 1)
                    ups(b, 10, b - 2)

                steady(pe)
                with pe.Fori(2, NE) as b:
                    turn(b)
                steady(pe)
                with pe.Fori(NE, NBLK) as b:
                    with pe.If(b < nb):
                        turn(b)
                down(nb2, 8, nb2)
                g_t(nb2 + 1)
                down(nb2 + 1, 10, nb2)
                next_phase(pe, PE_E, layer, PH_D)

                def front(t, j, pair):
                    pe.wait_ge(f_xn, ft(2, t) + 2)
                    pe.wait_ge(f_ev0, ft(2, t) + 1)
                    transposes(bank(0), xn[j], 0, 4, f_tp0)
                    pe.wait_ge(f_ev1, ft(2, t) + 1)
                    transposes(bank(1), xn[j], 4, 4, f_tp1)
                    pe.wait_ge(p_in[j], (layer * (NT // 2) + pair + 1) * 16)
                    pe.wait_ge(e_evp, it(t) + 1)
                    transposes(bank(6), p_sb[j], 0, 2, e_tpp)

                def turn(t, j, first, last, pair=None):
                    if first:
                        pe.wait_ge(ple_w_in, 32 * (layer + 1))
                        front(0, 0, 0)
                    lhs = lambda k: xT[j][:, k, :]
                    pe.wait_ge(f_ev0, ft(2, t) + 2)
                    pe.wait_ge(f_ev1, ft(2, t) + 2)
                    pe.wait_ge(e_evp, it(t) + 2)
                    pe.wait_ge(e_b0, it(t) + 1)
                    product(bank(2), lhs, lambda k: w_gate_sb[:, k, 0:512], KD, e_g0)
                    pe.wait_ge(e_b1, it(t) + 1)
                    product(bank(3), lhs, lambda k: w_gate_sb[:, k, 512:1024], KD, e_g1)
                    if not last:
                        front(t + 1, 1 - j, pair)
                    pe.wait_ge(e_h, it(t) + 1)
                    for i in range(2):
                        product(bank(4 + i), lambda k: pT[j][:, k, :], lambda k: w_ple_sb[:, k, i * 512:(i + 1) * 512], 2,
                                e_pl if i == 1 else None)

                turn(0, 0, True, False, 0)
                steady(pe)
                with pe.Fori(0, NT // 2 - 1) as i:
                    turn(i * 2 + 1, 1, False, False, i + 1)
                    turn(i * 2 + 2, 0, False, False, i + 1)
                turn(NT - 1, 1, False, True)
                next_phase(pe, PE_E, layer, PH_E)


_INS = ["x", "p", "g_mix_norm", "w_in", "g_cq", "g_ckv", "w_uq", "w_ukv", "g_qn", "g_kn", "g_v", "w_s", "b_s",
        "g_out_mla", "g_out_gmlp", "w_out", "g_ffn_norm", "w_router_group", "w_router_expert",
        "w1", "w3", "w2", "g_ple", "w_ple_gate", "b_ple_gate", "w_ple"]


def shape_constants(seq):
    import numpy as np

    f = np.float32
    part = np.arange(P, dtype=f)
    inv = (f(10000.0) ** (-np.arange(0, ROPE, 2, dtype=f) / f(ROPE))).astype(f)
    ang = (np.arange(seq, dtype=f)[:, None] * inv[None, :]).astype(f)
    tiled = lambda a: np.concatenate([a, a], axis=1).reshape(seq // P, P, ROPE).transpose(1, 0, 2).reshape(P, -1)
    row = lambda a: np.broadcast_to(np.asarray(a, f), (P, len(a)))
    return np.ascontiguousarray(np.concatenate([
        np.eye(P, dtype=f),
        (part[:, None] < part[None, :]).astype(f),
        np.ones((P, P), f),
        tiled(np.cos(ang)), tiled(np.sin(ang)),
        row(part),
        row(P * np.arange(NE)),
        row(P * np.arange(1, 9)),
        np.stack([P * t + part for t in range(8)], axis=1),
        row(np.arange(16)),
    ], axis=1).astype(f))


def kernel(**inputs):
    import numpy as _np
    import concourse.bacc as _bacc
    from concourse import mybir as _mybir
    from concourse.bass_utils import run_bass_kernel_spmd as _run

    nc = _bacc.Bacc("TRN2", target_bir_lowering=False, num_devices=1)
    arrays, args = {}, []
    for name in _INS:
        a = _np.ascontiguousarray(inputs[name])
        arrays[f"in_{name}"] = a
        args.append(nc.dram_tensor(f"in_{name}", a.shape, _mybir.dt.from_np(a.dtype), kind="ExternalInput").ap())
    shape = inputs["x"].shape
    a = shape_constants(shape[1])
    arrays["shape_consts"] = a
    args.append(nc.dram_tensor("shape_consts", a.shape, _mybir.dt.float32, kind="ExternalInput").ap())
    args.append(nc.dram_tensor("out_0", shape, _mybir.dt.float32, kind="ExternalOutput").ap())
    hybrid_trunk(nc, *args)
    r = _run(nc, [arrays], core_ids=[0])
    return r.results[0]["out_0"]
```

```python
from contextlib import ExitStack

import concourse.bass as bass
from concourse import mybir

P = 128
BANK = 512
F32 = mybir.dt.float32
F32R = mybir.dt.float32r
I32 = mybir.dt.int32
U32 = mybir.dt.uint32
ALU = mybir.AluOpType
ACT = mybir.ActivationFunctionType
AX_X = mybir.AxisListType.X
ds = bass.ds

EPS = 1e-6
NEG = -3.0e38
HEADS, NOPE, ROPE, VDIM = 8, 64, 32, 64
QK = NOPE + ROPE
Q_RANK, KV_RANK = 256, 128
GROUPS, GDIM = 8, 64
CHUNK = 64
NG, PER_G, NE, TOPK = 4, 8, 32, 2
FE = 512
PLE = 256
CONSTS = 4 * P + 8 * ROPE * 2 + 32 + 8 + 8 + 16


class Count:

    def __init__(self, per, turn):
        self.per, self.base, self.n = per, turn * per, 0

    def next(self):
        self.n += 1
        return self.base + self.n

    def close(self):
        assert self.n == self.per, (self.n, self.per)


def hybrid_trunk(nc, x, p, g_mix_norm, w_in, g_cq, g_ckv, w_uq, w_ukv, g_qn, g_kn, g_v, w_s, b_s,
                 g_out_mla, g_out_gmlp, w_out, g_ffn_norm, w_router_group, w_router_expert,
                 w1, w3, w2, g_ple, w_ple_gate, b_ple_gate, w_ple, shape_consts, out):
    DEPTH, D, IN_W = w_in.shape
    SEQ = x.shape[1]
    NT = SEQ // P
    KD = D // P
    KF = FE // P
    MIXW = HEADS * VDIM
    CQKV = Q_RANK + KV_RANK
    W_C = CQKV + ROPE
    U0, V0 = W_C, W_C + GROUPS * GDIM
    MAX_OVER = (TOPK * SEQ - 1) // P
    NBLK = NE + MAX_OVER
    NROUTE = NG + NE
    SCALE = float(QK) ** -0.5
    GROUP_OF = [0]
    GROUP_N = []
    for i in range(NT):
        GROUP_N += [min(4, i + 1 - g) for g in range(0, i + 1, 4)]
        GROUP_OF.append(len(GROUP_N))
    N_PT, PT_BACK = len(GROUP_N), 3
    K_DVE = 5
    PHASES = 6
    PH_WS, PH_A, PH_B, PH_C, PH_D, PH_E = range(PHASES)

    with ExitStack() as ctx:
        sem = lambda name: ctx.enter_context(nc.semaphore(name))

        arena = ctx.enter_context(nc.sbuf_tensor("arena", [P, 212832 // 4], F32))
        ARENA0 = 16512

        def at(name, shape, dt, offset):
            size = 4
            for n in shape[1:]:
                size *= n
            assert offset + size <= 212832, (name, offset, size)
            return nc.alloc_sbuf_tensor_at(name, shape, dt, offset=ARENA0 + offset)

        K = 1024
        h = at("h", [P, NT * D], F32, 0)
        RAW = NT * D * 4
        ring_raw = at("ring_raw", [P, 6, 2048], F32, RAW)
        w_in_sb = at("w_in_sb", [P, KD, IN_W], F32, RAW)
        w_out_sb = at("w_out_sb", [P, KD, D], F32, RAW)
        g_out_sb = at("g_out_sb", [P, D], F32, RAW + 32 * K)
        g_ffn_sb = at("g_ffn_sb", [P, D], F32, RAW + 36 * K)
        w_router = at("w_router", [P, KD, NROUTE], F32, RAW + 40 * K)
        R = RAW + 48 * K
        ring_hi = at("ring_hi", [P, 3, 2048], F32R, R)
        ring_lo = at("ring_lo", [P, 3, 2048], F32R, R + 24 * K)
        xg = at("xg", [P, D], F32, R + 48 * K)
        xg_hi = at("xg_hi", [P, KD, P], F32R, R + 52 * K)
        xg_lo = at("xg_lo", [P, KD, P], F32R, R + 56 * K)
        silu_sb = at("silu_sb", [P, FE], F32, R + 60 * K)
        gate_sb = at("gate_sb", [P, FE], F32, R + 62 * K)
        gT_hi = at("gT_hi", [P, KF, P], F32R, R + 64 * K)
        gT_lo = at("gT_lo", [P, KF, P], F32R, R + 66 * K)
        y_sb = at("y_sb", [P, D], F32, R + 68 * K)
        w_gate_sb = at("w_gate_sb", [P, KD, D], F32, R + 76 * K)
        w_out_hi = at("w_out_hi", [P, KD, D], F32R, R + 28 * K)
        w_out_lo = at("w_out_lo", [P, KD, D], F32R, RAW)
        w_gate_hi = at("w_gate_hi", [P, KD, D], F32R, RAW)
        w_gate_lo = at("w_gate_lo", [P, KD, D], F32R, R + 76 * K)
        w_ple_sb = at("w_ple_sb", [P, 2, D], F32, R + 108 * K)
        xT = [at(f"xT{j}", [P, KD, P], F32, R + 4 * K * j) for j in range(2)]
        xt_hi = [at(f"xt_hi{j}", [P, KD, P], F32R, R + 4 * K * j) for j in range(2)]
        xc_lo = [at(f"xc_lo{j}", [P, KD, P], F32R, R + (72 + 4 * j) * K) for j in range(2)]
        xe_lo = [at(f"xe_lo{j}", [P, KD, P], F32R, RAW + (32 + 4 * j) * K) for j in range(2)]
        xn = [at(f"xn{j}", [P, D], F32, R + (8 + 4 * j) * K) for j in range(2)]
        junk = at("junk", [P, D], F32, R + 16 * K)
        gv_sb = at("gv_sb", [P, 512], F32, R + 20 * K)
        gu_sb = at("gu_sb", [P, 512], F32, R + 22 * K)
        vsq = at("vsq", [P, 512], F32, R + 24 * K)
        vn = at("vn", [P, 512], F32, R + 26 * K)
        vn1 = at("vn1", [P, 512], F32, R + 28 * K)
        s_sb = at("s_sb", [P, 512], F32, R + 30 * K)
        cn = at("cn", [P, CQKV], F32, R + 32 * K)
        junk_c = at("junk_c", [P, CQKV], F32, R + 34 * K)
        ws_nat = [at("ws_nat0", [P, 6 * P], F32, RAW + 45 * K), at("ws_nat1", [P, 2 * P], F32, R + 116 * K)]
        g_mix_sb = at("g_mix_sb", [P, D], F32, R + 48 * K)
        g_c_sb = at("g_c_sb", [P, CQKV], F32, R + 52 * K)
        g_v_sb = at("g_v_sb", [P, 512], F32, R + 54 * K)
        g_qk_sb = at("g_qk_sb", [P, 2, QK], F32, R + 56 * K)
        bs_sb = at("bs_sb", [P, GROUPS], F32, R + 57 * K)
        w_uq_sb = at("w_uq_sb", [P, 2, HEADS * QK], F32, R + 58 * K)
        w_ukv_sb = at("w_ukv_sb", [P, HEADS * P], F32, R + 64 * K)
        wsT = at("wsT", [P, GROUPS, P], F32, R + 68 * K)
        kr_all = at("kr_all", [P, NT, ROPE], F32, R + 72 * K)
        cT = at("cT", [P, 3, SEQ], F32, R + 73 * K)
        m_all = at("m_all", [P, NT * 512], F32, R + 85 * K)
        a_all = at("a_all", [P, NT, MIXW], F32, R + 101 * K)
        qkb = at("qkb", [P, 2, NT, QK], F32, R)
        qksq = at("qksq", [P, 2, NT, QK], F32, R + 6 * K)
        rope_c, rope_s, kr_c, kr_rot = (at(n, [P, NT, ROPE], F32, R + (12 + i) * K)
                                        for i, n in enumerate(("rope_c", "rope_s", "kr_c", "kr_rot")))
        kr_s = at("kr_s", [P, NT, ROPE], F32, R + 46 * K)
        qkT = [at(f"qkT{j}", [QK, 2, SEQ], F32, R + (16 + 8 * j) * K) for j in range(2)]
        v_sb = [at(f"v_sb{j}", [P, NT, VDIM], F32, R + (32 + 2 * j) * K) for j in range(2)]
        prob = [at(f"prob{j}", [P, SEQ], F32, R + (36 + 4 * j) * K) for j in range(2)]
        probT = [at(f"probT{j}", [P, 4, P], F32, R + (44 + 2 * j) * K) for j in range(2)]
        xf = at("xf", [P, D], F32, R + 20 * K)
        xfT = at("xfT", [P, KD, P], F32, R + 24 * K)
        yg = [[at(f"yg{j}{k}", [P, D], F32, R + (20 + 8 * j + 4 * k) * K) for k in range(2)] for j in range(2)]
        g_ple_sb = at("g_ple_sb", [P, D], F32, R + 36 * K)
        b_gate_sb = at("b_gate_sb", [P, D], F32, R + 40 * K)
        gs = at("gs", [P, D], F32, R + 44 * K)
        p_sb = [at(f"p_sb{j}", [P, PLE], F32, R + (72 + j) * K) for j in range(2)]
        pT = [at(f"pT{j}", [P, 2, P], F32, R + (74 + j) * K) for j in range(2)]

        S0 = R + 117 * K
        off = [S0]

        def small(name, shape, dt=F32):
            n = 4
            for d in shape[1:]:
                n *= d
            off[0] += -off[0] % 32
            o = off[0]
            off[0] += n
            return at(name, shape, dt, o)

        consts = small("consts", [P, CONSTS])
        c0 = [0]

        def const(n):
            a = c0[0]
            c0[0] += n
            return consts[:, a:a + n]

        ident = const(P)
        before = const(P)
        ones = const(P)
        cos2 = const(8 * ROPE).rearrange("p (t r) -> p t r", t=8)
        sin2 = const(8 * ROPE).rearrange("p (t r) -> p t r", t=8)
        iota_r = const(P)
        iota_e = iota_r[:, 0:NE]
        block_e = const(NE)
        steps = const(8)
        tok_id = const(8)
        over_id = const(16)
        assert c0[0] == CONSTS

        half = small("half", [P, 16])
        stat_x = small("stat_x", [P, 2])
        rstd_x = small("rstd_x", [P, 2])
        stat_c = small("stat_c", [P, 2])
        rstd_c = small("rstd_c", [P, 2])
        stat_v = small("stat_v", [P, GROUPS])
        rstd_v = small("rstd_v", [P, GROUPS])
        tmp_p = small("tmp_p", [P, 16])
        stat_qk = small("stat_qk", [P, 16])
        rstd_qk = small("rstd_qk", [P, 16])
        row_max = small("row_max", [P, 2])
        neg_max = small("neg_max", [P, 2])
        row_sum = small("row_sum", [P, 2 * NT])
        ss_kr = small("ss_kr", [P, NT])
        row_inv = small("row_inv", [P, NT])
        stat_f = small("stat_f", [P, 1])
        rstd_f = small("rstd_f", [P, 1])
        lg8 = small("lg8", [P, 8])
        le = small("le", [P, NE])
        top8 = small("top8", [P, 8])
        gi8 = small("gi8", [P, 8], U32)
        gf = small("gf", [P, 1])
        lgm = small("lgm", [P, NG])
        lge = small("lge", [P, NG])
        gmask = small("gmask", [P, NG])
        gbias = small("gbias", [P, NG])
        top8e = small("top8e", [P, 8])
        ei8 = small("ei8", [P, 8], U32)
        sum_all = small("sum_all", [P, NT])
        gap_all = small("gap_all", [P, NT])
        ef_all = small("ef_all", [P, TOPK, NT])
        picks = small("picks", [P, NT + 1, NE])
        rank_k = small("rank_k", [P, TOPK * NT])
        ovs_k = small("ovs_k", [P, TOPK * NT])
        q_k = small("q_k", [P, TOPK * NT])
        ge_k = small("ge_k", [P, TOPK * NT])
        blk_k = small("blk_k", [P, TOPK * NT])
        row_k = small("row_k", [P, TOPK * NT])
        dest_u = small("dest_u", [P, TOPK * NT], U32)
        over_e = small("over_e", [P, NE])
        over_s = small("over_s", [P, NE])
        over_end = small("over_end", [P, NE])
        nb_f = small("nb_f", [P, 1])
        nb2_f = small("nb2_f", [P, 1])
        gb_f = small("gb_f", [P, 1])
        plan = small("plan", [P, 2], I32)
        next_gb = small("next_gb", [P, DEPTH + 1], I32)
        expert_i = small("expert_i", [P, NE + 16], I32)
        ex_f = small("ex_f", [P, 16])
        gates = small("gates", [P, TOPK * NT])
        exp_g = small("exp_g", [P, NT])
        slot_tok = small("slot_tok", [P, NBLK + 1], U32)
        idx_x = small("idx_x", [P, 1], U32)
        idx_y = [[small(f"idx_y{j}{k}", [P, 1], U32) for k in range(2)] for j in range(2)]
        cmp_s = at("cmp_s", [P, NE * 16], F32, R + 68 * K)
        oh_row = at("oh_row", [P, TOPK * NT, P], F32R, R + 72 * K)
        oh_blk = at("oh_blk", [P, TOPK * NT, NBLK + 1], F32R, R + 80 * K)
        oh_cmp = at("oh_cmp", [P, TOPK * NT, NBLK + 1], F32, R + 48 * K)
        onehot = at("onehot", [P, TOPK, NT, NE], F32, R + 62 * K)
        chosen = at("chosen", [P, NT, NE], F32, R + 64 * K)
        overT = at("overT", [NE, P], F32, R + 70 * K)
        sel = at("sel", [P, TOPK, NT, NE], F32, R + 66 * K)
        blk_iota = iota_r[:, 0:NBLK + 1]

        ps = ctx.enter_context(nc.psum_tensor("ps", [P, 8 * BANK], F32))

        def bank(b, n=1):
            return ps[:, b * BANK:(b + n) * BANK]

        xn_rows = nc.dram_tensor("xn_rows", (SEQ, D), F32, kind="Internal").ap()
        y_rows = nc.dram_tensor("y_rows", (NBLK * P, D), F32, kind="Internal").ap()
        x_v = x.rearrange("b (t p) d -> p (b t) d", p=P)
        out_v = out.rearrange("b (t p) d -> p (b t) d", p=P)
        p_v = p.rearrange("l b (t p) d -> (l b t) p d", p=P)
        w_in_v = w_in.rearrange("l (k p) n -> l p k n", p=P)
        w_out_v = w_out.rearrange("l (k p) n -> l p k n", p=P)
        w_gate_v = w_ple_gate.rearrange("l (k p) n -> l p k n", p=P)
        w_ple_v = w_ple.rearrange("l (k p) n -> l p k n", p=P)
        w_uq_v = w_uq.rearrange("l (k p) n -> l p k n", p=P)
        w_rg_v = w_router_group.rearrange("l (k p) n -> l p k n", p=P)
        w_re_v = w_router_expert.rearrange("l (k p) n -> l p k n", p=P)
        w_s_v = w_s.rearrange("l g t j -> l t g j")
        b_s_v = b_s.rearrange("l g t -> l t g")
        g_v_v = g_v.rearrange("l g c -> l (g c)")
        w1_v = w1.rearrange("l e (k p) f -> (l e) p k f", p=P)
        w3_v = w3.rearrange("l e (k p) f -> (l e) p k f", p=P)
        w2_v = w2.rearrange("l e (k p) d -> (l e) p k d", p=P)
        xn_v = xn_rows.rearrange("(t p) d -> t p d", p=P)
        y_v = y_rows.rearrange("(b p) d -> b p d", p=P)

        consts_in = sem("consts_in")
        x_in = [sem(f"x_in{i}") for i in range(3)]
        g_mix_in, ws_in, a_par_in, b_par_in = sem("g_mix_in"), sem("ws_in"), sem("a_par_in"), sem("b_par_in")
        w_in_v_in, w_in_c_in, w_in_u_in = sem("w_in_v_in"), sem("w_in_c_in"), sem("w_in_u_in")
        wout_in, cpar_in = sem("wout_in"), sem("cpar_in")
        ple_w_in, e_par_in, out_done = sem("ple_w_in"), sem("e_par_in"), sem("out_done")
        p_in = [sem(f"p_in{j}") for j in range(2)]
        raw_in = [sem(f"raw_in{s}") for s in range(6)]
        ACT_E, DVE_E, PE_E, POOL_E = "act", "dve", "pe", "pool"
        done = {e: sem(f"phase_done_{e}") for e in (ACT_E, DVE_E, PE_E, POOL_E)}
        half_set, y_filled = sem("half_set"), sem("y_filled")
        f_stat, f_pool, f_rstd, f_xn = sem("f_stat"), sem("f_pool"), sem("f_rstd"), sem("f_xn")
        f_tp0, f_tp1, f_ev0, f_ev1 = sem("f_tp0"), sem("f_tp1"), sem("f_ev0"), sem("f_ev1")
        f_hi0, f_hi1 = sem("f_hi0"), sem("f_hi1")
        c_whi, c_wlo, e_whi, e_wlo = sem("c_whi"), sem("c_wlo"), sem("e_whi"), sem("e_wlo")
        c_wlo_p, e_wlo_p = sem("c_wlo_p"), sem("e_wlo_p")
        a_mv, a_mc, a_mu = sem("a_mv"), sem("a_mc"), sem("a_mu")
        a_gv, a_gu, a_csq, a_rc = sem("a_gv"), sem("a_gu"), sem("a_csq"), sem("a_rc")
        a_v2, a_rv, a_cn, a_vn, a_m = sem("a_v2"), sem("a_rv"), sem("a_cn"), sem("a_vn"), sem("a_m")
        a_tc, a_ce, a_s = sem("a_tc"), sem("a_ce"), sem("a_s")
        a_pool_c, a_pool_v, a_dve = sem("a_pool_c"), sem("a_pool_v"), sem("a_dve")
        ws_t, ws_e, ws_dve = sem("ws_t"), sem("ws_e"), sem("ws_dve")
        b_proj, b_sq, b_pev, b_ss, b_rs, b_rp, b_qk = (sem(n) for n in
                                                       ("b_proj", "b_sq", "b_pev", "b_ss", "b_rs", "b_rp", "b_qk"))
        b_kr, b_sum, b_rot = sem("b_kr"), sem("b_sum"), sem("b_rot")
        b_t, b_tev_a, b_tev_d = sem("b_t"), sem("b_tev_a"), sem("b_tev_d")
        b_s, b_max, b_exp = sem("b_s"), sem("b_max"), sem("b_exp")
        b_pt, b_pte_a, b_pte_d = sem("b_pt"), sem("b_pte_a"), sem("b_pte_d")
        b_pv, b_o = sem("b_pv"), sem("b_o")
        b_dve, b_pool, b_max_c = (sem(n) for n in ("b_dve", "b_pool", "b_max_c"))
        c_y0, c_y1, c_h0, c_h1 = sem("c_y0"), sem("c_y1"), sem("c_h0"), sem("c_h1")
        c_sf, c_rf, c_xf, c_xst = sem("c_sf"), sem("c_rf"), sem("c_xf"), sem("c_xst")
        c_f0, c_f1, c_fe0, c_fe1 = sem("c_f0"), sem("c_f1"), sem("c_fe0"), sem("c_fe1")
        c_rt, c_lgm, c_lge = sem("c_rt"), sem("c_lgm"), sem("c_lge")
        c_pool2, c_dve, c_dve2 = sem("c_pool2"), sem("c_dve"), sem("c_dve2")
        r_rank, r_dve, r_ovt, r_ovsb, r_ovs, r_exp, r_gap = (sem("r_rank"), sem("r_dve"), sem("r_ovt"), sem("r_ovsb"),
                                                     sem("r_ovs"), sem("r_exp"), sem("r_gap"))
        r_oh, r_idx = sem("r_oh"), sem("r_idx")
        r_plan, r_over = sem("r_plan"), sem("r_over")
        d_idx, d_xg = sem("d_idx"), sem("d_xg")
        d_tx, d_xhi0, d_xhi1, d_xlo0, d_xlo1 = sem("d_tx"), sem("d_xhi0"), sem("d_xhi1"), sem("d_xlo0"), sem("d_xlo1")
        d_hi, d_lo, d_mm = sem("d_hi"), sem("d_lo"), sem("d_mm")
        d_silu, d_gm, d_tg, d_ghi, d_glo = sem("d_silu"), sem("d_gm"), sem("d_tg"), sem("d_ghi"), sem("d_glo")
        d_yev, d_yst = sem("d_yev"), sem("d_yst")
        e_idx, e_yg = sem("e_idx"), [sem(f"e_yg{j}") for j in range(2)]
        e_comb = sem("e_comb")
        e_tpp, e_evp = sem("e_tpp"), sem("e_evp")
        e_g0, e_g1, e_pl = sem("e_g0"), sem("e_g1"), sem("e_pl")
        e_b0, e_b1, e_sg, e_h = sem("e_b0"), sem("e_b1"), sem("e_sg"), sem("e_h")
        e_dve, e_fin = sem("e_dve"), sem("e_fin")
        r_gates, r_sel = sem("r_gates"), sem("r_sel")

        def steady(eng):
            eng.nop(nofuse=True)

        def next_phase(eng, me, layer, phase):
            steady(eng)
            eng.drain().then_inc(done[me], 1)
            for other in done:
                eng.wait_ge(done[other], layer * PHASES + phase + 1)

        def over_tiles(eng, turn):
            turn(0, 0, True, False)
            steady(eng)
            with eng.Fori(0, NT // 2 - 1) as i:
                turn(i * 2 + 1, 1, False, False)
                turn(i * 2 + 2, 0, False, False)
            turn(NT - 1, 1, False, True)

        def credit(eng, n, *signals):
            for s in signals:
                eng.sem_inc(s, n)

        def grouped(ap, g):
            return ap.rearrange("p (g c) -> p g c", g=g)

        def spread(ap, n):
            return ap.unsqueeze(2).broadcast_to([ap.shape[0], ap.shape[1], n])

        block = ctx.enter_context(nc.Block())

        @block.sync
        def _(sp):
            def load_mix(layer):
                sp.dma_start(g_mix_sb[:, :], g_mix_norm[ds(layer, 1)].broadcast_to([P, D])).then_inc(g_mix_in, 16)
                for dst, g0, g1 in ((ws_nat[0], 0, 6), (ws_nat[1], 6, GROUPS)):
                    sp.dma_start(grouped(dst[:, :], g1 - g0),
                                 w_s_v[ds(layer, 1)][:, :, g0:g1, :].rearrange("o t g j -> t (o g) j"))\
                        .then_inc(ws_in, 16)

            def load_w_in(layer, a, b, signal):
                sp.dma_start(w_in_sb[:, :, a:b],
                             w_in_v[:, :, :, a:b][ds(layer, 1)].rearrange("o p k n -> p (o k) n"))\
                                 .then_inc(signal, 16)

            def load_a(layer):
                one = lambda v: v[ds(layer, 1)]
                sp.dma_start(g_c_sb[:, 0:Q_RANK], one(g_cq).broadcast_to([P, Q_RANK])).then_inc(a_par_in, 16)
                sp.dma_start(g_c_sb[:, Q_RANK:CQKV], one(g_ckv).broadcast_to([P, KV_RANK])).then_inc(a_par_in, 16)
                sp.dma_start(g_v_sb[:, :], one(g_v_v).broadcast_to([P, 512])).then_inc(a_par_in, 16)
                sp.dma_start(bs_sb[:, :], one(b_s_v).rearrange("o t g -> (o t) g"),
                             allow_slow_non_contiguous=True).then_inc(a_par_in, 16)

            def load_b(layer):
                one = lambda v: v[ds(layer, 1)]
                sp.dma_start(g_qk_sb[:, 0, :], one(g_qn).broadcast_to([P, QK])).then_inc(b_par_in, 16)
                sp.dma_start(g_qk_sb[:, 1, :], one(g_kn).broadcast_to([P, QK])).then_inc(b_par_in, 16)
                sp.dma_start(w_uq_sb[:, :, :], one(w_uq_v).rearrange("o p k n -> p (o k) n")).then_inc(b_par_in, 16)
                sp.dma_start(w_ukv_sb[:, :], one(w_ukv).rearrange("o p n -> (o p) n")).then_inc(b_par_in, 16)

            def chunk(layer, expert, which, part, slot):
                if which == 2:
                    src = w2_v[ds(layer * NE + expert, 1)][:, :, 2 * part:2 * part + 2, :]
                    dst = ring_raw[:, slot, :].rearrange("p (k n) -> p k n", k=2)
                else:
                    src = (w1_v if which == 1 else w3_v)[ds(layer * NE + expert, 1)][:, :, 4 * part:4 * part + 4, :]
                    dst = ring_raw[:, slot, :].rearrange("p (k n) -> p k n", k=4)
                sp.dma_start(dst, src.rearrange("o p k n -> p (o k) n")).then_inc(raw_in[slot], 16)

            sp.sem_inc(c_xst, 16)
            sp.dma_start(consts[:, :], shape_consts).then_inc(consts_in, 16)
            def load_x(t):
                sp.dma_start(h[:, t * D:(t + 1) * D], x_v[:, t, :]).then_inc(x_in[min(t, 2)], 16)

            load_x(0)
            load_mix(0)
            load_w_in(0, V0, IN_W, w_in_v_in)
            load_x(1)
            load_w_in(0, 0, W_C, w_in_c_in)
            load_a(0)
            load_w_in(0, U0, V0, w_in_u_in)
            for t in range(2, NT):
                load_x(t)
            load_b(0)
            x_rows = x.rearrange("b s d -> (b s) d")
            for row in range(NE * P, NBLK * P, SEQ):
                n = min(SEQ, NBLK * P - row)
                sp.dma_start(y_rows[row:row + n, :], x_rows[0:n, :]).then_inc(y_filled, 16)
            with sp.Fori(0, DEPTH) as layer:
                ph = lambda e, phase: sp.wait_ge(done[e], layer * PHASES + phase + 1)
                ph(PE_E, PH_A)
                one = lambda v: v[ds(layer, 1)]
                sp.dma_start(w_out_sb[:, :, :], one(w_out_v).rearrange("o p k n -> p (o k) n")).then_inc(wout_in, 16)
                sp.dma_start(g_out_sb[:, 0:MIXW], one(g_out_mla).broadcast_to([P, MIXW])).then_inc(cpar_in, 16)
                sp.dma_start(g_out_sb[:, MIXW:D], one(g_out_gmlp).broadcast_to([P, MIXW])).then_inc(cpar_in, 16)
                sp.dma_start(g_ffn_sb[:, :], one(g_ffn_norm).broadcast_to([P, D])).then_inc(cpar_in, 16)
                sp.dma_start(w_router[:, :, 0:NG], one(w_rg_v).rearrange("o p k n -> p (o k) n"))\
                    .then_inc(cpar_in, 16)
                sp.dma_start(w_router[:, :, NG:NROUTE], one(w_re_v).rearrange("o p k n -> p (o k) n"))\
                    .then_inc(cpar_in, 16)
                steady(sp)
                with sp.Fori(0, NT) as t:
                    sp.wait_ge(c_xf, layer * NT + t + 1)
                    sp.dma_start(xn_v[ds(t, 1)].rearrange("o p d -> (o p) d"), xf[:, :]).then_inc(c_xst, 16)
                sp.wait_ge(c_y1, (layer + 1) * NT)
                steady(sp)
                before_here = sp.value_load(next_gb[0:1, ds(layer, 1)], min_val=0, max_val=DEPTH * NBLK)
                n = [0]

                def stream(expert, which, part, turn):
                    s = n[0]
                    n[0] += 1
                    sp.wait_ge(d_lo, before_here * 6 + turn * 6 + s + 1)
                    chunk(layer, expert, which, part, s % 6)

                def load_w_gate(k):
                    sp.dma_start(w_gate_sb[:, k:k + 2, :],
                                 w_gate_v[:, :, k:k + 2, :][ds(layer, 1)].rearrange("o p k n -> p (o k) n"))\
                        .then_inc(ple_w_in, 16)

                for b in range(2):
                    for which in (1, 3):
                        for part in range(2):
                            if n[0] == 4:
                                sp.wait_ge(c_rt, (layer + 1) * NT)
                                steady(sp)
                            if n[0] == 6:
                                sp.dma_start(w_ple_sb[:, :, :], one(w_ple_v).rearrange("o p k n -> p (o k) n"))\
                                    .then_inc(ple_w_in, 16)
                                load_w_gate(2)
                                load_w_gate(4)
                            stream(b, which, part, 0)

                load_w_gate(6)
                sp.wait_ge(r_plan, layer + 1)
                load_w_gate(0)

                def turn(b, before_last, this):
                    n[0] = 8
                    for part in range(2):
                        stream(before_last, 2, part, b - 2)
                    for which in (1, 3):
                        for part in range(2):
                            stream(this, which, part, b - 2)

                steady(sp)
                with sp.Fori(2, NE) as b:
                    turn(b, b - 2, b)
                sp.wait_ge(r_over, layer + 1)
                steady(sp)
                nb2 = sp.value_load(plan[0:1, 0:1], min_val=NE - 2, max_val=NBLK - 2)
                nb = nb2 + 2
                expert_of = lambda b: sp.value_load(expert_i[0:1, ds(b, 1)], min_val=0, max_val=NE - 1)
                steady(sp)
                with sp.Fori(NE, NBLK) as b:
                    with sp.If(b < nb):
                        steady(sp)
                        turn(b, expert_of(b - 2), expert_of(b))
                n[0] = 8
                for back in (2, 1):
                    steady(sp)
                    e = expert_of(nb2 + 2 - back)
                    for part in range(2):
                        stream(e, 2, part, nb2)
                for e in (PE_E, DVE_E, ACT_E):
                    ph(e, PH_D)
                sp.dma_start(g_ple_sb[:, :], one(g_ple).broadcast_to([P, D])).then_inc(e_par_in, 16)
                sp.dma_start(b_gate_sb[:, :], one(b_ple_gate).broadcast_to([P, D])).then_inc(e_par_in, 16)

                def load_p(t, j):
                    sp.wait_ge(e_tpp, layer * NT + t + 1)
                    sp.dma_start(p_sb[j][:, :], p_v[ds(layer * NT + t, 1)].rearrange("o p d -> (o p) d"))\
                      .then_inc(p_in[j], 16)

                load_p(0, 0)
                load_p(1, 1)
                steady(sp)
                with sp.Fori(1, NT // 2) as i:
                    load_p(i * 2, 0)
                    load_p(i * 2 + 1, 1)
                with sp.If(layer < DEPTH - 1):
                    after = nc.s_assert_within(layer + 1, min_val=1, max_val=DEPTH - 1,
                                               skip_runtime_bounds_check_because="only where layer < DEPTH - 1")
                    load_mix(after)
                    load_a(after)
                    load_b(after)
                    sp.wait_ge(e_g1, (layer + 1) * NT)
                    load_w_in(after, V0, IN_W, w_in_v_in)
                    load_w_in(after, 0, W_C, w_in_c_in)
                    load_w_in(after, U0, V0, w_in_u_in)
            for t in range(NT):
                sp.wait_ge(e_h, (DEPTH - 1) * NT + t + 2)
                sp.dma_start(out_v[:, t, :], h[:, t * D:(t + 1) * D]).then_inc(out_done, 16)
            sp.wait_ge(out_done, 16 * NT)

        @block.gpsimd
        def _(pool):
            def rsqrt(out_ap, in_ap, scale, order, done, raises):
                n = in_ap.shape[1]
                steady(pool)
                pool.tensor_scalar(tmp_p[:, 0:n], in_ap, scale, EPS, ALU.mult, ALU.add).then_inc(order, 1)
                pool.wait_ge(order, done)
                pool.tensor_tensor(out_ap, tmp_p[:, 0:n], half[:, 0:n], ALU.pow).then_inc(raises, 1)

            pool.memset(half[:, :], -0.5).then_inc(half_set, 1)
            pool.wait_ge(half_set, 1)
            pool.wait_ge(consts_in, 16)
            def w_lower(dst, src, hi, hi_done, lo_done, layer):
                for k in range(K_DVE, KD):
                    pool.wait_ge(hi_done, layer * KD + k + 1)
                    pool.tensor_tensor(dst[:, k, :], src[:, k, :], hi[:, k, :], ALU.subtract).then_inc(lo_done, 1)

            steady(pool)
            with pool.Fori(0, DEPTH) as layer:
                it = lambda t: layer * NT + t
                ft = lambda phase, t: (layer * 3 + phase) * NT + t
                next_phase(pool, POOL_E, layer, PH_WS)

                def rstd_x_of(t, j):
                    pool.wait_ge(f_stat, ft(0, t) + 1)
                    rsqrt(rstd_x[:, j:j + 1], stat_x[:, j:j + 1], 1.0, f_pool, ft(0, t) + 1, f_rstd)
                    pool.wait_ge(f_rstd, ft(0, t) + 1)

                def turn(t, j, first, last):
                    if first:
                        rstd_x_of(0, 0)
                    if not last:
                        rstd_x_of(t + 1, 1 - j)
                    pool.wait_ge(a_csq, it(t) + 1)
                    rsqrt(rstd_c[:, :], stat_c[:, :], 1.0, a_pool_c, it(t) + 1, a_rc)
                    pool.wait_ge(a_rc, it(t) + 1)
                    pool.wait_ge(a_v2, it(t) + 1)
                    rsqrt(rstd_v[:, :], stat_v[:, :], 1.0 / GDIM, a_pool_v, it(t) + 1, a_rv)
                    pool.wait_ge(a_rv, it(t) + 1)

                over_tiles(pool, turn)
                next_phase(pool, POOL_E, layer, PH_A)

                def normalise(hd):
                    steady(pool)
                    pool.wait_ge(b_pev, it(hd) * 4 + 2)
                    pool.wait_ge(b_qk, it(hd) * 2 + 1)
                    steady(pool)
                    pool.tensor_tensor(rope_c[:, :, :], qkb[:, 0, :, NOPE:QK], cos2, ALU.mult)
                    pool.tensor_tensor(rope_s[:, :, :], qkb[:, 0, :, NOPE:QK], sin2, ALU.mult).then_inc(b_rp, 1)
                    for i in range(2):
                        pool.wait_ge(b_ss, it(hd) * 2 + i + 1)
                        v = slice(i * NT, (i + 1) * NT)
                        rsqrt(rstd_qk[:, v], stat_qk[:, v], 1.0, b_pool, it(hd) * 2 + i + 1, b_rs)
                        pool.wait_ge(b_rs, it(hd) * 2 + i + 1)

                def turn(hd, j, first, last):
                    if first:
                        normalise(0)
                    if not last:
                        normalise(hd + 1)

                over_tiles(pool, turn)
                next_phase(pool, POOL_E, layer, PH_B)

                def rstd_c_of(t):
                    pool.wait_ge(f_stat, ft(1, t) + 1)
                    rsqrt(rstd_c[:, :], stat_c[:, :], 1.0, f_pool, ft(1, t) + 1, f_rstd)
                    pool.wait_ge(f_rstd, ft(1, t) + 1)

                def turn(t, j, first, last):
                    if first:
                        rstd_c_of(0)
                        w_lower(w_out_lo, w_out_sb, w_out_hi, c_whi, c_wlo_p, layer)
                    if not last:
                        rstd_c_of(t + 1)
                    pool.wait_ge(c_sf, it(t) + 2)
                    rsqrt(rstd_f[:, :], stat_f[:, :], 1.0, c_pool2, it(t) + 1, c_rf)
                    pool.wait_ge(c_rf, it(t) + 1)

                over_tiles(pool, turn)
                steady(pool)
                pool.drain().then_inc(done[POOL_E], 1)

                pool.wait_ge(c_xst, (layer * NT + NT + 1) * 16)
                pool.wait_ge(r_plan, layer + 1)
                steady(pool)
                nb2 = pool.value_load(plan[0:1, 0:1], min_val=NE - 2, max_val=NBLK - 2)
                nb = nb2 + 2
                gb = pool.value_load(plan[0:1, 1:2], min_val=0, max_val=DEPTH * NBLK)

                def gather(b):
                    pool.wait_ge(d_tx, gb + b + 1)
                    steady(pool)
                    pool.tensor_copy(idx_x[:, :], slot_tok[:, ds(b, 1)]).then_inc(d_idx, 1)
                    pool.wait_ge(d_idx, gb + b + 1)
                    steady(pool)
                    pool.indirect_dma_start(xg[:, :], None, xn_rows,
                                            bass.IndirectOffsetOnAxis(ap=idx_x[:, :], axis=0)).then_inc(d_xg, 16)

                steady(pool)
                with pool.Fori(0, NE) as b:
                    gather(b)
                steady(pool)
                with pool.Fori(NE, NBLK) as b:
                    with pool.If(b < nb):
                        gather(b)
                next_phase(pool, POOL_E, layer, PH_D)

                pool.wait_ge(d_yst, (gb + nb + 1) * 16)

                def gather2(t, j):
                    pool.wait_ge(e_comb, it(t) + 1)
                    steady(pool)
                    for k in range(TOPK):
                        pool.tensor_copy(idx_y[j][k][:, :], dest_u[:, ds(t + k * NT, 1)]).then_inc(e_idx, 1)
                    pool.wait_ge(e_idx, (it(t) + 1) * 2)
                    steady(pool)
                    for k in range(TOPK):
                        pool.indirect_dma_start(yg[j][k][:, :], None, y_rows,
                                                bass.IndirectOffsetOnAxis(ap=idx_y[j][k][:, :], axis=0))\
                            .then_inc(e_yg[j], 16)

                def rstd_e(t, j):
                    pool.wait_ge(f_stat, ft(2, t) + 1)
                    rsqrt(rstd_x[:, j:j + 1], stat_x[:, j:j + 1], 1.0, f_pool, ft(2, t) + 1, f_rstd)
                    pool.wait_ge(f_rstd, ft(2, t) + 1)

                def turn(t, j, first, last):
                    if first:
                        gather2(0, 0)
                        w_lower(w_gate_lo, w_gate_sb, w_gate_hi, e_whi, e_wlo_p, layer)
                        rstd_e(0, 0)
                    if not last:
                        gather2(t + 1, 1 - j)
                        rstd_e(t + 1, 1 - j)

                over_tiles(pool, turn)
                next_phase(pool, POOL_E, layer, PH_E)

        @block.scalar
        def _(act):
            credit(act, 1, c_sf, f_ev0, a_gv, a_gu, a_ce, b_pte_a,
                   c_fe0, c_lge, d_silu, d_yev, e_evp)
            credit(act, 2, b_exp)
            act.sem_inc(d_yst, 16)
            act.wait_ge(consts_in, 16)

            def copy(out_ap, in_ap):
                return act.activation(out_ap, in_ap, ACT.Copy)

            def x_upper(dst, done):
                for i, (tp, hi_done) in enumerate(((f_tp0, f_hi0), (f_tp1, f_hi1))):
                    act.wait_ge(tp, done)
                    copy(dst[:, 4 * i:4 * i + 4, :], grouped(bank(i), 4)).then_inc(hi_done, 1)

            def w_upper(dst, src, signal):
                for k in range(KD):
                    copy(dst[:, k, :], src[:, k, :]).then_inc(signal, 1)

            with act.Fori(0, DEPTH) as layer:
                it = lambda t: layer * NT + t
                ft = lambda phase, t: (layer * 3 + phase) * NT + t
                h_t = lambda t: h[:, ds(t * D, D)]
                next_phase(act, ACT_E, layer, PH_WS)

                def front(t, j, loads):
                    x_sem, n = loads
                    act.wait_ge(x_sem, 16 * n)
                    steady(act)
                    act.activation(junk[:, :], h_t(t), ACT.Square, scale=float(D) ** -0.5,
                                   accum_out=stat_x[:, j:j + 1]).then_inc(f_stat, 1)
                    act.wait_ge(f_tp0, ft(0, t) + 1)
                    copy(xT[j][:, 0:4, :], grouped(bank(0), 4)).then_inc(f_ev0, 1)

                def turn(t, j, first, last):
                    if first:
                        front(0, 0, (x_in[0], 1))
                    if not last:
                        front(t + 1, 1 - j, (x_in[1], 1) if first else (x_in[2], NT - 2))
                    act.wait_ge(a_mv, it(t) + 1)
                    act.wait_ge(a_m, it(t) + 1)
                    act.activation(gv_sb[:, :], bank(4), ACT.Gelu_apprx_tanh).then_inc(a_gv, 1)
                    act.wait_ge(a_mc, it(t) + 1)
                    act.activation(junk_c[:, 0:Q_RANK], bank(2)[:, 0:Q_RANK], ACT.Square, scale=float(Q_RANK) ** -0.5,
                                   accum_out=stat_c[:, 0:1])
                    act.activation(junk_c[:, Q_RANK:CQKV], bank(2)[:, Q_RANK:CQKV], ACT.Square,
                                   scale=float(KV_RANK) ** -0.5, accum_out=stat_c[:, 1:2]).then_inc(a_csq, 1)
                    act.wait_ge(a_mu, it(t) + 1)
                    act.activation(gu_sb[:, :], bank(3), ACT.Gelu_apprx_tanh).then_inc(a_gu, 1)
                    act.wait_ge(a_tc, it(t) + 2)
                    steady(act)
                    copy(cT[:, :, ds(t * P, P)], grouped(bank(5)[:, 0:CQKV], 3)).then_inc(a_ce, 1)

                over_tiles(act, turn)
                next_phase(act, ACT_E, layer, PH_A)

                def squares(hd, j, n, first=False):
                    act.wait_ge(b_proj, it(hd) * 4 + n + 1)
                    if not first:
                        act.wait_ge(b_ss, it(hd) * 2)
                    four = slice(4 * (n % 2), 4 * (n % 2) + 4)
                    if n < 2:
                        act.activation(qksq[:, 0, four, :], grouped(bank(0)[:, 0:4 * QK], 4), ACT.Square,
                                       scale=SCALE).then_inc(b_sq, 1)
                    else:
                        kv = grouped(bank(0), 4)
                        act.activation(qksq[:, 1, four, 0:NOPE], kv[:, :, 0:NOPE], ACT.Square, scale=SCALE)
                        copy(v_sb[j][:, four, :], kv[:, :, NOPE:P]).then_inc(b_sq, 1)

                def tr_ev(hd, j, n):
                    act.wait_ge(b_t, it(hd) * 4 + 2 + n + 1)
                    copy(qkT[j][:, n, 512:1024], bank(0)[0:QK, :]).then_inc(b_tev_a, 1)

                def exp_of(hd, j, i):
                    act.wait_ge(b_max, it(hd) * 8 + i + 1)
                    act.wait_ge(b_pt, it(hd) * N_PT + (GROUP_OF[i - 1] if i >= 1 else GROUP_OF[-2] - N_PT) + PT_BACK)
                    w = (i + 1) * P
                    act.activation(prob[i % 2][:, 0:w], bank(2 + 2 * (i % 2), 2)[:, 0:w], ACT.Exp,
                                   bias=neg_max[:, i % 2:i % 2 + 1], scale=SCALE,
                                   accum_out=row_sum[:, j * NT + i:j * NT + i + 1]).then_inc(b_exp, 1)

                def probs_ev(hd, i):
                    for g in range(GROUP_OF[i], GROUP_OF[i + 1]):
                        if g % 2 == 0:
                            n = GROUP_N[g]
                            act.wait_ge(b_pt, it(hd) * N_PT + g + 1 + PT_BACK)
                            copy(probT[g % 2][:, 0:n, :], grouped(bank(1)[:, 0:n * P], n)).then_inc(b_pte_a, 1)

                def turn(hd, j, first, last):
                    if first:
                        for n in range(4):
                            squares(0, 0, n, True)
                        for n in range(2):
                            tr_ev(0, 0, n)
                        exp_of(0, 0, 0)
                    for i in range(NT):
                        probs_ev(hd, i)
                        if i + 1 < NT:
                            exp_of(hd, j, i + 1)
                        elif not last:
                            act.wait_ge(b_o, it(hd) + 1)
                            exp_of(hd + 1, 1 - j, 0)
                        if not last:
                            if i < 4:
                                squares(hd + 1, 1 - j, i)
                            if i >= NT - 2:
                                tr_ev(hd + 1, 1 - j, i - (NT - 2))

                over_tiles(act, turn)
                next_phase(act, ACT_E, layer, PH_B)

                def stats(t):
                    act.wait_ge(f_xn, ft(1, t) + 1)
                    steady(act)
                    act.activation(junk[:, 0:MIXW], a_all[:, ds(t, 1), :].rearrange("p o c -> p (o c)"), ACT.Square,
                                   scale=float(MIXW) ** -0.5, accum_out=stat_c[:, 0:1])
                    act.activation(junk[:, MIXW:D], m_all[:, ds(t * MIXW, MIXW)], ACT.Square,
                                   scale=float(MIXW) ** -0.5, accum_out=stat_c[:, 1:2]).then_inc(f_stat, 1)

                def front(t, j):
                    x_upper(xt_hi[j], ft(1, t) + 1)

                def tail_ev(t):
                    act.wait_ge(c_f0, it(t) + 1)
                    copy(xfT[:, 0:4, :], grouped(bank(4), 4)).then_inc(c_fe0, 1)

                def tail_exp(t):
                    act.wait_ge(c_lgm, it(t) + 1)
                    steady(act)
                    act.activation(lge[:, :], lgm[:, :], ACT.Exp, accum_out=sum_all[:, ds(t, 1)]).then_inc(c_lge, 1)

                def turn(t, j, first, last):
                    if first:
                        stats(0)
                        act.wait_ge(wout_in, 16 * (layer + 1))
                        w_upper(w_out_hi, w_out_sb, c_whi)
                        front(0, 0)
                    if not last:
                        act.wait_ge(c_sf, it(t) + 1)
                        stats(t + 1)
                    if not first:
                        tail_ev(t - 1)
                    if not last:
                        front(t + 1, 1 - j)
                    act.wait_ge(c_h1, it(t) + 2)
                    steady(act)
                    act.activation(junk[:, :], h_t(t), ACT.Square, scale=float(D) ** -0.5,
                                   accum_out=stat_f[:, :]).then_inc(c_sf, 1)
                    if last:
                        tail_ev(t)
                    if not first:
                        tail_exp(t - 1)
                    if last:
                        tail_exp(t)

                over_tiles(act, turn)
                act.wait_ge(r_gap, layer + 1)
                act.activation(exp_g[:, :], gap_all[:, :], ACT.Exp).then_inc(r_exp, 1)
                act.wait_ge(c_rt, (layer + 1) * NT)
                act.wait_ge(c_xst, (layer * NT + NT + 1) * 16)
                steady(act)
                gb = act.value_load(next_gb[0:1, ds(layer, 1)], min_val=0, max_val=DEPTH * NBLK)

                def hi(s, turns):
                    q = s % 6
                    act.wait_ge(raw_in[q], (gb + turns + (s // 6 + 1)) * 16)
                    act.wait_ge(d_mm, gb * 6 + turns * 6 + s + 1)
                    copy(ring_hi[:, s % 3, :], ring_raw[:, q, :]).then_inc(d_hi, 1)

                for s in range(3):
                    hi(s, 0)
                next_phase(act, ACT_E, layer, PH_C)

                steady(act)
                nb2 = act.value_load(plan[0:1, 0:1], min_val=NE - 2, max_val=NBLK - 2)
                nb = nb2 + 2

                def x_hi(b):
                    for i, s in enumerate((d_xhi0, d_xhi1)):
                        act.wait_ge(d_tx, gb + b + 2)
                        copy(xg_hi[:, 4 * i:4 * i + 4, :], grouped(bank(i), 4)).then_inc(s, 1)

                def silu_of(b, chunks):
                    act.wait_ge(d_mm, gb * 6 + chunks + 3)
                    act.wait_ge(d_gm, gb + b + 1)
                    act.activation(silu_sb[:, :], bank(3), ACT.Silu).then_inc(d_silu, 1)

                def g_hi(b):
                    act.wait_ge(d_tg, gb + b + 2)
                    copy(gT_hi[:, :, :], grouped(bank(2), 4)).then_inc(d_ghi, 1)

                def y_out(b, chunks):
                    act.wait_ge(d_mm, gb * 6 + chunks + 3)
                    act.wait_ge(d_yst, (gb + b + 1) * 16)
                    for i in range(2):
                        last = copy(y_sb[:, i * 512:(i + 1) * 512], bank(5 + i))
                    last.then_inc(d_yev, 1)
                    act.wait_ge(d_yev, gb + b + 2)
                    steady(act)
                    act.dma_start(y_v[ds(b, 1)].rearrange("o p d -> (o p) d"), y_sb[:, :]).then_inc(d_yst, 16)

                act.wait_ge(y_filled, 16 * -(-MAX_OVER * P // SEQ))
                x_hi(0)
                hi(3, 0)
                silu_of(0, 2)
                x_hi(1)
                for s in (4, 5):
                    hi(s, 0)
                g_hi(0)
                for s in (6, 7, 8, 9):
                    hi(s, 0)

                def turn(b):
                    silu_of(b - 1, (b - 2) * 6 + 6)
                    x_hi(b)
                    hi(10, b - 2)
                    hi(11, b - 2)
                    y_out(b - 2, (b - 2) * 6 + 10)
                    g_hi(b - 1)
                    for s in (12, 13, 14, 15):
                        hi(s, b - 2)

                steady(act)
                with act.Fori(2, NE) as b:
                    turn(b)
                steady(act)
                with act.Fori(NE, NBLK) as b:
                    with act.If(b < nb):
                        turn(b)
                silu_of(nb2 + 1, nb2 * 6 + 6)
                hi(10, nb2)
                hi(11, nb2)
                g_hi(nb2 + 1)
                y_out(nb2, nb2 * 6 + 10)
                y_out(nb2 + 1, nb2 * 6 + 12)
                next_phase(act, ACT_E, layer, PH_D)

                def p_front(t, j):
                    act.wait_ge(e_tpp, it(t) + 3)
                    copy(pT[j][:, :, :], grouped(bank(6)[:, 0:PLE], 2)).then_inc(e_evp, 1)

                def front(t, j):
                    act.wait_ge(e_comb, it(t) + 3)
                    steady(act)
                    act.activation(junk[:, :], h_t(t), ACT.Square, scale=float(D) ** -0.5,
                                   accum_out=stat_x[:, j:j + 1]).then_inc(f_stat, 1)
                    x_upper(xt_hi[j], ft(2, t) + 1)

                def turn(t, j, first, last):
                    if first:
                        act.wait_ge(ple_w_in, 80 * (layer + 1))
                        w_upper(w_gate_hi, w_gate_sb, e_whi)
                        p_front(0, 0)
                        front(0, 0)
                    if not last:
                        front(t + 1, 1 - j)
                        p_front(t + 1, 1 - j)
                    act.wait_ge(e_b1, it(t) + 2)
                    act.activation(gs[:, :], gs[:, :], ACT.Sigmoid).then_inc(e_sg, 1)

                over_tiles(act, turn)
                next_phase(act, ACT_E, layer, PH_E)

        @block.vector
        def _(dve):
            credit(dve, 1, f_xn, f_ev1, a_cn, a_m, b_pte_d, b_o, c_h0,
                   c_h1, c_fe1, d_xlo0, d_xlo1, d_gm, d_glo, e_b0, e_b1, e_h)
            credit(dve, 1, b_qk)
            credit(dve, 2, e_comb)
            credit(dve, 6, d_lo)
            dve.memset(next_gb[:, :], 0)
            dve.memset(gb_f[:, :], 0.0)
            dve.memset(lg8[:, :], NEG)
            dve.memset(picks[:, 0, :], 0.0)
            dve.wait_ge(consts_in, 16)
            dve.tensor_copy(expert_i[:, 0:NE], iota_e)
            stt = dve.scalar_tensor_tensor
            tt = dve.tensor_tensor
            ts = dve.tensor_scalar

            def x_lower(dst, hi, done):
                for i, (hi_done, ev) in enumerate(((f_hi0, f_ev0), (f_hi1, f_ev1))):
                    v = slice(4 * i, 4 * i + 4)
                    dve.wait_ge(hi_done, done)
                    tt(dst[:, v, :], grouped(bank(i), 4), hi[:, v, :], ALU.subtract).then_inc(ev, 1)

            def w_lower(dst, src, hi, k, hi_done, lo_done, layer):
                dve.wait_ge(hi_done, layer * KD + k + 1)
                tt(dst[:, k, :], src[:, k, :], hi[:, k, :], ALU.subtract).then_inc(lo_done, 1)

            with dve.Fori(0, DEPTH) as layer:
                it = lambda t: layer * NT + t
                ft = lambda phase, t: (layer * 3 + phase) * NT + t
                h_t = lambda t: h[:, ds(t * D, D)]

                c = Count(2, layer)
                for i in range(2):
                    dve.wait_ge(ws_t, layer * 2 + i + 1)
                    dve.tensor_copy(wsT[:, 4 * i:4 * i + 4, :], grouped(bank(i), 4)).then_inc(ws_dve, 1)
                    dve.wait_ge(ws_dve, c.next())
                c.close()
                dve.memset(wsT[CHUNK:P, :, 0:CHUNK], 0.0).then_inc(ws_e, 1)
                dve.wait_ge(g_mix_in, 16 * (layer + 1))
                next_phase(dve, DVE_E, layer, PH_WS)

                def front(t, j):
                    dve.wait_ge(f_rstd, ft(0, t) + 1)
                    stt(xn[j][:, :], h_t(t), rstd_x[:, j:j + 1], g_mix_sb[:, :], ALU.mult, ALU.mult)\
                        .then_inc(f_xn, 1)
                    dve.wait_ge(f_tp1, ft(0, t) + 1)
                    dve.tensor_copy(xT[j][:, 4:8, :], grouped(bank(1), 4)).then_inc(f_ev1, 1)

                def turn(t, j, first, last):
                    if first:
                        front(0, 0)
                    if not last:
                        front(t + 1, 1 - j)
                    c = Count(3, it(t))
                    if first:
                        dve.wait_ge(a_par_in, 16 * 4 * (layer + 1))
                    dve.wait_ge(a_gv, it(t) + 2)
                    tt(vsq[:, :], gv_sb[:, :], gv_sb[:, :], ALU.mult).then_inc(a_dve, 1)
                    dve.wait_ge(a_dve, c.next())
                    dve.reduce_sum(stat_v[:, :], grouped(vsq[:, :], GROUPS), axis=AX_X).then_inc(a_v2, 1)
                    dve.wait_ge(a_rc, it(t) + 1)
                    dve.wait_ge(a_tc, it(t) + 1)
                    stt(cn[:, 0:Q_RANK], bank(2)[:, 0:Q_RANK], rstd_c[:, 0:1], g_c_sb[:, 0:Q_RANK], ALU.mult, ALU.mult)
                    stt(cn[:, Q_RANK:CQKV], bank(2)[:, Q_RANK:CQKV], rstd_c[:, 1:2], g_c_sb[:, Q_RANK:CQKV],
                        ALU.mult, ALU.mult)
                    dve.tensor_copy(kr_all[:, ds(t, 1), :].rearrange("p o r -> p (o r)"), bank(2)[:, CQKV:W_C])\
                        .then_inc(a_cn, 1)
                    dve.wait_ge(a_rv, it(t) + 1)
                    dve.wait_ge(a_s, it(t) + 1)
                    tt(grouped(vn1[:, :], GROUPS), grouped(gv_sb[:, :], GROUPS), spread(rstd_v[:, :], GDIM), ALU.mult)\
                        .then_inc(a_dve, 1)
                    dve.wait_ge(a_dve, c.next())
                    tt(vn[:, :], vn1[:, :], g_v_sb[:, :], ALU.mult).then_inc(a_vn, 1)
                    dve.wait_ge(a_s, it(t) + 2)
                    tt(grouped(s_sb[:, :], GROUPS), grouped(bank(6), GROUPS), spread(bs_sb[:, :], GDIM), ALU.add)\
                        .then_inc(a_dve, 1)
                    dve.wait_ge(a_dve, c.next())
                    c.close()
                    dve.wait_ge(a_gu, it(t) + 2)
                    tt(m_all[:, ds(t * 512, 512)], s_sb[:, :], gu_sb[:, :], ALU.mult).then_inc(a_m, 1)

                over_tiles(dve, turn)
                next_phase(dve, DVE_E, layer, PH_A)

                dve.wait_ge(b_par_in, 16 * 4 * (layer + 1))
                c = Count(6, layer)
                tt(kr_rot[:, :, :], kr_all[:, :, :], kr_all[:, :, :], ALU.mult).then_inc(b_kr, 1)
                dve.wait_ge(b_kr, c.next())
                dve.reduce_sum(ss_kr[:, :], kr_rot[:, :, :], axis=AX_X).then_inc(b_kr, 1)
                dve.wait_ge(b_kr, c.next())
                tt(kr_all[:, :, :], kr_all[:, :, :], g_qk_sb[:, 1:2, NOPE:QK].broadcast_to([P, NT, ROPE]), ALU.mult)\
                    .then_inc(b_kr, 1)
                dve.wait_ge(b_kr, c.next())
                tt(kr_c[:, :, :], kr_all[:, :, :], cos2, ALU.mult).then_inc(b_kr, 1)
                dve.wait_ge(b_kr, c.next())
                tt(kr_s[:, :, :], kr_all[:, :, :], sin2, ALU.mult).then_inc(b_kr, 1)
                dve.wait_ge(b_kr, c.next())
                hf = ROPE // 2
                tt(kr_rot[:, :, 0:hf], kr_c[:, :, 0:hf], kr_s[:, :, hf:ROPE], ALU.subtract)
                tt(kr_rot[:, :, hf:ROPE], kr_c[:, :, hf:ROPE], kr_s[:, :, 0:hf], ALU.add).then_inc(b_kr, 1)
                dve.wait_ge(b_kr, c.next())
                c.close()

                def proj_ev(hd, n, first=False):
                    dve.wait_ge(b_sq, it(hd) * 4 + n + 1)
                    if not first:
                        dve.wait_ge(b_t, it(hd) * 4)
                    four = slice(4 * (n % 2), 4 * (n % 2) + 4)
                    if n < 2:
                        tt(qkb[:, 0, four, :], grouped(bank(0)[:, 0:4 * QK], 4),
                           g_qk_sb[:, 0:1, :].broadcast_to([P, 4, QK]), ALU.mult).then_inc(b_pev, 1)
                    else:
                        tt(qkb[:, 1, four, 0:NOPE], grouped(bank(0), 4)[:, :, 0:NOPE],
                           g_qk_sb[:, 1:2, 0:NOPE].broadcast_to([P, 4, NOPE]), ALU.mult).then_inc(b_pev, 1)

                def sum_q(hd):
                    dve.wait_ge(b_sq, it(hd) * 4 + 2)
                    dve.reduce_sum(stat_qk[:, 0:NT], qksq[:, 0, :, :], axis=AX_X).then_inc(b_ss, 1)

                def sum_k(hd):
                    dve.wait_ge(b_sq, it(hd) * 4 + 4)
                    dve.reduce_sum(stat_qk[:, NT:2 * NT], qksq[:, 1, :, 0:NOPE], axis=AX_X).then_inc(b_sum, 1)
                    dve.wait_ge(b_sum, it(hd) + 1)
                    stt(stat_qk[:, NT:2 * NT], ss_kr[:, :], 1.0 / QK, stat_qk[:, NT:2 * NT], ALU.mult, ALU.add)\
                        .then_inc(b_ss, 1)

                def norm_q(hd):
                    dve.wait_ge(b_rp, it(hd) + 1)
                    dve.wait_ge(b_pev, it(hd) * 4 + 2)
                    tt(qkb[:, 0, :, NOPE:NOPE + hf], rope_c[:, :, 0:hf], rope_s[:, :, hf:ROPE], ALU.subtract)
                    tt(qkb[:, 0, :, NOPE + hf:QK], rope_c[:, :, hf:ROPE], rope_s[:, :, 0:hf], ALU.add)\
                        .then_inc(b_rot, 1)
                    dve.wait_ge(b_rot, it(hd) + 1)
                    dve.wait_ge(b_rs, it(hd) * 2 + 1)
                    tt(qkb[:, 0, :, :], qkb[:, 0, :, :], spread(rstd_qk[:, 0:NT], QK), ALU.mult).then_inc(b_qk, 1)

                def norm_k(hd):
                    dve.wait_ge(b_rs, it(hd) * 2 + 2)
                    dve.wait_ge(b_pev, it(hd) * 4 + 4)
                    r = rstd_qk[:, NT:2 * NT]
                    tt(qkb[:, 1, :, 0:NOPE], qkb[:, 1, :, 0:NOPE], spread(r, NOPE), ALU.mult)
                    tt(qkb[:, 1, :, NOPE:QK], kr_rot[:, :, :], spread(r, ROPE), ALU.mult).then_inc(b_qk, 1)

                def tr_ev(hd, j, n):
                    dve.wait_ge(b_t, it(hd) * 4 + n + 1)
                    dve.tensor_copy(qkT[j][:, n, 0:512], bank(0)[0:QK, :]).then_inc(b_tev_d, 1)

                def max_of(hd, i):
                    w = (i + 1) * P
                    s = bank(2 + 2 * (i % 2), 2)
                    c = Count(2, it(hd) * 8 + i)
                    dve.wait_ge(b_s, it(hd) * 8 + i + 1)
                    dve.memset(s[0:CHUNK, w - CHUNK:w], NEG).then_inc(b_max_c, 1)
                    dve.wait_ge(b_max_c, c.next())
                    dve.reduce_max(row_max[:, i % 2:i % 2 + 1], s[:, 0:w], axis=AX_X).then_inc(b_max_c, 1)
                    dve.wait_ge(b_max_c, c.next())
                    dve.wait_ge(b_exp, it(hd) * 8 + i + 1)
                    ts(neg_max[:, i % 2:i % 2 + 1], row_max[:, i % 2:i % 2 + 1], -SCALE, None, ALU.mult)\
                        .then_inc(b_max, 1)

                def probs_ev(hd, i):
                    for g in range(GROUP_OF[i], GROUP_OF[i + 1]):
                        if g % 2 == 1:
                            n = GROUP_N[g]
                            dve.wait_ge(b_pt, it(hd) * N_PT + g + 1 + PT_BACK)
                            dve.tensor_copy(probT[g % 2][:, 0:n, :], grouped(bank(6)[:, 0:n * P], n))\
                                .then_inc(b_pte_d, 1)

                def turn(hd, j, first, last):
                    if first:
                        proj_ev(0, 0, True)
                        proj_ev(0, 1, True)
                        sum_q(0)
                        proj_ev(0, 2, True)
                        proj_ev(0, 3, True)
                        sum_k(0)
                        norm_q(0)
                        norm_k(0)
                        tr_ev(0, 0, 0)
                        tr_ev(0, 0, 1)
                        max_of(0, 0)
                        max_of(0, 1)
                    for i in range(NT):
                        probs_ev(hd, i)
                        if i + 2 < NT:
                            max_of(hd, i + 2)
                        elif not last:
                            max_of(hd + 1, i + 2 - NT)
                        if not last:
                            if i == 2:
                                sum_q(hd + 1)
                            if i == 3:
                                norm_q(hd + 1)
                            if i < 4:
                                proj_ev(hd + 1, i)
                            if i == 3:
                                sum_k(hd + 1)
                            if i == 4:
                                tr_ev(hd + 1, 1 - j, 0)
                                norm_k(hd + 1)
                            if i == 5:
                                tr_ev(hd + 1, 1 - j, 1)
                    dve.wait_ge(b_exp, it(hd) * 8 + 10)
                    dve.reciprocal(row_inv[:, :], row_sum[:, j * NT:(j + 1) * NT]).then_inc(b_dve, 1)
                    dve.wait_ge(b_dve, it(hd) + 1)
                    dve.wait_ge(b_pv, it(hd) + 1)
                    tt(a_all[:, :, ds(hd * VDIM, VDIM)], grouped(bank(7), NT), spread(row_inv[:, :], VDIM), ALU.mult)\
                        .then_inc(b_o, 1)

                over_tiles(dve, turn)
                dve.wait_ge(cpar_in, 16 * 5 * (layer + 1))
                next_phase(dve, DVE_E, layer, PH_B)

                def cat(t, j):
                    dve.wait_ge(f_rstd, ft(1, t) + 1)
                    stt(xn[j][:, 0:MIXW], a_all[:, ds(t, 1), :].rearrange("p o c -> p (o c)"), rstd_c[:, 0:1],
                        g_out_sb[:, 0:MIXW], ALU.mult, ALU.mult)
                    stt(xn[j][:, MIXW:D], m_all[:, ds(t * MIXW, MIXW)], rstd_c[:, 1:2],
                        g_out_sb[:, MIXW:D], ALU.mult, ALU.mult).then_inc(f_xn, 1)

                def cat_ev(t, j):
                    x_lower(xc_lo[j], xt_hi[j], layer * 2 * NT + t + 1)

                def tail_ev(t):
                    dve.wait_ge(c_f1, it(t) + 2)
                    dve.tensor_copy(xfT[:, 4:8, :], grouped(bank(5), 4)).then_inc(c_fe1, 1)

                def route(t):
                    c = Count(12, it(t))
                    dve.wait_ge(c_rt, it(t) + 1)
                    dve.tensor_copy(le[:, :], bank(6)[:, NG:NROUTE])
                    dve.tensor_copy(lg8[:, 0:NG], bank(6)[:, 0:NG]).then_inc(c_dve, 1)
                    dve.wait_ge(c_dve, c.next())
                    steady(dve)
                    dve.max(top8[:, :], lg8[:, :]).then_inc(c_dve, 1)
                    dve.wait_ge(c_dve, c.next())
                    dve.wait_ge(c_lge, it(t) + 1)
                    ts(lgm[:, :], lg8[:, 0:NG], top8[:, 0:1], None, ALU.subtract).then_inc(c_lgm, 1)
                    dve.max_index(gi8[:, :], top8[:, :], lg8[:, :]).then_inc(c_dve, 1)
                    dve.wait_ge(c_dve, c.next())
                    dve.tensor_copy(gf[:, :], gi8[:, 0:1]).then_inc(c_dve, 1)
                    dve.wait_ge(c_dve, c.next())
                    ts(gmask[:, :], iota_e[:, 0:NG], gf[:, 0:1], None, ALU.is_equal).then_inc(c_dve, 1)
                    dve.wait_ge(c_dve, c.next())
                    ts(gbias[:, :], gmask[:, :], -NEG, NEG, ALU.mult, ALU.add).then_inc(c_dve, 1)
                    dve.wait_ge(c_dve, c.next())
                    tt(grouped(le[:, :], NG), grouped(le[:, :], NG), spread(gmask[:, :], PER_G), ALU.mult)\
                        .then_inc(c_dve, 1)
                    dve.wait_ge(c_dve, c.next())
                    tt(grouped(le[:, :], NG), grouped(le[:, :], NG), spread(gbias[:, :], PER_G), ALU.add)\
                        .then_inc(c_dve, 1)
                    dve.wait_ge(c_dve, c.next())
                    steady(dve)
                    dve.max(top8e[:, :], le[:, :]).then_inc(c_dve, 1)
                    dve.wait_ge(c_dve, c.next())
                    tt(gap_all[:, ds(t, 1)], top8e[:, 1:2], top8e[:, 0:1], ALU.subtract)
                    dve.max_index(ei8[:, :], top8e[:, :], le[:, :]).then_inc(c_dve, 1)
                    dve.wait_ge(c_dve, c.next())
                    for k in range(TOPK):
                        last = dve.tensor_copy(ef_all[:, k, ds(t, 1)], ei8[:, k:k + 1])
                    last.then_inc(c_dve, 1)
                    dve.wait_ge(c_dve, c.next())
                    for k in range(TOPK):
                        last = ts(onehot[:, k, ds(t, 1), :].rearrange("p o e -> p (o e)"), iota_e,
                                  ef_all[:, k, ds(t, 1)], None, ALU.is_equal)
                    last.then_inc(c_dve, 1)
                    dve.wait_ge(c_dve, c.next())
                    c.close()
                    c = Count(2, it(t))
                    one = lambda a: a.rearrange("p o e -> p (o e)")
                    tt(one(chosen[:, ds(t, 1), :]), one(onehot[:, 0, ds(t, 1), :]), one(onehot[:, 1, ds(t, 1), :]),
                              ALU.add).then_inc(c_dve2, 1)
                    dve.wait_ge(c_dve2, c.next())
                    tt(one(picks[:, ds(t + 1, 1), :]), one(picks[:, ds(t, 1), :]), one(chosen[:, ds(t, 1), :]),
                              ALU.add).then_inc(c_dve2, 1)
                    dve.wait_ge(c_dve2, c.next())
                    c.close()

                def turn(t, j, first, last):
                    if first:
                        cat(0, 0)
                        for k in range(K_DVE):
                            if k == 2:
                                cat_ev(0, 0)
                            w_lower(w_out_lo, w_out_sb, w_out_hi, k, c_whi, c_wlo, layer)
                    if not last:
                        cat(t + 1, 1 - j)
                    if not first:
                        tail_ev(t - 1)
                    if not last:
                        cat_ev(t + 1, 1 - j)
                    for i, (y, hs) in enumerate(((c_y0, c_h0), (c_y1, c_h1))):
                        dve.wait_ge(y, it(t) + 1)
                        part = h[:, ds(t * D + i * 512, 512)]
                        tt(part, bank(2 + i), part, ALU.add).then_inc(hs, 1)
                    if not first and not last:
                        route(t - 1)
                    dve.wait_ge(c_rf, it(t) + 1)
                    dve.wait_ge(c_f1, it(t) + 1)
                    dve.wait_ge(c_xst, (it(t) + 1) * 16)
                    stt(xf[:, :], h_t(t), rstd_f[:, 0:1], g_ffn_sb[:, :], ALU.mult, ALU.mult).then_inc(c_xf, 1)
                    if last:
                        tail_ev(t)
                        route(t - 1)
                        route(t)

                over_tiles(dve, turn)

                dve.sem_inc(r_gap, 1)
                R_LINKS = 19
                c = Count(R_LINKS, layer)
                all_k = [P, TOPK, NT, NE]
                by_choice = sel[:, :, :, :].rearrange("p k t e -> p (k t) e")
                dve.wait_ge(r_rank, layer + 1)
                cmp7 = cmp_s[:, 0:NE * 7].rearrange("p (e s) -> p e s", s=7)
                tt(cmp7, spread(bank(1)[:, 0:NE], 7), steps[:, 0:7].unsqueeze(1).broadcast_to([P, NE, 7]),
                   ALU.is_gt).then_inc(r_dve, 1)
                dve.wait_ge(r_dve, c.next())
                dve.reduce_sum(over_e[:, :], cmp7, axis=AX_X).then_inc(r_dve, 1)
                dve.wait_ge(r_dve, c.next())
                dve.sem_inc(r_ovt, 1)
                rank_in = grouped(bank(0)[:, 0:NT * NE], NT).unsqueeze(1).broadcast_to(all_k)
                tt(sel[:, :, :, :], onehot[:, :, :, :], rank_in, ALU.mult).then_inc(r_sel, 1)
                dve.wait_ge(r_ovsb, layer * 2 + 1)
                dve.tensor_copy(overT[:, :], bank(2)[0:NE, 0:P]).then_inc(r_ovs, 1)
                dve.reduce_sum(nb_f[:, :], over_e[:, :], axis=AX_X).then_inc(r_dve, 1)
                dve.wait_ge(r_dve, c.next())
                dve.wait_ge(r_sel, 3 * layer + 1)
                dve.reduce_sum(rank_k[:, :], by_choice, axis=AX_X).then_inc(r_sel, 1)
                ts(nb2_f[:, :], nb_f[:, :], float(NE - 2), None, ALU.add)
                ts(nb_f[:, :], nb_f[:, :], float(NE), None, ALU.add).then_inc(r_dve, 1)
                dve.wait_ge(r_dve, c.next())
                dve.tensor_copy(plan[:, 0:1], nb2_f[:, :])
                dve.tensor_copy(plan[:, 1:2], gb_f[:, :])
                tt(gb_f[:, :], gb_f[:, :], nb_f[:, :], ALU.add).then_inc(r_dve, 1)
                dve.wait_ge(r_dve, c.next())
                dve.wait_ge(r_ovsb, layer * 2 + 2)
                dve.tensor_copy(over_s[:, :], bank(3)[:, 0:NE]).then_inc(r_dve, 1)
                dve.wait_ge(r_dve, c.next())
                dve.wait_ge(r_sel, 3 * layer + 2)
                tt(sel[:, :, :, :], onehot[:, :, :, :],
                   over_s[:, :].unsqueeze(1).unsqueeze(1).broadcast_to(all_k), ALU.mult).then_inc(r_sel, 1)
                ef = ef_all[:, :, :].rearrange("p k t -> p (k t)")
                cmpr = cmp_s[:, 0:16 * 7].rearrange("p (t s) -> p t s", s=7)
                tt(cmpr, spread(rank_k[:, :], 7), steps[:, 0:7].unsqueeze(1).broadcast_to([P, 16, 7]),
                   ALU.is_ge).then_inc(r_dve, 1)
                dve.wait_ge(r_dve, c.next())
                dve.reduce_sum(q_k[:, :], cmpr, axis=AX_X).then_inc(r_dve, 1)
                dve.wait_ge(r_dve, c.next())
                dve.wait_ge(r_sel, 3 * layer + 3)
                dve.reduce_sum(ovs_k[:, :], by_choice, axis=AX_X)
                ts(ge_k[:, :], q_k[:, :], 1.0, None, ALU.is_ge)
                stt(row_k[:, :], q_k[:, :], -float(P), rank_k[:, :], ALU.mult, ALU.add).then_inc(r_dve, 1)
                dve.wait_ge(r_dve, c.next())
                tt(blk_k[:, :], q_k[:, :], ovs_k[:, :], ALU.add).then_inc(r_dve, 1)
                dve.wait_ge(r_dve, c.next())
                stt(blk_k[:, :], blk_k[:, :], float(NE - 1), ef, ALU.add, ALU.subtract).then_inc(r_dve, 1)
                dve.wait_ge(r_dve, c.next())
                tt(blk_k[:, :], blk_k[:, :], ge_k[:, :], ALU.mult).then_inc(r_dve, 1)
                dve.wait_ge(r_dve, c.next())
                tt(blk_k[:, :], blk_k[:, :], ef, ALU.add).then_inc(r_dve, 1)
                dve.wait_ge(r_dve, c.next())
                tt(oh_cmp[:, :, :], blk_iota.unsqueeze(1).broadcast_to([P, TOPK * NT, NBLK + 1]),
                   spread(blk_k[:, :], NBLK + 1), ALU.is_equal).then_inc(r_dve, 1)
                dve.wait_ge(r_dve, c.next())
                for k in range(TOPK):
                    v = slice(k * NT, (k + 1) * NT)
                    tt(oh_blk[:, v, :], oh_cmp[:, v, :], spread(tok_id, NBLK + 1), ALU.mult)
                for q in range(4):
                    v = slice(4 * q, 4 * q + 4)
                    tt(oh_row[:, v, :], iota_r.unsqueeze(1).broadcast_to([P, 4, P]), spread(row_k[:, v], P),
                       ALU.is_equal).then_inc(r_oh, 1)
                dve.tensor_copy(next_gb[:, ds(layer + 1, 1)], gb_f[:, :])
                dve.wait_ge(r_idx, layer + 1)
                dve.tensor_copy(slot_tok[:, :], bank(4)[:, 0:NBLK + 1]).then_inc(r_plan, 1)
                next_phase(dve, DVE_E, layer, PH_C)

                steady(dve)
                nb2 = dve.value_load(plan[0:1, 0:1], min_val=NE - 2, max_val=NBLK - 2)
                nb = nb2 + 2
                gb = dve.value_load(plan[0:1, 1:2], min_val=0, max_val=DEPTH * NBLK)

                def lo(s, turns):
                    dve.wait_ge(d_hi, gb * 6 + turns * 6 + s + 1)
                    tt(ring_lo[:, s % 3, :], ring_raw[:, s % 6, :], ring_hi[:, s % 3, :], ALU.subtract)\
                        .then_inc(d_lo, 1)

                def x_lo(b):
                    for i, (hi_s, lo_s) in enumerate(((d_xhi0, d_xlo0), (d_xhi1, d_xlo1))):
                        dve.wait_ge(hi_s, gb + b + 1)
                        tt(xg_lo[:, 4 * i:4 * i + 4, :], grouped(bank(i), 4), xg_hi[:, 4 * i:4 * i + 4, :], ALU.subtract)\
                            .then_inc(lo_s, 1)

                def g_mul(b, chunks):
                    dve.wait_ge(d_silu, gb + b + 2)
                    dve.wait_ge(d_mm, gb * 6 + chunks + 3)
                    dve.wait_ge(d_tg, gb + b + 1)
                    tt(gate_sb[:, :], bank(4), silu_sb[:, :], ALU.mult).then_inc(d_gm, 1)

                def g_lo(b):
                    dve.wait_ge(d_ghi, gb + b + 1)
                    tt(gT_lo[:, :, :], grouped(bank(2), 4), gT_hi[:, :, :], ALU.subtract).then_inc(d_glo, 1)

                for s in range(3):
                    lo(s, 0)
                x_lo(0)
                lo(3, 0)
                tt(over_end[:, :], over_s[:, :], over_e[:, :], ALU.add).then_inc(r_dve, 1)
                dve.wait_ge(r_dve, c.next())
                cmp16 = cmp_s[:, :].rearrange("p (b e) -> p b e", e=NE)
                tt(cmp16, over_end[:, :].unsqueeze(1).broadcast_to([P, 16, NE]), spread(over_id, NE),
                   ALU.is_le).then_inc(r_dve, 1)
                dve.wait_ge(r_dve, c.next())
                dve.reduce_sum(ex_f[:, :], cmp16, axis=AX_X).then_inc(r_dve, 1)
                dve.wait_ge(r_dve, c.next())
                ts(ex_f[:, :], ex_f[:, :], float(NE - 1), None, ALU.min).then_inc(r_dve, 1)
                dve.wait_ge(r_dve, c.next())
                dve.tensor_copy(expert_i[:, NE:NE + 16], ex_f[:, :]).then_inc(r_over, 1)
                stt(rank_k[:, :], blk_k[:, :], float(P), row_k[:, :], ALU.mult, ALU.add).then_inc(r_dve, 1)
                dve.wait_ge(r_dve, c.next())
                dve.tensor_copy(dest_u[:, :], rank_k[:, :])
                c.close()
                c = Count(3, layer)
                dve.wait_ge(r_exp, layer + 1)
                ts(gates[:, 0:NT], exp_g[:, :], 1.0, None, ALU.add).then_inc(r_gates, 1)
                dve.wait_ge(r_gates, c.next())
                tt(gates[:, 0:NT], gates[:, 0:NT], sum_all[:, :], ALU.mult).then_inc(r_gates, 1)
                dve.wait_ge(r_gates, c.next())
                dve.reciprocal(gates[:, 0:NT], gates[:, 0:NT]).then_inc(r_gates, 1)
                dve.wait_ge(r_gates, c.next())
                tt(gates[:, NT:2 * NT], gates[:, 0:NT], exp_g[:, :], ALU.mult)
                c.close()
                g_mul(0, 4)
                x_lo(1)
                for s in (4, 5):
                    lo(s, 0)
                g_lo(0)
                for s in (6, 7, 8, 9):
                    lo(s, 0)

                def turn(b):
                    g_mul(b - 1, (b - 2) * 6 + 8)
                    x_lo(b)
                    lo(10, b - 2)
                    lo(11, b - 2)
                    g_lo(b - 1)
                    for s in (12, 13, 14, 15):
                        lo(s, b - 2)

                steady(dve)
                with dve.Fori(2, NE) as b:
                    turn(b)
                steady(dve)
                with dve.Fori(NE, NBLK) as b:
                    with dve.If(b < nb):
                        turn(b)
                g_mul(nb2 + 1, nb2 * 6 + 8)
                lo(10, nb2)
                lo(11, nb2)
                g_lo(nb2 + 1)
                next_phase(dve, DVE_E, layer, PH_D)

                dve.wait_ge(e_par_in, 32 * (layer + 1))

                def front(t, j, pair):
                    dve.wait_ge(e_yg[j], (layer * (NT // 2) + pair + 1) * 32)
                    stt(h_t(t), yg[j][0][:, :], gates[:, ds(t, 1)], h_t(t), ALU.mult, ALU.add).then_inc(e_dve, 1)
                    dve.wait_ge(e_dve, it(t) + 1)
                    stt(h_t(t), yg[j][1][:, :], gates[:, ds(t + NT, 1)], h_t(t), ALU.mult, ALU.add)\
                        .then_inc(e_comb, 1)
                    dve.wait_ge(f_rstd, ft(2, t) + 1)
                    stt(xn[j][:, :], h_t(t), rstd_x[:, j:j + 1], g_ple_sb[:, :], ALU.mult, ALU.mult)\
                        .then_inc(f_xn, 1)
                    x_lower(xe_lo[j], xt_hi[j], (layer * 2 + 1) * NT + t + 1)

                def gate(t):
                    for i, (g, b_) in enumerate(((e_g0, e_b0), (e_g1, e_b1))):
                        dve.wait_ge(g, it(t) + 1)
                        tt(gs[:, i * 512:(i + 1) * 512], bank(2 + i), b_gate_sb[:, i * 512:(i + 1) * 512], ALU.add)\
                            .then_inc(b_, 1)

                def finish(t):
                    dve.wait_ge(e_sg, it(t) + 1)
                    dve.wait_ge(e_pl, it(t) + 1)
                    tt(gs[:, :], bank(4, 2), gs[:, :], ALU.mult).then_inc(e_fin, 1)
                    dve.wait_ge(e_fin, it(t) + 1)
                    tt(h_t(t), h_t(t), gs[:, :], ALU.add).then_inc(e_h, 1)
                    dve.wait_ge(e_h, it(t) + 2)

                def turn(t, j, first, last, pair=None):
                    if first:
                        for k in range(K_DVE):
                            w_lower(w_gate_lo, w_gate_sb, w_gate_hi, k, e_whi, e_wlo, layer)
                        front(0, 0, 0)
                    if not last:
                        front(t + 1, 1 - j, pair)
                    gate(t)
                    finish(t)

                turn(0, 0, True, False, 0)
                steady(dve)
                with dve.Fori(0, NT // 2 - 1) as i:
                    turn(i * 2 + 1, 1, False, False, i + 1)
                    turn(i * 2 + 2, 0, False, False, i + 1)
                turn(NT - 1, 1, False, True)
                next_phase(dve, DVE_E, layer, PH_E)

        @block.tensor
        def _(pe):
            credit(pe, 1, a_tc, a_s, c_f1, d_tx, d_tg)
            credit(pe, 2, e_tpp)
            credit(pe, 3, d_mm)
            credit(pe, PT_BACK, b_pt)
            pe.wait_ge(consts_in, 16)
            mm = pe.matmul

            def transposes(dst, src, n0, n, raises, rows=P):
                for i in range(n):
                    last = pe.transpose(dst[:, i * P:(i + 1) * P], src[:, (n0 + i) * P:(n0 + i + 1) * P], ident)
                last.then_inc(raises, 1)

            def product(dst, lhs, rhs, kn, raises=None):
                for k in range(kn):
                    last = mm(dst, lhs(k), rhs(k), start=(k == 0), stop=(k == kn - 1))
                if raises:
                    last.then_inc(raises, 1)

            def split_mm(dst, a_hi, a_lo, w_hi, w_lo, start, stop):
                mm(dst, a_hi, w_hi, start=start, stop=False)
                mm(dst, a_hi, w_lo, start=False, stop=False)
                return mm(dst, a_lo, w_hi, start=False, stop=stop)

            def split_product(dst, a_hi, a_lo, w_hi, w_lo, cols, raises, w_done=None, layer=None):
                for k in range(KD):
                    if w_done and k < K_DVE:
                        pe.wait_ge(w_done[0], layer * K_DVE + k + 1)
                    elif w_done:
                        pe.wait_ge(w_done[1], layer * (KD - K_DVE) + k - K_DVE + 1)
                    last = split_mm(dst, a_hi[:, k, :], a_lo[:, k, :], w_hi[:, k, cols], w_lo[:, k, cols],
                                    k == 0, k == KD - 1)
                last.then_inc(raises, 1)

            with pe.Fori(0, DEPTH) as layer:
                it = lambda t: layer * NT + t
                ft = lambda phase, t: (layer * 3 + phase) * NT + t
                pe.wait_ge(ws_in, 16 * 2 * (layer + 1))
                for i in range(2):
                    for g in range(4 * i, 4 * i + 4):
                        src = ws_nat[g // 6][:, g % 6 * P:(g % 6 + 1) * P]
                        last = pe.transpose(bank(i)[:, (g - 4 * i) * P:(g - 4 * i + 1) * P], src, ident)
                    last.then_inc(ws_t, 1)
                next_phase(pe, PE_E, layer, PH_WS)

                def front(t, j):
                    pe.wait_ge(f_xn, ft(0, t) + 2)
                    pe.wait_ge(f_ev0, ft(0, t) + 1)
                    transposes(bank(0), xn[j], 0, 4, f_tp0)
                    pe.wait_ge(f_ev1, ft(0, t) + 1)
                    transposes(bank(1), xn[j], 4, 4, f_tp1)

                def turn(t, j, first, last):
                    if first:
                        front(0, 0)
                        pe.wait_ge(w_in_v_in, 16 * (layer + 1))
                    pe.wait_ge(f_ev0, ft(0, t) + 2)
                    pe.wait_ge(f_ev1, ft(0, t) + 2)
                    pe.wait_ge(a_gv, it(t) + 1)
                    lhs = lambda k: xT[j][:, k, :]
                    product(bank(4), lhs, lambda k: w_in_sb[:, k, V0:IN_W], KD, a_mv)
                    if not last:
                        front(t + 1, 1 - j)
                    pe.wait_ge(a_cn, it(t) + 1)
                    if first:
                        pe.wait_ge(w_in_c_in, 16 * (layer + 1))
                    product(bank(2)[:, 0:W_C], lhs, lambda k: w_in_sb[:, k, 0:W_C], KD, a_mc)
                    pe.wait_ge(a_gu, it(t) + 1)
                    if first:
                        pe.wait_ge(w_in_u_in, 16 * (layer + 1))
                    product(bank(3), lhs, lambda k: w_in_sb[:, k, U0:V0], KD, a_mu)
                    pe.wait_ge(a_cn, it(t) + 2)
                    pe.wait_ge(a_ce, it(t) + 1)
                    transposes(bank(5), cn, 0, 3, a_tc)
                    pe.wait_ge(a_vn, it(t) + 1)
                    pe.wait_ge(a_m, it(t) + 1)
                    for g in range(GROUPS):
                        last_mm = mm(bank(6)[:, g * GDIM:(g + 1) * GDIM], wsT[:, g, :], vn[:, g * GDIM:(g + 1) * GDIM],
                                     start=True, stop=True)
                    last_mm.then_inc(a_s, 1)

                over_tiles(pe, turn)
                next_phase(pe, PE_E, layer, PH_A)

                def project(hd, n, first=False):
                    if n > 0:
                        pe.wait_ge(b_pev, it(hd) * 4 + n)
                    elif not first:
                        pe.wait_ge(b_tev_a, it(hd) * 2)
                    for i in range(4):
                        cols = slice((4 * (n % 2) + i) * P, (4 * (n % 2) + i + 1) * P)
                        if n < 2:
                            for k in range(2):
                                last = mm(bank(0)[:, i * QK:(i + 1) * QK], cT[:, k, cols],
                                          w_uq_sb[:, k, ds(hd * QK, QK)], start=(k == 0), stop=(k == 1))
                        else:
                            last = mm(bank(0)[:, i * P:(i + 1) * P], cT[:, 2, cols],
                                      w_ukv_sb[:, ds(hd * P, P)], start=True, stop=True)
                    last.then_inc(b_proj, 1)

                def transpose_qk(hd, n):
                    if n == 0:
                        pe.wait_ge(b_pev, it(hd) * 4 + 4)
                        pe.wait_ge(b_qk, it(hd) * 2 + 2)
                    if n == 1:
                        pe.wait_ge(b_qk, it(hd) * 2 + 3)
                        pe.wait_ge(b_tev_d, it(hd) * 2 + 1)
                    if n == 2:
                        pe.wait_ge(b_tev_d, it(hd) * 2 + 2)
                    if n == 3:
                        pe.wait_ge(b_tev_a, it(hd) * 2 + 1)
                    for i in range(4):
                        last = pe.transpose(bank(0)[0:QK, i * P:(i + 1) * P],
                                            qkb[:, n % 2, 4 * (n // 2) + i, :], ident)
                    last.then_inc(b_t, 1)

                def scores(hd, j, i):
                    if i == 0:
                        pe.wait_ge(b_tev_d, it(hd) * 2 + 2)
                    if i == 4:
                        pe.wait_ge(b_tev_a, it(hd) * 2 + 2)
                    pe.wait_ge(b_exp, it(hd) * 8 + i + 1)
                    w = (i + 1) * P
                    for c0_ in range(0, w, BANK):
                        n = min(BANK, w - c0_)
                        last = mm(bank(2 + 2 * (i % 2), 2)[:, c0_:c0_ + n], qkT[j][:, 0, i * P:(i + 1) * P],
                                  qkT[j][:, 1, c0_:c0_ + n], start=True, stop=True)
                    last.then_inc(b_s, 1)

                def weigh(hd, j, i, g):
                    if g % 2 == 0:
                        pe.wait_ge(b_pte_a, it(hd) * 6 + g // 2 + 2)
                    else:
                        pe.wait_ge(b_pte_d, it(hd) * 6 + g // 2 + 2)
                    if g == 0:
                        pe.wait_ge(b_o, it(hd) + 1)
                    k0 = 4 * (g - GROUP_OF[i])
                    for k in range(k0, k0 + GROUP_N[g]):
                        last = mm(bank(7)[:, i * VDIM:(i + 1) * VDIM], probT[g % 2][:, k - k0, :], v_sb[j][:, k, :],
                                  start=(k == 0), stop=(k == i))
                    if g == N_PT - 1:
                        last.then_inc(b_pv, 1)

                def turn(hd, j, first, last):
                    if first:
                        pe.wait_ge(b_par_in, 16 * 4 * (layer + 1))
                        for n in range(4):
                            project(0, n, True)
                        for n in range(4):
                            transpose_qk(0, n)
                        scores(0, 0, 0)
                        scores(0, 0, 1)
                    before_g = None
                    for i in range(NT):
                        pe.wait_ge(b_exp, it(hd) * 8 + i + 3)
                        for g in range(GROUP_OF[i], GROUP_OF[i + 1]):
                            if g % 2 == 0:
                                pe.wait_ge(b_pte_a, it(hd) * 6 + g // 2 + 1)
                            else:
                                pe.wait_ge(b_pte_d, it(hd) * 6 + g // 2 + 1)
                            transposes(bank(1 if g % 2 == 0 else 6), prob[i % 2], 4 * (g - GROUP_OF[i]), GROUP_N[g],
                                       b_pt)
                            if before_g:
                                weigh(hd, j, *before_g)
                            before_g = (i, g)
                            if not last and g == GROUP_OF[6]:
                                transpose_qk(hd + 1, 2)
                            if not last and g == GROUP_OF[7]:
                                transpose_qk(hd + 1, 3)
                        if i + 2 < NT:
                            scores(hd, j, i + 2)
                        elif not last:
                            scores(hd + 1, 1 - j, i + 2 - NT)
                        if not last:
                            if i < 4:
                                project(hd + 1, i)
                            if i == 4:
                                transpose_qk(hd + 1, 0)
                            if i == 5:
                                transpose_qk(hd + 1, 1)
                    weigh(hd, j, *before_g)

                over_tiles(pe, turn)
                next_phase(pe, PE_E, layer, PH_B)

                def front(t, j):
                    pe.wait_ge(f_xn, ft(1, t) + 2)
                    pe.wait_ge(f_ev0, ft(1, t) + 1)
                    transposes(bank(0), xn[j], 0, 4, f_tp0)
                    pe.wait_ge(f_ev1, ft(1, t) + 1)
                    transposes(bank(1), xn[j], 4, 4, f_tp1)

                def tail_t(t):
                    pe.wait_ge(c_xf, it(t) + 1)
                    pe.wait_ge(c_fe0, it(t) + 1)
                    transposes(bank(4), xf, 0, 4, c_f0)
                    pe.wait_ge(c_fe1, it(t) + 1)
                    transposes(bank(5), xf, 4, 4, c_f1)

                def router(t):
                    pe.wait_ge(c_fe0, it(t) + 2)
                    pe.wait_ge(c_fe1, it(t) + 2)
                    pe.wait_ge(c_lge, it(t) + 1)
                    product(bank(6)[:, 0:NROUTE], lambda k: xfT[:, k, :], lambda k: w_router[:, k, :], KD, c_rt)

                def turn(t, j, first, last):
                    if first:
                        front(0, 0)
                    pe.wait_ge(f_ev0, ft(1, t) + 2)
                    pe.wait_ge(f_ev1, ft(1, t) + 2)
                    pe.wait_ge(c_h0, it(t) + 1)
                    split_product(bank(2), xt_hi[j], xc_lo[j], w_out_hi, w_out_lo, slice(0, 512), c_y0,
                                  (c_wlo, c_wlo_p) if first else None, layer)
                    if not first:
                        tail_t(t - 1)
                    if not last:
                        front(t + 1, 1 - j)
                    pe.wait_ge(c_h1, it(t) + 1)
                    split_product(bank(3), xt_hi[j], xc_lo[j], w_out_hi, w_out_lo, slice(512, D), c_y1)
                    if not first:
                        router(t - 1)
                    if last:
                        tail_t(t)
                        router(t)

                over_tiles(pe, turn)
                for t in range(NT):
                    if t == 0:
                        pe.wait_ge(c_dve2, (layer * NT + NT - 1) * 2)
                    if t == NT - 1:
                        pe.wait_ge(r_gap, layer + 1)
                    dst = bank(0)[:, t * NE:(t + 1) * NE]
                    mm(dst, before, chosen[:, t, :], start=True, stop=False)
                    mm(dst, ones, picks[:, t, :], start=False, stop=True)
                mm(bank(1)[:, 0:NE], ones, picks[:, NT, :], start=True, stop=True).then_inc(r_rank, 1)
                pe.wait_ge(r_ovt, layer + 1)
                pe.transpose(bank(2)[0:NE, 0:P], over_e[:, :], ident).then_inc(r_ovsb, 1)
                pe.wait_ge(r_ovs, layer + 1)
                mm(bank(3)[:, 0:NE], overT[:, :], before[0:NE, 0:NE], start=True, stop=True).then_inc(r_ovsb, 1)
                for n in range(TOPK * NT):
                    if n % 4 == 0:
                        pe.wait_ge(r_oh, layer * 4 + n // 4 + 1)
                    last = mm(bank(4)[:, 0:NBLK + 1], oh_row[:, n, :], oh_blk[:, n, :],
                              start=(n == 0), stop=(n == TOPK * NT - 1))
                last.then_inc(r_idx, 1)
                next_phase(pe, PE_E, layer, PH_C)

                steady(pe)
                nb2 = pe.value_load(plan[0:1, 0:1], min_val=NE - 2, max_val=NBLK - 2)
                nb = nb2 + 2
                gb = pe.value_load(plan[0:1, 1:2], min_val=0, max_val=DEPTH * NBLK)

                def x_t(b):
                    pe.wait_ge(d_xg, (gb + b + 1) * 16)
                    pe.wait_ge(d_xlo0, gb + b + 1)
                    pe.wait_ge(d_xlo1, gb + b + 1)
                    for i in range(KD):
                        last = pe.transpose(ps[:, i * P:(i + 1) * P], xg[:, i * P:(i + 1) * P], ident)
                    last.then_inc(d_tx, 1)

                def up(s, turns, dst):
                    pe.wait_ge(d_lo, gb * 6 + turns * 6 + s + 7)
                    part = s % 2
                    for k in range(4):
                        w = slice(k * FE, (k + 1) * FE)
                        last = split_mm(dst, xg_hi[:, 4 * part + k, :], xg_lo[:, 4 * part + k, :],
                                        ring_hi[:, s % 3, w], ring_lo[:, s % 3, w], part == 0 and k == 0,
                                        part == 1 and k == 3)
                    last.then_inc(d_mm, 1)

                def ups(b, s, turns):
                    pe.wait_ge(d_xlo0, gb + b + 2)
                    pe.wait_ge(d_xlo1, gb + b + 2)
                    pe.wait_ge(d_silu, gb + b + 1)
                    up(s, turns, bank(3))
                    up(s + 1, turns, bank(3))
                    pe.wait_ge(d_gm, gb + b + 1)
                    up(s + 2, turns, bank(4))
                    up(s + 3, turns, bank(4))

                def down(b, s, turns):
                    pe.wait_ge(d_glo, gb + b + 2)
                    pe.wait_ge(d_yev, gb + b + 1)
                    for part in range(2):
                        pe.wait_ge(d_lo, gb * 6 + turns * 6 + s + part + 7)
                        for k in range(2):
                            for i in range(2):
                                w = slice(k * D + i * 512, k * D + (i + 1) * 512)
                                last = split_mm(bank(5 + i), gT_hi[:, 2 * part + k, :], gT_lo[:, 2 * part + k, :],
                                                ring_hi[:, (s + part) % 3, w], ring_lo[:, (s + part) % 3, w],
                                                part == 0 and k == 0, part == 1 and k == 1)
                        last.then_inc(d_mm, 1)

                def g_t(b):
                    pe.wait_ge(d_gm, gb + b + 2)
                    pe.wait_ge(d_glo, gb + b + 1)
                    transposes(bank(2), gate_sb, 0, 4, d_tg)

                x_t(0)
                ups(0, 0, 0)
                x_t(1)
                g_t(0)
                ups(1, 4, 0)

                def turn(b):
                    x_t(b)
                    down(b - 2, 8, b - 2)
                    g_t(b - 1)
                    ups(b, 10, b - 2)

                steady(pe)
                with pe.Fori(2, NE) as b:
                    turn(b)
                steady(pe)
                with pe.Fori(NE, NBLK) as b:
                    with pe.If(b < nb):
                        turn(b)
                down(nb2, 8, nb2)
                g_t(nb2 + 1)
                down(nb2 + 1, 10, nb2)
                next_phase(pe, PE_E, layer, PH_D)

                def p_front(t, j, pair):
                    pe.wait_ge(p_in[j], (layer * (NT // 2) + pair + 1) * 16)
                    pe.wait_ge(e_evp, it(t) + 1)
                    transposes(bank(6), p_sb[j], 0, 2, e_tpp)

                def front(t, j):
                    pe.wait_ge(f_xn, ft(2, t) + 2)
                    pe.wait_ge(f_ev0, ft(2, t) + 1)
                    transposes(bank(0), xn[j], 0, 4, f_tp0)
                    pe.wait_ge(f_ev1, ft(2, t) + 1)
                    transposes(bank(1), xn[j], 4, 4, f_tp1)

                def embed(t, j):
                    pe.wait_ge(e_evp, it(t) + 2)
                    pe.wait_ge(e_h, it(t) + 1)
                    for i in range(2):
                        product(bank(4 + i), lambda k: pT[j][:, k, :],
                                lambda k: w_ple_sb[:, k, i * 512:(i + 1) * 512], 2, e_pl if i == 1 else None)

                def turn(t, j, first, last, pair=None):
                    if first:
                        pe.wait_ge(ple_w_in, 80 * (layer + 1))
                        p_front(0, 0, 0)
                        embed(0, 0)
                        front(0, 0)
                    pe.wait_ge(f_ev0, ft(2, t) + 2)
                    pe.wait_ge(f_ev1, ft(2, t) + 2)
                    pe.wait_ge(e_b0, it(t) + 1)
                    split_product(bank(2), xt_hi[j], xe_lo[j], w_gate_hi, w_gate_lo, slice(0, 512), e_g0,
                                  (e_wlo, e_wlo_p) if first else None, layer)
                    pe.wait_ge(e_b1, it(t) + 1)
                    split_product(bank(3), xt_hi[j], xe_lo[j], w_gate_hi, w_gate_lo, slice(512, D), e_g1)
                    if not last:
                        front(t + 1, 1 - j)
                        p_front(t + 1, 1 - j, pair)
                    if not first:
                        embed(t, j)

                turn(0, 0, True, False, 0)
                steady(pe)
                with pe.Fori(0, NT // 2 - 1) as i:
                    turn(i * 2 + 1, 1, False, False, i + 1)
                    turn(i * 2 + 2, 0, False, False, i + 1)
                turn(NT - 1, 1, False, True)
                next_phase(pe, PE_E, layer, PH_E)


_INS = ["x", "p", "g_mix_norm", "w_in", "g_cq", "g_ckv", "w_uq", "w_ukv", "g_qn", "g_kn", "g_v", "w_s", "b_s",
        "g_out_mla", "g_out_gmlp", "w_out", "g_ffn_norm", "w_router_group", "w_router_expert",
        "w1", "w3", "w2", "g_ple", "w_ple_gate", "b_ple_gate", "w_ple"]


def shape_constants(seq):
    import numpy as np

    f = np.float32
    part = np.arange(P, dtype=f)
    inv = (f(10000.0) ** (-np.arange(0, ROPE, 2, dtype=f) / f(ROPE))).astype(f)
    ang = (np.arange(seq, dtype=f)[:, None] * inv[None, :]).astype(f)
    tiled = lambda a: np.concatenate([a, a], axis=1).reshape(seq // P, P, ROPE).transpose(1, 0, 2).reshape(P, -1)
    row = lambda a: np.broadcast_to(np.asarray(a, f), (P, len(a)))
    return np.ascontiguousarray(np.concatenate([
        np.eye(P, dtype=f),
        (part[:, None] < part[None, :]).astype(f),
        np.ones((P, P), f),
        tiled(np.cos(ang)), tiled(np.sin(ang)),
        row(part),
        row(P * np.arange(NE)),
        row(P * np.arange(1, 9)),
        np.stack([P * t + part for t in range(8)], axis=1),
        row(np.arange(16)),
    ], axis=1).astype(f))


def kernel(**inputs):
    import numpy as _np
    import concourse.bacc as _bacc
    from concourse import mybir as _mybir
    from concourse.bass_utils import run_bass_kernel_spmd as _run

    nc = _bacc.Bacc("TRN2", target_bir_lowering=False, num_devices=1)
    arrays, args = {}, []
    for name in _INS:
        a = _np.ascontiguousarray(inputs[name])
        arrays[f"in_{name}"] = a
        args.append(nc.dram_tensor(f"in_{name}", a.shape, _mybir.dt.from_np(a.dtype), kind="ExternalInput").ap())
    shape = inputs["x"].shape
    a = shape_constants(shape[1])
    arrays["shape_consts"] = a
    args.append(nc.dram_tensor("shape_consts", a.shape, _mybir.dt.float32, kind="ExternalInput").ap())
    args.append(nc.dram_tensor("out_0", shape, _mybir.dt.float32, kind="ExternalOutput").ap())
    hybrid_trunk(nc, *args)
    r = _run(nc, [arrays], core_ids=[0])
    return r.results[0]["out_0"]
```
